# Optimizing a Trainium2 kernel written in Bass

```python
import jax, jax.numpy as jnp
from jax import lax
import numpy as np
import math

D_MODEL = 1024
BATCH = 1
SEQ = 512
DEPTH = 1

GRID_W = 64
CTX_LEN = 256
CONV_W = 1024
CONV_K = 3
N_HEADS = 16
HEAD_DIM = 64
ATTN_W = N_HEADS * HEAD_DIM
WIN_ROWS_MAX = 8
WIN_COLS = 16
ROPE_BASE = 10000.0
EPS = 1e-6
N_BRANCH = 2
IN_SIZES = [CONV_W] * 4 + [ATTN_W] * 4 + [D_MODEL] * N_BRANCH
IN_COLS = sum(IN_SIZES)
K_OFF = 4 * CONV_W + ATTN_W
V_END = 4 * CONV_W + 3 * ATTN_W


def _rmsnorm(u, g):
    u32 = u.astype(jnp.float32)
    return (u32 * lax.rsqrt(jnp.mean(u32 * u32, axis=-1, keepdims=True) + EPS)).astype(u.dtype) * g

def _modulation(cond, w_mod, b_mod):
    m = jax.nn.silu(cond) @ w_mod + b_mod
    return jnp.split(m, 3, axis=-1)

def _split_in(p):
    idx = np.cumsum(IN_SIZES)[:-1].tolist()
    return jnp.split(p, idx, axis=-1)

def _dwconv3(u, w, b):
    L = u.shape[1]
    up = jnp.pad(u, ((0, 0), (1, 1), (0, 0)))
    return up[:, :L] * w[0] + up[:, 1:L + 1] * w[1] + up[:, 2:] * w[2] + b

def _rope_2d_tables(L, dtype):
    t = jnp.arange(L, dtype=jnp.int32)
    row = (t // GRID_W).astype(jnp.float32)
    col = (t % GRID_W).astype(jnp.float32)
    half = HEAD_DIM // 2
    inv = ROPE_BASE ** (-jnp.arange(0, half, 2, dtype=jnp.float32) / half)
    ang_r = row[:, None] * inv
    ang_c = col[:, None] * inv
    ang = jnp.concatenate([ang_r, ang_r, ang_c, ang_c], axis=-1)
    return jnp.cos(ang).astype(dtype), jnp.sin(ang).astype(dtype)

def _rot_half_axial(u):
    u1, u2, u3, u4 = jnp.split(u, 4, axis=-1)
    return jnp.concatenate([-u2, u1, -u4, u3], axis=-1)

def _apply_rope(u, cos, sin):
    return u * cos[None, :, None, :] + _rot_half_axial(u) * sin[None, :, None, :]

def _heads(u):
    return u.reshape(u.shape[0], u.shape[1], N_HEADS, HEAD_DIM)

def _neighbourhood_attention(q, k, v, k_ctx, v_ctx, rpb):
    bsz, L, H, Dh = q.shape
    rows = L // GRID_W
    wr = min(WIN_ROWS_MAX, rows)
    n_nb = wr * WIN_COLS
    scale = HEAD_DIM ** -0.5
    qg = q.reshape(bsz, rows, GRID_W, H, Dh)
    kg = k.reshape(bsz, rows, GRID_W, H, Dh)
    vg = v.reshape(bsz, rows, GRID_W, H, Dh)
    col = jnp.arange(GRID_W, dtype=jnp.int32)
    col_start = jnp.clip(col - WIN_COLS // 2, 0, GRID_W - WIN_COLS)
    col_idx = col_start[:, None] + jnp.arange(WIN_COLS, dtype=jnp.int32)
    dc_idx = col_idx - col[:, None] + (WIN_COLS - 1)

    def row_block(r):
        rs = jnp.clip(r - wr // 2, 0, rows - wr)
        q_r = lax.dynamic_index_in_dim(qg, r, axis=1, keepdims=False)
        k_slab = lax.dynamic_slice_in_dim(kg, rs, wr, axis=1)
        v_slab = lax.dynamic_slice_in_dim(vg, rs, wr, axis=1)
        k_win = k_slab[:, :, col_idx]
        v_win = v_slab[:, :, col_idx]
        dr_idx = rs + jnp.arange(wr, dtype=jnp.int32) - r + (WIN_ROWS_MAX - 1)
        bias = rpb[:, dr_idx[None, :, None], dc_idx[:, None, :]]
        s_nb = (jnp.einsum('bqhd,bpqjhd->bqhpj', q_r, k_win).astype(jnp.float32) * scale
                + jnp.transpose(bias, (1, 0, 2, 3))[None].astype(jnp.float32))
        s_nb = s_nb.reshape(bsz, GRID_W, H, n_nb)
        s_ctx = jnp.einsum('bqhd,bchd->bqhc', q_r, k_ctx).astype(jnp.float32) * scale
        p = jax.nn.softmax(jnp.concatenate([s_nb, s_ctx], axis=-1), axis=-1).astype(v.dtype)
        p_nb = p[..., :n_nb].reshape(bsz, GRID_W, H, wr, WIN_COLS)
        p_ctx = p[..., n_nb:]
        return (jnp.einsum('bqhpj,bpqjhd->bqhd', p_nb, v_win)
                + jnp.einsum('bqhc,bchd->bqhd', p_ctx, v_ctx))

    out = lax.map(row_block, jnp.arange(rows, dtype=jnp.int32))
    return jnp.transpose(out, (1, 0, 2, 3, 4)).reshape(bsz, L, H * Dh)

def _ctx_attention(q, k, v):
    scale = HEAD_DIM ** -0.5
    s = jnp.einsum('bqhd,bkhd->bhqk', q, k).astype(jnp.float32) * scale
    p = jax.nn.softmax(s, axis=-1).astype(v.dtype)
    o = jnp.einsum('bhqk,bkhd->bqhd', p, v)
    return o.reshape(o.shape[0], o.shape[1], ATTN_W)

def _mixer_out(parts, attn_o, conv_w, conv_b, w_out_conv, w_out_attn, w_o):
    b_gate, c_gate, x_in, z_a, _, _, _, z_b, g_a, g_b = parts
    y_a = (jax.nn.silu(z_a) * b_gate * _dwconv3(c_gate * x_in, conv_w, conv_b)) @ w_out_conv
    y_b = (jax.nn.silu(z_b) * attn_o) @ w_out_attn
    merged = jax.nn.sigmoid(g_a) * y_a + jax.nn.sigmoid(g_b) * y_b
    return merged @ w_o

def first_inputs(seed: int = 0) -> dict:
    key = jax.random.key(seed)
    ks = jax.random.split(key, 16)
    f32 = jnp.float32
    nrm = lambda k, shape, s: jax.random.normal(k, shape, f32) * s
    return {
        "x": nrm(ks[0], (BATCH, SEQ, D_MODEL), 1.0),
        "c": nrm(ks[1], (BATCH, D_MODEL), 1.0),
        "ctx": nrm(ks[2], (BATCH, CTX_LEN, D_MODEL), 1.0),
        "c_ctx": nrm(ks[3], (D_MODEL,), 1.0),
        "w_mod": nrm(ks[4], (DEPTH, D_MODEL, 3 * D_MODEL), D_MODEL ** -0.5),
        "b_mod": nrm(ks[5], (DEPTH, 3 * D_MODEL), 0.02),
        "pre_g": 1.0 + nrm(ks[6], (DEPTH, D_MODEL), 0.05),
        "post_g": 1.0 + nrm(ks[7], (DEPTH, D_MODEL), 0.05),
        "w_in": nrm(ks[8], (DEPTH, D_MODEL, IN_COLS), D_MODEL ** -0.5),
        "conv_w": nrm(ks[9], (DEPTH, CONV_K, CONV_W), CONV_K ** -0.5),
        "conv_b": nrm(ks[10], (DEPTH, CONV_W), 0.02),
        "rpb": nrm(ks[11], (DEPTH, N_HEADS, 2 * WIN_ROWS_MAX - 1, 2 * WIN_COLS - 1), 0.1),
        "w_out_conv": nrm(ks[12], (DEPTH, CONV_W, D_MODEL), CONV_W ** -0.5),
        "w_out_attn": nrm(ks[13], (DEPTH, ATTN_W, D_MODEL), ATTN_W ** -0.5),
        "w_o": nrm(ks[14], (DEPTH, D_MODEL, D_MODEL), D_MODEL ** -0.5),
    }

def first_block(x, c, ctx, c_ctx, w_mod, b_mod, pre_g, post_g, w_in, conv_w, conv_b, rpb,
              w_out_conv, w_out_attn, w_o):
    L = x.shape[1]
    cos, sin = _rope_2d_tables(L, x.dtype)
    for i in range(DEPTH):
        last = i == DEPTH - 1
        sh, sc, gt = _modulation(c, w_mod[i], b_mod[i])
        sh_c, sc_c, gt_c = _modulation(c_ctx, w_mod[i], b_mod[i])
        h = _rmsnorm(x, pre_g[i]) * (1.0 + sc[:, None, :]) + sh[:, None, :]
        hc = _rmsnorm(ctx, pre_g[i]) * (1.0 + sc_c) + sh_c
        parts = _split_in(h @ w_in[i])
        q = _apply_rope(_heads(parts[4]), cos, sin)
        k = _apply_rope(_heads(parts[5]), cos, sin)
        v = _heads(parts[6])
        if last:
            kv_c = hc @ w_in[i][:, K_OFF:V_END]
            k_c, v_c = jnp.split(kv_c, 2, axis=-1)
            k_c, v_c = _heads(k_c), _heads(v_c)
        else:
            parts_c = _split_in(hc @ w_in[i])
            k_c, v_c = _heads(parts_c[5]), _heads(parts_c[6])
        attn = _neighbourhood_attention(q, k, v, k_c, v_c, rpb[i])
        y = _mixer_out(parts, attn, conv_w[i], conv_b[i], w_out_conv[i], w_out_attn[i], w_o[i])
        if not last:
            attn_c = _ctx_attention(_heads(parts_c[4]), k_c, v_c)
            y_c = _mixer_out(parts_c, attn_c, conv_w[i], conv_b[i], w_out_conv[i], w_out_attn[i], w_o[i])
            ctx = ctx + gt_c * _rmsnorm(y_c, post_g[i])
        x = x + gt[:, None, :] * _rmsnorm(y, post_g[i])
    return x


MEM_LEN = 256
N_DIFF_HEADS = 4
DIFF_V_DIM = 2 * HEAD_DIM
N_FOX_HEADS = 8
N_MEM_HEADS = 4
MEM_HEAD_DIM = D_MODEL // N_MEM_HEADS
D_FF = 4 * D_MODEL
N_BUCKETS = 32
MAX_DISTANCE = 128
Q_BLOCK = 128

DIFF_QK_W = N_DIFF_HEADS * 2 * HEAD_DIM
DIFF_V_W = N_DIFF_HEADS * DIFF_V_DIM
FOX_W = N_FOX_HEADS * HEAD_DIM
IN_SPLITS = [DIFF_QK_W, DIFF_QK_W, DIFF_V_W, FOX_W, FOX_W, FOX_W, N_FOX_HEADS, D_MODEL, D_MODEL]
IN_COLS_2 = int(sum(IN_SPLITS))
IN_OFFSETS = [int(v) for v in np.cumsum(IN_SPLITS)[:-1]]


def _rmsnorm_2(x, g):
    xf = x.astype(jnp.float32)
    y = xf * lax.rsqrt(jnp.mean(xf * xf, axis=-1, keepdims=True) + EPS)
    return (y * g.astype(jnp.float32)).astype(x.dtype)

def _split_heads(t, n_heads):
    b, s, _ = t.shape
    return t.reshape(b, s, n_heads, -1).transpose(0, 2, 1, 3)

def _merge_blocks(o):
    nb, b, h, qb, d = o.shape
    return o.transpose(1, 0, 3, 2, 4).reshape(b, nb * qb, h, d)

def _t5_bucket(dist):
    dist = jnp.maximum(dist, 0)
    max_exact = N_BUCKETS // 2
    d = jnp.maximum(dist, 1).astype(jnp.float32)
    large = max_exact + (jnp.log(d / max_exact) / math.log(MAX_DISTANCE / max_exact)
                         * (N_BUCKETS - max_exact)).astype(jnp.int32)
    large = jnp.minimum(large, N_BUCKETS - 1)
    return jnp.where(dist < max_exact, dist, large)

def _hybrid_mixer(h, w_in, b_forget, lq1, lk1, lq2, lk2, g_subln, rel_bias,
                  w_diff_out, w_fox_out, w_o, lambda_init):
    b, s, _ = h.shape
    proj = h @ w_in
    qa, ka, va, qb, kb, vb, fl, ga, gb = jnp.split(proj, IN_OFFSETS, axis=-1)

    qa = _split_heads(qa, 2 * N_DIFF_HEADS).reshape(b, N_DIFF_HEADS, 2, s, HEAD_DIM)
    ka = _split_heads(ka, 2 * N_DIFF_HEADS).reshape(b, N_DIFF_HEADS, 2, s, HEAD_DIM)
    qa1, qa2 = qa[:, :, 0], qa[:, :, 1]
    ka1, ka2 = ka[:, :, 0], ka[:, :, 1]
    va = _split_heads(va, N_DIFF_HEADS)
    lam = (jnp.exp(jnp.sum(lq1.astype(jnp.float32) * lk1.astype(jnp.float32)))
           - jnp.exp(jnp.sum(lq2.astype(jnp.float32) * lk2.astype(jnp.float32)))
           + lambda_init)

    qb = _split_heads(qb, N_FOX_HEADS)
    kb = _split_heads(kb, N_FOX_HEADS)
    vb = _split_heads(vb, N_FOX_HEADS)
    log_f = jax.nn.log_sigmoid(fl.astype(jnp.float32) + b_forget.astype(jnp.float32))
    cum = jnp.cumsum(log_f, axis=1).transpose(0, 2, 1)

    scale = HEAD_DIM ** -0.5
    table = rel_bias.astype(jnp.float32)
    k_pos = jnp.arange(s)

    def block(i):
        q0 = i * Q_BLOCK
        q_pos = q0 + jnp.arange(Q_BLOCK)
        dist = q_pos[:, None] - k_pos[None, :]
        causal = dist >= 0
        rel = jnp.transpose(table[_t5_bucket(dist)], (2, 0, 1))
        sl = lambda t: lax.dynamic_slice_in_dim(t, q0, Q_BLOCK, axis=2)
        s1 = jnp.einsum('bhqd,bhkd->bhqk', sl(qa1), ka1).astype(jnp.float32) * scale + rel
        s2 = jnp.einsum('bhqd,bhkd->bhqk', sl(qa2), ka2).astype(jnp.float32) * scale + rel
        a1 = jax.nn.softmax(jnp.where(causal, s1, -jnp.inf), axis=-1)
        a2 = jax.nn.softmax(jnp.where(causal, s2, -jnp.inf), axis=-1)
        oa = jnp.einsum('bhqk,bhkd->bhqd', (a1 - lam * a2).astype(va.dtype), va)
        c_q = lax.dynamic_slice_in_dim(cum, q0, Q_BLOCK, axis=2)
        sb = (jnp.einsum('bhqd,bhkd->bhqk', sl(qb), kb).astype(jnp.float32) * scale
              + (c_q[..., None] - cum[:, :, None, :]))
        pb = jax.nn.softmax(jnp.where(causal, sb, -jnp.inf), axis=-1)
        ob = jnp.einsum('bhqk,bhkd->bhqd', pb.astype(vb.dtype), vb)
        return oa, ob

    oa, ob = lax.map(block, jnp.arange(s // Q_BLOCK))
    ya = _rmsnorm_2(_merge_blocks(oa), g_subln) * (1.0 - lambda_init)
    ya = ya.reshape(b, s, DIFF_V_W)
    yb = _merge_blocks(ob).reshape(b, s, FOX_W)
    merged = jax.nn.sigmoid(ga) * (ya @ w_diff_out) + jax.nn.sigmoid(gb) * (yb @ w_fox_out)
    return merged @ w_o

def _memory_cross_attention(h, mem_n, w_q, w_kv, w_o):
    b, s, _ = h.shape
    q = _split_heads(h @ w_q, N_MEM_HEADS)
    k, v = jnp.split(mem_n @ w_kv, 2, axis=-1)
    k = _split_heads(k, N_MEM_HEADS)
    v = _split_heads(v, N_MEM_HEADS)
    sc = jnp.einsum('bhqd,bhkd->bhqk', q, k).astype(jnp.float32) * (MEM_HEAD_DIM ** -0.5)
    p = jax.nn.softmax(sc, axis=-1).astype(v.dtype)
    o = jnp.einsum('bhqk,bhkd->bhqd', p, v).transpose(0, 2, 1, 3).reshape(b, s, D_MODEL)
    return o @ w_o

def _sq_relu_mlp(h, w1, w2):
    a = jax.nn.relu(h @ w1)
    return (a * a) @ w2

def second_inputs(seed: int = 0) -> dict:
    key = jax.random.key(seed)
    ks = jax.random.split(key, 24)
    n = lambda k, shape, s: jax.random.normal(k, shape, jnp.float32) * s
    gain = lambda k, shape: 1.0 + 0.02 * jax.random.normal(k, shape, jnp.float32)
    L = DEPTH
    return {
        "x": n(ks[0], (BATCH, SEQ, D_MODEL), 1.0),
        "mem": n(ks[1], (BATCH, MEM_LEN, D_MODEL), 1.0),
        "w_in": n(ks[2], (L, D_MODEL, IN_COLS_2), D_MODEL ** -0.5),
        "b_forget": 3.0 + n(ks[3], (L, N_FOX_HEADS), 1.0),
        "lambda_q1": n(ks[4], (L, HEAD_DIM), 0.1),
        "lambda_k1": n(ks[5], (L, HEAD_DIM), 0.1),
        "lambda_q2": n(ks[6], (L, HEAD_DIM), 0.1),
        "lambda_k2": n(ks[7], (L, HEAD_DIM), 0.1),
        "g_subln": gain(ks[8], (L, DIFF_V_DIM)),
        "rel_bias": n(ks[9], (N_BUCKETS, N_DIFF_HEADS), 0.5),
        "w_diff_out": n(ks[10], (L, DIFF_V_W, D_MODEL), DIFF_V_W ** -0.5),
        "w_fox_out": n(ks[11], (L, FOX_W, D_MODEL), FOX_W ** -0.5),
        "w_o": n(ks[12], (L, D_MODEL, D_MODEL), D_MODEL ** -0.5),
        "g_mix": gain(ks[13], (L, D_MODEL)),
        "g_mem_q": gain(ks[14], (L, D_MODEL)),
        "g_mem_kv": gain(ks[15], (L, D_MODEL)),
        "w_q_mem": n(ks[16], (L, D_MODEL, D_MODEL), D_MODEL ** -0.5),
        "w_kv_mem": n(ks[17], (L, D_MODEL, 2 * D_MODEL), D_MODEL ** -0.5),
        "w_o_mem": n(ks[18], (L, D_MODEL, D_MODEL), D_MODEL ** -0.5),
        "g_mlp": gain(ks[19], (L, D_MODEL)),
        "w1": n(ks[20], (L, D_MODEL, D_FF), D_MODEL ** -0.5),
        "w2": n(ks[21], (L, D_FF, D_MODEL), D_FF ** -0.5),
        "g_final": gain(ks[22], (D_MODEL,)),
    }

def second_block(x, mem, w_in, b_forget, lambda_q1, lambda_k1, lambda_q2, lambda_k2, g_subln,
              rel_bias, w_diff_out, w_fox_out, w_o, g_mix, g_mem_q, g_mem_kv, w_q_mem,
              w_kv_mem, w_o_mem, g_mlp, w1, w2, g_final):
    for l in range(DEPTH):
        lambda_init = 0.8 - 0.6 * math.exp(-0.3 * l)
        x = x + _hybrid_mixer(_rmsnorm_2(x, g_mix[l]), w_in[l], b_forget[l], lambda_q1[l],
                              lambda_k1[l], lambda_q2[l], lambda_k2[l], g_subln[l], rel_bias,
                              w_diff_out[l], w_fox_out[l], w_o[l], lambda_init)
        x = x + _memory_cross_attention(_rmsnorm_2(x, g_mem_q[l]), _rmsnorm_2(mem, g_mem_kv[l]),
                                        w_q_mem[l], w_kv_mem[l], w_o_mem[l])
        x = x + _sq_relu_mlp(_rmsnorm_2(x, g_mlp[l]), w1[l], w2[l])
    return _rmsnorm_2(x, g_final)


def setup_inputs(seed=0):
    out = dict(first_inputs(seed))
    for name, value in second_inputs(seed + 1).items():
        if name != "x":
            out[name + "_2"] = value
    return out


def reference(
    x, c, ctx, c_ctx, w_mod, b_mod, pre_g, post_g, w_in, conv_w, conv_b, rpb, w_out_conv,
    w_out_attn, w_o, mem_2, w_in_2, b_forget_2, lambda_q1_2, lambda_k1_2, lambda_q2_2,
    lambda_k2_2, g_subln_2, rel_bias_2, w_diff_out_2, w_fox_out_2, w_o_2, g_mix_2, g_mem_q_2,
    g_mem_kv_2, w_q_mem_2, w_kv_mem_2, w_o_mem_2, g_mlp_2, w1_2, w2_2, g_final_2,
):
    x = first_block(
        x, c, ctx, c_ctx, w_mod, b_mod, pre_g, post_g, w_in, conv_w, conv_b, rpb, w_out_conv,
        w_out_attn, w_o,
    )
    return second_block(
        x, mem_2, w_in_2, b_forget_2, lambda_q1_2, lambda_k1_2, lambda_q2_2, lambda_k2_2,
        g_subln_2, rel_bias_2, w_diff_out_2, w_fox_out_2, w_o_2, g_mix_2, g_mem_q_2, g_mem_kv_2,
        w_q_mem_2, w_kv_mem_2, w_o_mem_2, g_mlp_2, w1_2, w2_2, g_final_2,
    )


_drawn_inputs = setup_inputs


def setup_inputs(seed=0):
    import zlib

    import numpy as np

    out = dict(_drawn_inputs(seed))
    spreads = {}
    factors = {'conv_b': 7.726,
     'rpb': 8.0,
     'lambda_q1_2': 8.0,
     'lambda_k1_2': 3.715,
     'lambda_q2_2': 3.159,
     'g_subln_2': 8.0,
     'g_mix_2': 3.924,
     'g_mem_q_2': 8.0,
     'g_mem_kv_2': 8.0,
     'g_mlp_2': 8.862,
     'g_final_2': 8.749}
    for name, (base, spread) in spreads.items():
        noise = np.random.default_rng([zlib.crc32(name.encode()), seed]).standard_normal(out[name].shape)
        drawn = base * np.exp(spread * noise) if base else spread * noise
        out[name] = __import__('jax').numpy.asarray(drawn.astype(out[name].dtype))
    for name, factor in factors.items():
        out[name] = (out[name] * factor).astype(out[name].dtype)
    return out
```

```python
import concourse.bass as bass
from concourse import mybir
from contextlib import ExitStack
import math
import numpy as np

D = 1024
SEQ = 512
KT = D // 128
GW, GR = 64, 8
CTX = 256
WIN = 16
JW = 256
MASKED = -1e30
EPS = 1e-6
LAMBDA_INIT = 0.8 - 0.6 * float(np.exp(-0.3 * 0))
STRIP = 32 * 15
NDIST = 640

PHASES = [("V", 4, 6), ("QK", 8, 4), ("CONV", 16, 2), ("ZB", 4, 2), ("GO", 16, 2), ("WO", 8, 2),
          ("MKV", 8, 2), ("FL", 1, 2), ("V2", 4, 4), ("DQK", 4, 2), ("FQK", 4, 2),
          ("GO2", 12, None), ("WO2", 4, 2), ("QM", 4, 2), ("OM", 4, 2), ("MLP", 32, 2)]
JB, GB = {}, {}
_j = _g = 0
for _name, _n, _per in PHASES:
    JB[_name], GB[_name] = _j, _g
    _j += _n
    _g += _n * _per if _per else (_n // 3) * 8
NJ, NG = _j, _g

P_PRE, P_POST, P_BMOD, P_CW, P_CB = 0, 8, 16, 40, 64
P_MIX, P_MQ, P_MKV, P_MLP, P_FIN, P_C = 72, 80, 88, 96, 104, 112
P_BF = 128
NPAR = 129


class Chain:

    def __init__(self, eng, sem):
        self.eng, self.sem, self.n, self.off = eng, sem, 0, 0

    def link(self, ins):
        self.n += 1
        ins.then_inc(self.sem, 1)
        self.eng.wait_ge(self.sem, self.off + self.n)

    def loop(self, it, per):
        self.off, self.start, self.per = it * per, self.n, per

    def done(self, iterations):
        assert self.n - self.start == self.per, (self.n - self.start, self.per)
        self.n, self.off = self.start + self.per * iterations, 0


class Stage:

    def __init__(self, n, g0, ot0, cols, P, osb, pt):
        self.n, self.g0, self.ot0, self.cols, self.P, self.osb, self.pt = n, g0, ot0, cols, P, osb, pt


def build(nc, A, out):
    f32, f32r = mybir.dt.float32, mybir.dt.float32r
    ALU, ACT, AX = mybir.AluOpType, mybir.ActivationFunctionType, mybir.AxisListType
    ctx = ExitStack()
    with ctx:
        def sb(name, shape, dt=f32):
            return ctx.enter_context(nc.sbuf_tensor(name, shape, dt))

        def sem(name):
            return ctx.enter_context(nc.semaphore(name))

        raw = sb("raw", [128, 2, KT, JW])
        wh = sb("wh", [128, 2, KT, JW], f32r)
        wl = sb("wl", [128, 2, KT, JW], f32r)
        par = sb("par", [128, NPAR])
        ident = sb("ident", [128, 128])
        ones = sb("ones", [128, 128])
        small = sb("small", [128, 168])
        silr = sb("silr", [128, 2, 16], f32r)
        F_KB, R_KB = 29.5, 128
        farena = sb("farena", [128, int(F_KB * 256)])
        with nc.sbuf_tensor("wmod_a", [128, KT, 2 * D], f32) as wmod_a:
            pass
        rarena = sb("rarena", [128, R_KB * 256], f32r)

        def view(arena, kb, shape):
            n = int(np.prod(shape))
            ap = arena[:, int(kb * 256):int(kb * 256) + n]
            if len(shape) == 1:
                return ap
            names = "abc"[:len(shape)]
            return ap.rearrange("p (%s) -> p %s" % (" ".join(names), " ".join(names)),
                                **{c: s for c, s in zip(names, shape)})

        def R(kb, *shape):
            n = int(np.prod(shape)) / 256
            return view(rarena, kb, shape), view(rarena, kb + n, shape)

        def F(kb, *shape):
            return view(farena, kb, shape)

        h = R(0, KT, SEQ)
        V = R(32, 4, D)
        Vc = R(64, 2, D)
        hc = R(80, KT, CTX)
        hseam = R(96, KT, 128)
        qs = [R(96, SEQ), R(100, SEQ)]
        ks = [R(104, SEQ), R(108, SEQ)]
        kcs = [R(112, CTX), R(114, CTX)]
        pt = [R(116, SEQ), R(120, SEQ)]
        cin = R(32, KT, SEQ)
        og = R(64, KT, SEQ)
        merged = R(96, KT, SEQ)
        hm = R(0, KT, CTX)
        mk, mv = R(32, KT, CTX), R(48, 2, D)
        mkv_all = rarena[:, 32 * 256:64 * 256].bitcast(f32)
        h2 = R(64, KT, SEQ)
        v2 = R(0, 4, D)
        cumst = [view(rarena, 48 + 2 * n, (SEQ,)) for n in range(4)]
        cum16, ncum16 = view(rarena, 120, (SEQ,)), view(rarena, 122, (SEQ,))
        sel16 = view(rarena, 124, (8, 128))
        q2, k2, pt2 = qs, ks, [R(112, SEQ), R(116, SEQ)]
        oa2, ob2 = R(32, 4, SEQ), R(48, 4, SEQ)
        xg = R(0, KT, SEQ)
        qm = [R(64, 2, SEQ), R(72, 2, SEQ)]
        ptm = [R(80, CTX), R(82, CTX)]
        om = R(96, KT, SEQ)
        act2 = R(32, KT, SEQ)

        x0, ctx0 = F(0, KT, SEQ), F(16, KT, CTX)
        sq0 = [F(24, SEQ), F(26, SEQ)]
        rstd_x, rstd_c = F(24, SEQ), F(28, CTX)
        cos_t, sin_t, ptile = F(0, SEQ), F(2, SEQ), [F(4, SEQ), F(6, SEQ)]
        rope_a, rope_b = F(8, SEQ), F(10, SEQ)
        strip = F(12, 4, STRIP)
        bm = [F(19.5, 256), F(20.5, 256)]
        wmask = F(21.5, 3, 256)
        osb = [F(24.5, 128), F(25, 128)]
        stage, sin_q = F(25.5, SEQ), F(27.5, SEQ)
        c_t, u_t, y_t, sg_t = F(0, 2, SEQ), F(4, 2, SEQ), F(8, 2, SEQ), F(12, 2, SEQ)
        o_in = [F(16, 2, SEQ), F(20, 2, SEQ)]
        onehot, relb, relt, lamv = F(4, NDIST), F(8, 128), F(9, NDIST), F(19.5, 4, 64)
        h2f, fl_sel = [F(26, SEQ), F(20, SEQ)], F(24, 8, 128)
        ga_t, gb_t, ya_t, yb_t = F(0, 2, SEQ), F(4, 2, SEQ), F(8, 2, SEQ), F(12, 2, SEQ)
        y = F(0, KT, SEQ)
        sq, acc_sq = F(16, SEQ), F(18, SEQ)
        sqm, mem, rstd_m = F(14, CTX), F(20, KT, CTX), F(28, CTX)
        xin, rstd, tmp = [F(20, SEQ), F(22, SEQ)], F(24, SEQ), F(26, SEQ)
        fl_t = [F(16 + 2 * n, SEQ) for n in range(4)]
        ptile2, strip2, odiff = [F(0, SEQ), F(2, SEQ)], [F(4, SEQ), F(6, SEQ)], F(8, 16, 128)
        osb2 = [F(16, 128), F(16.5, 128)]
        cmask, subsq, gsub = F(17, 128), F(17.5, 128), F(18, 128)
        ptilem, osbm = [F(20, CTX), F(21, CTX)], [F(22, 256), F(23, 256)]
        mt = [F(20, SEQ), F(22, SEQ)]

        eps = small[:, 0:1]
        mod_ax, mod_bx, mod_ac, mod_bc = (small[:, 1 + 8 * n:9 + 8 * n] for n in range(4))
        gtp = small[:, 33:41]
        negmax, rowsum, rinv = small[:, 41:49], small[:, 49:57], small[:, 57:65]
        mods = small[:, 65:113].rearrange("p (m s) -> p m s", s=2)
        nlam = small[:, 113:114]
        lamt = small[:, 114:118]
        ssum, srst = small[:, 118:134], small[:, 134:150]
        silc = small[:, 150:166]
        one1 = ones[:, 0:1]

        acc = [ctx.enter_context(nc.psum_tensor(f"acc{n}", [128, SEQ], f32)) for n in range(2)]
        S = [ctx.enter_context(nc.psum_tensor(f"S{n}", [128, SEQ], f32)) for n in range(2)]
        T = [ctx.enter_context(nc.psum_tensor(f"T{n}", [128, SEQ], f32)) for n in range(2)]
        O = [ctx.enter_context(nc.psum_tensor(f"O{n}", [128, SEQ], f32)) for n in range(2)]

        o_dram = nc.dram_tensor("o_scratch", (KT // 2, 2, 128, SEQ), f32, kind="Internal").ap()
        x_dram = nc.dram_tensor("x_scratch", (128, KT, SEQ), f32, kind="Internal").ap()
        mkv_dram = nc.dram_tensor("mkv_scratch", (128, 32 * 256), f32, kind="Internal").ap()
        t_dram = nc.dram_tensor("t_scratch", (4, NDIST), f32, kind="Internal").ap()

        sems = {}

        def s_(name):
            if name not in sems:
                sems[name] = sem(name)
            return sems[name]

        def W(eng, name, value):
            if not (isinstance(value, int) and value <= 0):
                eng.wait_ge(s_(name), value)

        def job_no(it, per, base):
            return it * per + base

        def half(it, per, base):
            return it * (per // 2) + base // 2

        def split_hi(act, it, per, base):
            s = base % 2
            act.wait_ge(s_(f"raw_loaded{s}"), half(it, per, base) * 16 + 16)
            nc.scalar.activation(wh[:, s], raw[:, s], ACT.Copy).then_inc(s_("hi_done"), 1)

        def split_job(eng, it, per, base):
            s = base % 2
            eng.wait_ge(s_("hi_done"), job_no(it, per, base) + 1)
            eng.tensor_tensor(wl[:, s], raw[:, s], wh[:, s].bitcast(f32), ALU.subtract)\
               .then_inc(s_("lo_done"), 1)

        def acc_wait_free(pe, it, per, base):
            pe.wait_ge(s_(f"acc_free{base % 2}"), half(it, per, base) + 1)

        def acc_wait_ready(eng, it, per, base):
            eng.wait_ge(s_("acc_ready"), job_no(it, per, base) + 1)

        def wait_evacuated(eng, it, per, base):
            eng.wait_ge(s_(f"acc_free{base % 2}"), half(it, per, base) + 2)

        def free_acc(ins, base):
            ins.then_inc(s_(f"acc_free{base % 2}"), 1)

        block = ctx.enter_context(nc.Block())

        NB = Stage(8, 0, 0, lambda i: SEQ, ptile, osb, pt)
        DF = Stage(8, 64, 32, lambda i: 128 * (i // 2 + 1), ptile2, osb2, pt2)
        FX = Stage(8, 96, 32, lambda i: 128 * (i // 2 + 1), ptile2, osb2, pt2)
        MM = Stage(4, 128, 48, lambda i: CTX, ptilem, osbm, ptm)

        def step_no(s, it, pc, i):
            return it * (2 * s.n) + (s.g0 + s.n * pc + i)

        def step_half(s, it, pc, i):
            return it * s.n + (s.g0 + s.n * pc + i) // 2

        def ot_no(s, it, pc, i):
            return it * 8 + (s.ot0 + 4 * pc + i // 2 - 2)

        @block.sync
        def _(sp):
            sp.dma_start(par[:], A["par"]).then_inc(s_("par_in"), 16)
            for n in range(2):
                sp.dma_start(ctx0[:, 4 * n:4 * n + 4], A["ctx"][:, 4 * n:4 * n + 4]).then_inc(s_(f"ctx_in{n}"), 16)
            for n in range(4):
                sp.dma_start(x0[:, 2 * n:2 * n + 2], A["x_grid"][:, 2 * n:2 * n + 2]).then_inc(s_(f"x_in{n}"), 16)
            for n in range(4):
                sp.dma_start(wmod_a[:, :, 512 * n:512 * n + 512], A["wmod"][:, :, 512 * n:512 * n + 512])\
                  .then_inc(s_(f"wmod_in{n}"), 16)
            for j in range(2):
                sp.dma_start(raw[:, j], A["w"][j]).then_inc(s_(f"raw_loaded{j}"), 16)
            with sp.Fori(0, (NJ - 2) // 2) as it:
                for c in range(2):
                    sp.wait_ge(s_("hi_done"), it * 2 + (c + 1))
                    sp.wait_ge(s_("lo_done"), it * 2 + (c + 1))
                    sp.dma_start(raw[:, c], A["w"][bass.ds(it * 2 + (c + 2), 1)].rearrange("a p k n -> (a p) k n"))\
                      .then_inc(s_(f"raw_loaded{c}"), 16)
            for j in range(2 + (NJ - 2) // 2 * 2, NJ):
                sp.wait_ge(s_("hi_done"), j - 1)
                sp.wait_ge(s_("lo_done"), j - 1)
                sp.dma_start(raw[:, j % 2], A["w"][j]).then_inc(s_(f"raw_loaded{j % 2}"), 16)
            for k in range(KT):
                sp.wait_ge(s_("final_ready"), k + 1)
                sp.dma_start(out[:, k], y[:, k]).then_inc(s_("out_stored"), 16)
            sp.wait_ge(s_("out_stored"), 16 * KT)

        @block.tensor
        def _(pe):
            mm = nc.tensor.matmul

            def mm3(o, w, m, start, stop):
                mm(o, w[0], m[0], start=start, stop=False)
                mm(o, w[0], m[1], start=False, stop=False)
                return mm(o, w[1], m[0], start=False, stop=stop)

            def at(pair, *idx):
                return tuple(t.__getitem__(idx) for t in pair)

            def wt(s, k, t):
                return wh[:, s, k, 128 * t:128 * t + 128], wl[:, s, k, 128 * t:128 * t + 128]

            def tiles_job(it, per, base, gper, gbase, x, n=SEQ, k_ready=None):
                s = base % 2
                pe.wait_ge(s_("lo_done"), job_no(it, per, base) + 1)
                for t in range(2):
                    acc_wait_free(pe, it, gper, gbase + t)
                    for k in range(KT):
                        if k_ready and t == 0:
                            pe.wait_ge(s_(k_ready[0]), k_ready[1] + k + 1)
                        last = mm3(acc[(gbase + t) % 2][:, 0:n], wt(s, k, t), at(x, slice(None), k),
                                   k == 0, k == KT - 1)
                    last.then_inc(s_("acc_ready"), 1)

            def token_group(base, gbase, it, gper, stat, n=JW, rows=KT):
                s = base % 2
                acc_wait_free(pe, it, gper, gbase)
                for k in range(KT):
                    st = stat(k)
                    o = acc[gbase % 2][:, 0:n]
                    mm(o, st[0], wh[:, s, k], start=k == 0, stop=False)
                    mm(o, st[0], wl[:, s, k], start=False, stop=False)
                    last = mm(o, st[1], wh[:, s, k], start=False, stop=k == KT - 1)
                last.then_inc(s_("acc_ready"), 1)

            def norm_sum(bank, src, n=SEQ):
                return mm(bank[:, 0:n], ones[:], src, start=True, stop=True)

            pe.wait_ge(s_("consts_ready"), 3)
            for n in range(2 * KT):
                w, bank = (CTX, S[1]) if n < KT else (SEQ, S[0])
                pe.wait_ge(s_("sq0_ready"), n + 1)
                mm(bank[:, 0:w], ones[:], sq0[n % 2][:, 0:w], start=n % KT == 0, stop=n % KT == KT - 1)\
                    .then_inc(s_("sq0_used"), 1)

            pe.wait_ge(s_("silc_ready"), 1)
            for m in range(16):
                if m % 4 == 0:
                    pe.wait_ge(s_(f"wmod_in{m // 4}"), 16)
                for k in range(KT):
                    last = mm(T[0][:, 2 * m:2 * m + 2], wmod_a[:, k, 128 * m:128 * m + 128],
                              silc[:, 2 * k:2 * k + 2], start=k == 0, stop=k == KT - 1)
            last.then_inc(s_("mod_done"), 1)

            def h_block(b):
                if b < 3:
                    return lambda k: at(h, slice(None), k, slice(64 + 128 * b, 192 + 128 * b))
                return lambda k: at(hseam, slice(None), k)

            pe.wait_ge(s_("hc_ready"), KT)
            with pe.Fori(0, 2) as it:
                for c in range(2):
                    base, g = JB["V"] + c, GB["V"] + 6 * c
                    pe.wait_ge(s_("lo_done"), it * 2 + (base + 1))
                    for b in range(2):
                        token_group(base, g + b, it, 12,
                                    lambda k, b=b: at(hc, slice(None), k, slice(128 * b, 128 * b + 128)))
                    if c == 0:
                        pe.wait_ge(s_("h_ready"), KT)
                    for b in range(4):
                        if c == 0 and b == 3:
                            pe.wait_ge(s_("seam_ready"), 4)
                        token_group(base, g + 2 + b, it, 12, h_block(b))
            pe.wait_ge(s_("relb_in"), 32)
            pe.wait_ge(s_("relb_ready"), 1)
            mm(S[0][:], relb[0:32], onehot[0:32, 0:SEQ], start=True, stop=True)
            mm(S[1][:, 0:128], relb[0:32], onehot[0:32, SEQ:NDIST], start=True, stop=True)\
                .then_inc(s_("relt_done"), 1)

            def chunk(it, pc, i):
                base, g = JB["QK"] + pc + 1, GB["QK"] + 4 * (pc + 1)
                s = base % 2
                if i == 0:
                    pe.wait_ge(s_("lo_done"), it * 2 + (base + 1))
                if i in (0, 2, 4, 5):
                    gi = {0: 0, 2: 1, 4: 2, 5: 3}[i]
                    acc_wait_free(pe, it, 8, g + gi)
                if i < 4:
                    t = i // 2
                    for k in range(4 * (i % 2), 4 * (i % 2) + 4):
                        last = mm3(acc[(g + t) % 2][:], wt(s, k, t), at(h, slice(None), k), k == 0, k == KT - 1)
                    if i % 2:
                        last.then_inc(s_("acc_ready"), 1)
                else:
                    c0 = 128 * (i - 4)
                    for k in range(KT):
                        last = mm3(acc[(g + i) % 2][:, 0:128], wt(s, k, 1),
                                   at(hc, slice(None), k, slice(c0, c0 + 128)), k == 0, k == KT - 1)
                    last.then_inc(s_("acc_ready"), 1)

            def scores_nb(it, pc, i, o):
                qb, e, sl = i // 2, i % 2, pc % 2
                if i == 0:
                    pe.wait_ge(s_("rope_lo"), it * 4 + 2 * pc + 2)
                    for x in range(2):
                        wait_evacuated(pe, it, 8, GB["QK"] + 4 * pc + 2 + x)
                r = slice(64 * e, 64 * e + 64)
                q = at(qs[sl], r, slice(128 * qb, 128 * qb + 128))
                kk = at(ks[sl], r)
                seam = tuple(t.rearrange("p (c n) -> p c n", n=64)[:, 7::-7, :] for t in kk)
                if qb == 0:
                    sets = [(0, 128, seam), (128, 128, at(kk, slice(None), slice(64, 192)))]
                elif qb == 3:
                    sets = [(0, 128, at(kk, slice(None), slice(320, 448))), (128, 128, seam)]
                else:
                    sets = [(0, 256, at(kk, slice(None), slice(128 * qb - 64, 128 * qb + 192)))]
                for c0, n, m in sets + [(256, 256, at(kcs[sl], r))]:
                    last = mm3(o[:, c0:c0 + n], q, m, True, True)
                return last

            def values_nb(it, pc, i, o, p):
                if i < 0:
                    pc, i = pc - 1, i + 8
                qb, e = i // 2, i % 2
                c0 = it * 256 + (128 * pc + 64 * e)
                for b in range(4):
                    vb = at(V, slice(None), (qb - 1) % 4 if b == 0 else qb) if b < 2 else at(Vc, slice(None), b - 2)
                    last = mm3(o[:, 0:64], at(p, slice(None), slice(128 * b, 128 * b + 128)),
                               tuple(t[:, bass.ds(c0, 64)] for t in vb), b == 0, b == 3)
                return last

            def scores_causal(fox):
                def scores(it, pc, i, o):
                    qb, e, sl = i // 2, i % 2, pc % 2
                    n = 128 * (qb + 1)
                    if i == 0:
                        for x in range(2):
                            wait_evacuated(pe, 0, 2, GB["DQK"] + 2 * (pc + 4 * fox) + x)
                    r = slice(64 * e, 64 * e + 64)
                    last = mm3(o[:, 0:n], at(q2[sl], r, slice(128 * qb, n)), at(k2[sl], r, slice(0, n)), True, not fox)
                    if fox:
                        hd = 2 * pc + e
                        mm(o[:, 0:n], sel16[0:16, hd], ncum16[0:16, 0:n], start=False, stop=False)
                        for b in range(qb + 1):
                            last = mm(o[:, 128 * b:128 * b + 128], cum16[0:16, 128 * qb:n], sel16[0:16, hd],
                                      start=False, stop=b == qb)
                    return last
                return scores

            def values_causal(fox):
                def values(it, pc, i, o, p):
                    if i < 0:
                        pc, i = pc - 1, i + 8
                    qb, e = i // 2, i % 2
                    c0, w = (512 + 128 * pc + 64 * e, 64) if fox else (128 * pc, 128)
                    for b in range(qb + 1):
                        last = mm3(o[:, 0:w], at(p, slice(None), slice(128 * b, 128 * b + 128)),
                                   at(v2, slice(None), b, slice(c0, c0 + w)), b == 0, b == qb)
                    return last
                return values

            def scores_mm(it, pc, i, o):
                if i == 0:
                    pe.wait_ge(s_("qm_lo"), 2 * pc + 2)
                if i == 0 and pc == 0:
                    pe.wait_ge(s_("mkv_back"), 16)
                for t in range(2):
                    last = mm3(o[:, 0:CTX], at(qm[pc % 2], slice(None), t, slice(128 * i, 128 * i + 128)),
                               at(mk, slice(None), 2 * pc + t), t == 0, t == 1)
                return last

            def values_mm(it, pc, i, o, p):
                if i < 0:
                    pc, i = pc - 1, i + 4
                for b in range(2):
                    last = mm3(o[:, 0:256], at(p, slice(None), slice(128 * b, 128 * b + 128)),
                               at(mv, slice(None), b, slice(256 * pc, 256 * pc + 256)), b == 0, b == 1)
                return last

            def attend(s, it, pc, first, last_pair, scores, values, part=None):
                def made(j):
                    return (j >= 0 or not first) and j < s.n
                for i in range(s.n + (4 if last_pair else 0)):
                    g, gh = step_no(s, it, pc, i), step_half(s, it, pc, i)
                    a = i % 2
                    if i < s.n:
                        W(pe, "exp_done", g - 1)
                        scores(it, pc, i, S[a]).then_inc(s_("qk_done"), 1)
                        if part:
                            part(it, pc, i)
                    if made(i - 1):
                        pe.wait_ge(s_("exp_done"), g)
                        W(pe, "plo_done", g - 2)
                        b = 1 - a
                        for c0 in range(0, s.cols((i - 1) % s.n), 128):
                            tr = nc.tensor.transpose(T[b][:, c0:c0 + 128], s.P[b][:, c0:c0 + 128], ident[:])
                        tr.then_inc(s_("t_done"), 1)
                    if s is MM and made(i - 3):
                        b = 1 - a
                        pe.wait_ge(s_(f"o_free{b}"), step_half(s, it, pc, i - 3) + 1)
                        for c0 in range(0, 256, 128):
                            tr = nc.tensor.transpose(O[b][:, 256 + c0:384 + c0], osbm[b][:, c0:c0 + 128], ident[:])
                        tr.then_inc(s_("ot_done"), 1)
                    if s in (NB, FX) and a == 0 and made(i - 4) and made(i - 3):
                        for b in range(2):
                            pe.wait_ge(s_(f"o_free{b}"), step_half(s, it, pc, i - 4) + 1)
                        W(pe, "ot_free", ot_no(s, it, pc, i))
                        nc.tensor.transpose(O[1][:, 256:384], s.osb[(i // 2) % 2][:], ident[:])\
                            .then_inc(s_("ot_done"), 1)
                    if made(i - 2):
                        pe.wait_ge(s_("plo_done"), g - 1)
                        W(pe, f"o_free{a}", gh - 1)
                        if s in (NB, FX) and a == 1:
                            W(pe, "ot_free", ot_no(s, it, pc, i - 1) + 1)
                        if s is MM:
                            W(pe, "ot_free", s.ot0 + s.n * pc + i - 3)
                        values(it, pc, i - 2, O[a], s.pt[a]).then_inc(s_("pv_done"), 1)

            base, g = JB["QK"], GB["QK"]
            pe.wait_ge(s_("lo_done"), base + 1)
            for t in range(2):
                acc_wait_free(pe, 0, 2, g + t)
                for k in range(KT):
                    last = mm3(acc[(g + t) % 2][:], wt(base % 2, k, t), at(h, slice(None), k), k == 0, k == KT - 1)
                last.then_inc(s_("acc_ready"), 1)
            for x in range(2):
                acc_wait_free(pe, 0, 2, g + 2 + x)
                for k in range(KT):
                    last = mm3(acc[(g + x) % 2][:, 0:128], wt(base % 2, k, 1),
                               at(hc, slice(None), k, slice(128 * x, 128 * x + 128)), k == 0, k == KT - 1)
                last.then_inc(s_("acc_ready"), 1)

            def nb_part(it, pc, i):
                if i < 6:
                    chunk(it, pc, i)

            attend(NB, 0, 0, True, False, scores_nb, values_nb, nb_part)
            with pe.Fori(0, 3) as it:
                for pc in (1, 2):
                    attend(NB, it, pc, False, False, scores_nb, values_nb, nb_part)
            attend(NB, 0, 7, False, True, scores_nb, values_nb)

            def jobs(name, count, x, per=2, k_ready=None):
                with pe.Fori(0, count // per) as it:
                    for c in range(per):
                        tiles_job(it, per, JB[name] + c, 2 * per, GB[name] + 2 * c, x)

            jobs("CONV", 16, h, 4)
            jobs("ZB", 4, h)

            with pe.Fori(0, 4) as it:
                for c in range(4):
                    x = (h, cin, h, og)[c]
                    if c == 1:
                        pe.wait_ge(s_("cin_ready"), KT)
                    if c == 3:
                        pe.wait_ge(s_("og_ready"), KT)
                    tiles_job(it, 4, JB["GO"] + c, 8, GB["GO"] + 2 * c, x)

            for c in range(4):
                tiles_job(0, 2, JB["WO"] + 2 * c, 2, GB["WO"] + 4 * c, merged, k_ready=("merged_ready", 0) if c == 0 else None)
                tiles_job(0, 2, JB["WO"] + 2 * c + 1, 2, GB["WO"] + 4 * c + 2,
                          tuple(silr[:, n].rearrange("p (k s) -> p k s", s=2) for n in range(2)), 2)
                if c == 1:
                    pe.wait_ge(s_("accm_done"), KT)
                    norm_sum(S[1], rstd_m[:], CTX).then_inc(s_("summ_done"), 1)

            for c in range(8):
                base, g = JB["MKV"] + c, GB["MKV"] + 2 * c
                if c == 0:
                    pe.wait_ge(s_("hm_ready"), KT)
                if c < 4:
                    tiles_job(0, 2, base, 2, g, hm, CTX)
                else:
                    pe.wait_ge(s_("lo_done"), base + 1)
                    for b in range(2):
                        token_group(base, g + b, 0, 2,
                                    lambda k, b=b: at(hm, slice(None), k, slice(128 * b, 128 * b + 128)))
                if c == 0:
                    pe.wait_ge(s_("accy_done"), KT)
                    norm_sum(S[0], acc_sq[:]).then_inc(s_("sumy_done"), 1)
                if c == 4:
                    pe.wait_ge(s_("acc1_done"), KT)
                    norm_sum(S[0], acc_sq[:]).then_inc(s_("sum1_done"), 1)

            base, g = JB["FL"], GB["FL"]
            pe.wait_ge(s_("lo_done"), base + 1)
            pe.wait_ge(s_("h2_ready"), KT)
            for x in range(2):
                acc_wait_free(pe, 0, 2, g + x)
                for k in range(KT):
                    last = mm3(acc[(g + x) % 2][:, 0:256], wt(base % 2, k, 0),
                               at(h2, slice(None), k, slice(256 * x, 256 * x + 256)), k == 0, k == KT - 1)
                last.then_inc(s_("acc_ready"), 1)

            for c in range(4):
                base, g = JB["V2"] + c, GB["V2"] + 4 * c
                pe.wait_ge(s_("lo_done"), base + 1)
                for b in range(4):
                    token_group(base, g + b, 0, 2,
                                lambda k, b=b: at(h2, slice(None), k, slice(128 * b, 128 * b + 128)))

            def part2(n):
                base, g = JB["DQK"] + n, GB["DQK"] + 2 * n

                def part(it, pc, i):
                    if i == 0:
                        pe.wait_ge(s_("lo_done"), base + 1)
                    if i in (0, 3):
                        acc_wait_free(pe, 0, 2, g + i // 3)
                    t, ks_ = (0, [range(0, 3), range(3, 6), range(6, 8)]) if i < 3 else \
                             (1, [range(0, 3), range(3, 6), range(6, 8)])
                    if i < 6:
                        for k in ks_[i % 3]:
                            last = mm3(acc[(g + t) % 2][:], wt(base % 2, k, t), at(h2, slice(None), k),
                                       k == 0, k == KT - 1)
                        if i % 3 == 2:
                            last.then_inc(s_("acc_ready"), 1)
                return part

            tiles_job(0, 2, JB["DQK"], 2, GB["DQK"], h2)
            for pc in range(4):
                attend(DF, 0, pc, pc == 0, pc == 3, scores_causal(0), values_causal(0), part2(pc + 1))
            pe.wait_ge(s_("cum_in"), 64)
            pe.wait_ge(s_("sel_ready"), 1)
            for pc in range(4):
                attend(FX, 0, pc, pc == 0, pc == 3, scores_causal(1), values_causal(1), part2(pc + 5) if pc < 3 else None)

            for t in range(16):
                pe.wait_ge(s_("sub_ready"), t + 1)
                W(pe, "subt_lo", t - 1)
                nc.tensor.transpose(T[t % 2][:, 0:128], odiff[:, t], ident[:]).then_inc(s_("subt_done"), 1)
            with pe.Fori(0, 2) as it:
                for c in range(6):
                    base, g = JB["GO2"] + c, GB["GO2"] + 8 * (c // 3) + 2 * (c % 3)
                    if c % 3 < 2:
                        tiles_job(it, 6, base, 16, g, h2)
                        continue
                    pe.wait_ge(s_("lo_done"), it * 6 + (base + 1))
                    pe.wait_ge(s_("subt_lo"), 16)
                    pe.wait_ge(s_("ot_free"), 48)
                    for u in range(4):
                        acc_wait_free(pe, it, 16, g + u)
                        src, k0 = (oa2, 0) if u % 2 == 0 else (ob2, 4)
                        for k in range(4):
                            last = mm3(acc[(g + u) % 2][:], wt(base % 2, k0 + k, u // 2), at(src, slice(None), k),
                                       k == 0, k == 3)
                        last.then_inc(s_("acc_ready"), 1)

            for c in range(4):
                tiles_job(0, 2, JB["WO2"] + c, 2, GB["WO2"] + 2 * c, merged, k_ready=("merged2_ready", 0) if c == 0 else None)

            tiles_job(0, 2, JB["QM"], 2, GB["QM"], xg, k_ready=("xg_ready", 0))
            pe.wait_ge(s_("acc2_done"), KT)
            norm_sum(S[0], acc_sq[:]).then_inc(s_("sum2_done"), 1)

            def partm(n):
                base, g = JB["QM"] + n, GB["QM"] + 2 * n

                def part(it, pc, i):
                    if i == 0:
                        pe.wait_ge(s_("lo_done"), base + 1)
                    if i in (0, 2):
                        acc_wait_free(pe, 0, 2, g + i // 2)
                    t = i // 2
                    for k in range(4 * (i % 2), 4 * (i % 2) + 4):
                        last = mm3(acc[(g + t) % 2][:], wt(base % 2, k, t), at(xg, slice(None), k), k == 0, k == KT - 1)
                    if i % 2:
                        last.then_inc(s_("acc_ready"), 1)
                return part

            pe.wait_ge(s_("rms_ready"), 3)
            for pc in range(4):
                attend(MM, 0, pc, pc == 0, pc == 3, scores_mm, values_mm, partm(pc + 1) if pc < 3 else None)

            pe.wait_ge(s_("ot_free"), 64)
            for c in range(4):
                tiles_job(0, 2, JB["OM"] + c, 2, GB["OM"] + 2 * c, om)

            def quarter(it, per, gper, base, g, q0, made):
                for c in range(8):
                    if c < 4:
                        tiles_job(it, per, base + c, gper, g + 2 * c, xg,
                                  k_ready=("xg_ready", KT) if q0 and c == 0 else None)
                    else:
                        if c == 4:
                            pe.wait_ge(s_("act_ready"), made)
                        tiles_job(it, per, base + c, gper, g + 2 * c, act2)
                    if q0 and c == 0:
                        pe.wait_ge(s_("acc3_done"), KT)
                        norm_sum(S[0], acc_sq[:]).then_inc(s_("sum3_done"), 1)

            quarter(0, 8, 16, JB["MLP"], GB["MLP"], True, 8)
            with pe.Fori(0, 2) as it:
                quarter(it, 8, 16, JB["MLP"] + 8, GB["MLP"] + 16, False, it * 8 + 16)
            quarter(0, 8, 16, JB["MLP"] + 24, GB["MLP"] + 48, False, 32)

            pe.wait_ge(s_("acc4_done"), KT)
            norm_sum(S[0], acc_sq[:]).then_inc(s_("sum4_done"), 1)

        @block.scalar
        def _(act):
            f = nc.scalar.activation
            ex = Chain(act, s_("act_own"))

            def nat(t):
                return t.rearrange("p (c r) -> p c r", r=GR)

            def nat_out(t):
                return t.rearrange("p (r c) -> p c r", c=GW)

            def hi_of(name, it, gper, g, dst, src):
                acc_wait_ready(act, it, gper, g)
                f(dst, src, ACT.Copy).then_inc(s_(name), 1)

            act.wait_ge(s_("par_in"), 16)
            f(silc, par[:, P_C:P_C + 16], ACT.Sigmoid).then_inc(s_("sigc_ready"), 1)
            act.wait_ge(s_("silc_ready"), 1)
            f(silr[:, 0], silc, ACT.Copy).then_inc(s_("silr_hi"), 1)
            for n in range(2 * KT):
                k = n % KT
                if n < KT:
                    act.wait_ge(s_(f"ctx_in{k // 4}"), 16)
                else:
                    act.wait_ge(s_(f"x_in{k // 2}"), 16)
                W(act, "sq0_used", n - 1)
                w, src = (CTX, ctx0) if n < KT else (SEQ, x0)
                f(sq0[n % 2][:, 0:w], src[:, k], ACT.Square).then_inc(s_("sq0_ready"), 1)
                if n == KT:
                    act.wait_ge(s_("sq0_used"), KT)
                    act.wait_ge(s_("consts_ready"), 3)
                    f(rstd_c, S[1][:, 0:CTX], ACT.Sqrt, scale=1.0 / D, bias=eps).then_inc(s_("rms0_ready"), 1)
            act.wait_ge(s_("sq0_used"), 2 * KT)
            f(rstd_x, S[0][:], ACT.Sqrt, scale=1.0 / D, bias=eps).then_inc(s_("rms0_ready"), 1)
            for k in range(KT):
                act.wait_ge(s_("hcf_ready"), k + 1)
                f(hc[0][:, k], ctx0[:, k], ACT.Copy).then_inc(s_("hc_hi"), 1)
                if k == 0:
                    split_hi(act, 0, 2, 0)
            for k in range(KT):
                act.wait_ge(s_("hf_ready"), k + 1)
                f(h[0][:, k], x0[:, k], ACT.Copy).then_inc(s_("h_hi"), 1)
            act.wait_ge(s_("h_ready"), KT)
            act.wait_ge(s_("relb_ready"), 1)
            act.dma_start(relb[0:32, 0:4], A["rel_bias"]).then_inc(s_("relb_in"), 16)
            act.dma_start(onehot[0:32], A["onehot"]).then_inc(s_("relb_in"), 16)
            act.dma_start(relt[0:4], A["masked_rows"]).then_inc(s_("relt_in"), 16)
            act.dma_start(cos_t, A["cos"]).then_inc(s_("rope_in"), 16)
            act.dma_start(sin_t, A["sin"]).then_inc(s_("rope_in"), 16)
            act.dma_start(sin_q, A["sin_eighth"]).then_inc(s_("rope_in"), 16)
            act.dma_start(wmask, A["wmask"]).then_inc(s_("wmask_in"), 16)
            act.dma_start(lamv, A["lam"]).then_inc(s_("lam_in"), 16)

            with act.Fori(0, 2) as it:
                for c in range(2):
                    split_hi(act, it, 2, JB["V"] + c + 1)
                    for gi in range(6):
                        g = GB["V"] + 6 * c + gi
                        dst = Vc[0][:, gi] if gi < 2 else V[0][:, gi - 2]
                        hi_of("v_hi", it, 12, g, dst[:, bass.ds(it * 512 + 256 * c, 256)], acc[g % 2][:, 0:256])
            act.wait_ge(s_("lam_sum"), 1)
            f(lamt[:, 2:4], lamt[:, 0:2], ACT.Exp).then_inc(s_("lam_exp"), 1)
            act.wait_ge(s_("relt_sum"), 1)
            act.dma_start(t_dram, relt[0:4]).then_inc(s_("relt_out"), 16)

            def load_strips(it, pc):
                for e in range(2):
                    hd = it * 4 + (2 * pc + e)
                    if isinstance(it, int):
                        src = A["rpb"][hd]
                    else:
                        src = A["rpb"][bass.ds(hd, 1)].rearrange("a n -> (a n)")
                    src = bass.AP(src.tensor, src.offset, [[15, 16], [1, 8], [1, STRIP]])
                    act.dma_start(strip[:, 2 * (pc % 2) + e], src).then_inc(s_(f"strip_in{pc % 2}"), 16)

            load_strips(0, 0)
            load_strips(0, 1)
            split_hi(act, 0, 2, JB["QK"] + 1)

            def rope_hi(it, pc, x):
                act.wait_ge(s_("rope_sum"), it * 4 + (2 * pc + x) + 1)
                f((qs, ks)[x][pc % 2][0], rope_a, ACT.Copy).then_inc(s_("rope_hi"), 1)

            def kc_hi(it, pc, x):
                g = GB["QK"] + 4 * pc + 2 + x
                acc_wait_ready(act, it, 8, g)
                f(kcs[pc % 2][0][:, 128 * x:128 * x + 128], acc[g % 2][:, 0:128], ACT.Copy).then_inc(s_("kc_hi"), 1)

            rope_hi(0, 0, 0)
            rope_hi(0, 0, 1)
            kc_hi(0, 0, 0)
            kc_hi(0, 0, 1)

            def attend(s, it, pc, first, last_pair, extra=None):
                def made(j):
                    return (j >= 0 or not first) and j < s.n
                for i in range(s.n + (4 if last_pair else 0)):
                    g = step_no(s, it, pc, i)
                    a, b = i % 2, 1 - i % 2
                    if i < s.n:
                        act.wait_ge(s_("max_done"), g + 1)
                        W(act, "t_done", g - 1)
                        n, cc = s.cols(i), i % 8
                        f(s.P[a][:, 0:n], S[a][:, 0:n], ACT.Exp, bias=negmax[:, cc:cc + 1],
                          accum_out=rowsum[:, cc:cc + 1]).then_inc(s_("exp_done"), 1)
                    if made(i - 1):
                        n = s.cols((i - 1) % s.n)
                        act.wait_ge(s_("t_done"), g)
                        W(act, "pv_done", g - 2)
                        f(s.pt[b][0][:, 0:n], T[b][:, 0:n], ACT.Copy).then_inc(s_("phi_done"), 1)
                    if s is NB and a == 0 and made(i - 4) and made(i - 3):
                        o = ot_no(s, it, pc, i)
                        act.wait_ge(s_("ot_done"), o + 1)
                        qb = (i // 2 - 2) % 4
                        if qb == 0:
                            W(act, "o_spilled", it * 32 + 16 * pc)
                        f(stage[:, 128 * qb:128 * qb + 128], O[1][:, 256:384], ACT.Copy).then_inc(s_("ot_free"), 1)
                        if qb == 3:
                            pr = pc - 1 if i < 4 else pc
                            act.wait_ge(s_("ot_free"), o + 1)
                            if isinstance(it, int):
                                dst = o_dram[pr // 2, pr % 2]
                            else:
                                dst = o_dram[bass.ds(it, 1), pc - 1].rearrange("a p n -> (a p) n")
                            act.dma_start(dst, stage).then_inc(s_("o_spilled"), 16)
                    if s is FX and a == 0 and made(i - 4) and made(i - 3):
                        o = ot_no(s, it, pc, i)
                        act.wait_ge(s_("ot_done"), o + 1)
                        qb, pr = (i // 2 - 2) % 4, pc - 1 if i < 4 else pc
                        f(ob2[0][:, pr, 128 * qb:128 * qb + 128], O[1][:, 256:384], ACT.Copy).then_inc(s_("ot_hi"), 1)
                    if s is MM and made(i - 3):
                        j = (i - 3) % 4
                        pr = pc - 1 if i < 3 else pc
                        act.wait_ge(s_("ot_done"), s.ot0 + 4 * pc + i - 3 + 1)
                        f(om[0][:, 2 * pr:2 * pr + 2, 128 * j:128 * j + 128],
                          O[b][:, 256:512].rearrange("p (t n) -> p t n", t=2), ACT.Copy).then_inc(s_("ot_hi"), 1)
                    if made(i - 2) and not (s is DF and a == 1):
                        j = (i - 2) % s.n
                        act.wait_ge(s_("pv_done"), g - 1)
                        act.wait_ge(s_("rinv_done"), g - 1)
                        cc = j % 8
                        if s in (NB, FX):
                            W(act, "ot_done", it * 8 + (s.ot0 + 4 * pc + (i - 2) // 2 - 1))
                            dst, w = s.osb[(j // 2) % 2][:, 64 * a:64 * a + 64], 64
                        elif s is DF:
                            W(act, "o_free1", step_half(s, it, pc, i - 5) + 1)
                            dst, w = s.osb[(j // 2) % 2], 128
                        else:
                            W(act, "ot_done", s.ot0 + 4 * pc + i - 3)
                            dst, w = s.osb[a], 256
                        f(dst, O[a][:, 0:w], ACT.Copy, scale=rinv[:, cc:cc + 1]).then_inc(s_(f"o_free{a}"), 1)
                    if extra:
                        extra(it, pc, i)

            def nb_extra(it, pc, i):
                if i == 1:
                    act.wait_ge(s_("acc_ready"), it * 8 + (GB["QK"] + 4 * (pc + 1)))
                    split_hi(act, it, 2, JB["QK"] + pc + 2)
                if i == 3:
                    rope_hi(it, pc + 1, 0)
                if i == 5:
                    rope_hi(it, pc + 1, 1)
                if i == 6:
                    kc_hi(it, pc + 1, 0)
                    kc_hi(it, pc + 1, 1)
                if i == 4 and not (isinstance(it, int) and pc == 0):
                    act.wait_ge(s_("bm_done"), it * 16 + 8 * pc)
                    load_strips(it, pc + 1)

            attend(NB, 0, 0, True, False, nb_extra)
            with act.Fori(0, 3) as it:
                for pc in (1, 2):
                    attend(NB, it, pc, False, False, nb_extra)
            attend(NB, 0, 7, False, True)

            with act.Fori(0, 4) as it:
                for c in range(4):
                    split_hi(act, it, 4, JB["CONV"] + c + 1)
                    for t in range(2):
                        g = GB["CONV"] + 2 * c + t
                        if c == 0:
                            acc_wait_ready(act, it, 8, g)
                            free_acc(f(c_t[:, t], acc[g % 2][:], ACT.Copy), g)
                        if c == 1:
                            wait_evacuated(act, it, 8, g)
                            f(y_t[:, t], u_t[:, t], ACT.Identity, bias=par[:, bass.ds(it * 2 + (P_CB + t), 1)],
                              scale=par[:, bass.ds(it * 2 + (P_CW + 8 + t), 1)]).then_inc(s_("tap_ready"), 1)
                        if c == 3:
                            acc_wait_ready(act, it, 8, g)
                            f(sg_t[:, t], acc[g % 2][:], ACT.Sigmoid).then_inc(s_("zsig_ready"), 1)
                    if c == 2:
                        acc_wait_ready(act, it, 8, GB["CONV"] + 5)
                for t in range(2):
                    act.wait_ge(s_("cinf_ready"), it * 2 + (t + 1))
                    f(cin[0][:, bass.ds(it * 2 + t, 1)].rearrange("p a n -> p (a n)"), y_t[:, t], ACT.Copy).then_inc(s_("cin_hi"), 1)

            def load_o(n):
                act.dma_start(o_in[n % 2], o_dram[n].rearrange("t p n -> p t n")).then_inc(s_(f"o_in{n % 2}"), 16)

            act.wait_ge(s_("o_spilled"), 16 * 8)
            load_o(0)
            load_o(1)
            for c in range(4):
                split_hi(act, 0, 2, JB["ZB"] + c + 1)
                for t in range(2):
                    g = GB["ZB"] + 2 * c + t
                    acc_wait_ready(act, 0, 2, g)
                    W(act, "ogf_ready", 2 * c + t - 1)
                    f(sg_t[:, t], acc[g % 2][:], ACT.Sigmoid).then_inc(s_("bsig_ready"), 1)
                for t in range(2):
                    act.wait_ge(s_("ogf_ready"), 2 * c + t + 1)
                    f(og[0][:, 2 * c + t], y_t[:, t], ACT.Copy).then_inc(s_("og_hi"), 1)
                if c < 2:
                    act.wait_ge(s_("ogf_ready"), 2 * c + 2)
                    load_o(c + 2)

            with act.Fori(0, 4) as it:
                for c in range(4):
                    split_hi(act, it, 4, JB["GO"] + c + 1)
                    for t in range(2):
                        g = GB["GO"] + 2 * c + t
                        if c in (0, 2):
                            acc_wait_ready(act, it, 8, g)
                            free_acc(f((ga_t, gb_t)[c // 2][:, t], acc[g % 2][:], ACT.Sigmoid), g)
                    if c == 1:
                        acc_wait_ready(act, it, 8, GB["GO"] + 3)
                for t in range(2):
                    act.wait_ge(s_("mf_ready"), it * 2 + (t + 1))
                    f(merged[0][:, bass.ds(it * 2 + t, 1)].rearrange("p a n -> p (a n)"), ya_t[:, t], ACT.Copy).then_inc(s_("merged_hi"), 1)

            act.wait_ge(s_("merged_ready"), KT)
            act.dma_start(mem, A["mem"]).then_inc(s_("mem_in"), 16)
            for c in range(4):
                split_hi(act, 0, 2, JB["WO"] + 2 * c + 1)
                if c == 1:
                    act.wait_ge(s_("mem_in"), 16)
                    for k in range(KT):
                        W(act, "accm_done", k)
                        f(sqm, mem[:, k], ACT.Square).then_inc(s_("sqm_ready"), 1)
                if c == 2:
                    act.wait_ge(s_("summ_done"), 1)
                    f(rstd_m, S[1][:, 0:CTX], ACT.Sqrt, scale=1.0 / D, bias=eps).then_inc(s_("rmsm_ready"), 1)
                if c == 3:
                    for k in range(KT):
                        act.wait_ge(s_("hmf_ready"), k + 1)
                        f(hm[0][:, k], mem[:, k], ACT.Copy).then_inc(s_("hm_hi"), 1)
                for t in range(2):
                    m, g = 2 * c + t, GB["WO"] + 4 * c + t
                    acc_wait_ready(act, 0, 2, g)
                    if m == 7:
                        act.wait_ge(s_("accm_done"), KT)
                    f(nat_out(y[:, m]), nat(acc[g % 2][:]), ACT.Copy).then_inc(s_("y_ready"), 1)
                    act.wait_ge(s_("y_ready"), m + 1)
                    W(act, "accy_done", m)
                    free_acc(f(nat_out(sq), nat(acc[g % 2][:]), ACT.Square), g)
                split_hi(act, 0, 2, JB["WO"] + 2 * c + 2)
                acc_wait_ready(act, 0, 2, GB["WO"] + 4 * c + 3)

            for c in range(8):
                split_hi(act, 0, 2, JB["MKV"] + c + 1)
                for t in range(2):
                    g = GB["MKV"] + 2 * c + t
                    dst = mk[0][:, 2 * c + t] if c < 4 else mv[0][:, t, 256 * (c - 4):256 * (c - 4) + 256]
                    hi_of("mkv_hi", 0, 2, g, dst, acc[g % 2][:, 0:256])
                if c == 0:
                    act.wait_ge(s_("sumy_done"), 1)
                    act.wait_ge(s_("hm_ready"), KT)
                    f(rstd, S[0][:], ACT.Sqrt, scale=1.0 / D, bias=eps).then_inc(s_("rms_ready"), 1)
                    for k in range(2):
                        act.dma_start(xin[k], A["x_natural"][:, k]).then_inc(s_(f"xin{k}"), 16)
                if c < 4:
                    for k in (2 * c, 2 * c + 1):
                        act.wait_ge(s_("x1_ready"), k + 1)
                        W(act, "acc1_done", k)
                        f(sq, y[:, k], ACT.Square).then_inc(s_("sq1_ready"), 1)
                        if k < 6:
                            act.dma_start(xin[k % 2], A["x_natural"][:, k + 2]).then_inc(s_(f"xin{k % 2}"), 16)
                if c == 3:
                    act.dma_start(x_dram, y).then_inc(s_("x_spilled"), 16)
                if c == 4:
                    act.wait_ge(s_("sum1_done"), 1)
                    f(rstd, S[0][:], ACT.Sqrt, scale=1.0 / D, bias=eps).then_inc(s_("rms_ready"), 1)
                if c in (5, 6):
                    for k in range(4 * (c - 5), 4 * (c - 5) + 4):
                        act.wait_ge(s_("h2f_ready"), k + 1)
                        f(h2[0][:, k], h2f[k % 2], ACT.Copy).then_inc(s_("h2_hi"), 1)
            for t in range(2):
                wait_evacuated(act, 0, 2, GB["MKV"] + 14 + t)
            act.dma_start(mkv_dram, mkv_all).then_inc(s_("mkv_spilled"), 16)

            split_hi(act, 0, 2, JB["FL"] + 1)
            act.wait_ge(s_("fl_ready"), 1)
            z, az, lf = fl_t[0][0:8], fl_t[1][0:8], fl_t[3][0:8]
            ex.link(f(az, z, ACT.Abs))
            ex.link(f(az, az, ACT.Exp, scale=-1.0))
            f(az, az, ACT.Ln, bias=one1[0:8]).then_inc(s_("lnf_ready"), 1)
            act.wait_ge(s_("mkv_spilled"), 16)
            act.wait_ge(s_("cum_ready"), 1)
            f(cumst[0][0:8], lf, ACT.Copy).then_inc(s_("cum_hi"), 1)
            f(cumst[2][0:8], lf, ACT.Copy, scale=-1.0).then_inc(s_("cum_hi"), 1)
            act.dma_start(fl_sel[0:16], A["sel"]).then_inc(s_("sel_in"), 16)
            act.wait_ge(s_("sel_in"), 16)
            f(sel16[0:16], fl_sel[0:16], ACT.Copy).then_inc(s_("sel_ready"), 1)
            act.wait_ge(s_("cum_lo"), 2)
            for n, dst in ((0, cum16), (2, ncum16)):
                act.dma_start(dst[0:8].bitcast(f32), cumst[n][0:8].bitcast(f32)).then_inc(s_("cum_in"), 16)
                act.dma_start(dst[8:16].bitcast(f32), cumst[n + 1][0:8].bitcast(f32)).then_inc(s_("cum_in"), 16)

            for c in range(4):
                split_hi(act, 0, 2, JB["V2"] + c + 1)
                for b in range(4):
                    g = GB["V2"] + 4 * c + b
                    hi_of("v2_hi", 0, 2, g, v2[0][:, b, 256 * c:256 * c + 256], acc[g % 2][:, 0:256])

            act.wait_ge(s_("cum_in"), 64)
            act.wait_ge(s_("x_spilled"), 16)

            def load_strip2(n):
                src = bass.AP(t_dram.tensor, n * NDIST, [[1, 128], [1, SEQ]])
                act.dma_start(strip2[n % 2], src).then_inc(s_(f"strip2_in{n % 2}"), 16)

            load_strip2(0)
            load_strip2(1)
            act.dma_start(cmask, A["cmask"]).then_inc(s_("cmask_in"), 16)
            act.dma_start(gsub, A["gsub"]).then_inc(s_("gsub_in"), 16)

            def qk2_hi(n, x):
                g = GB["DQK"] + 2 * n + x
                acc_wait_ready(act, 0, 2, g)
                f((q2, k2)[x][n % 2][0], acc[g % 2][:], ACT.Copy, scale=(0.125, 1.0)[x]).then_inc(s_("qk2_hi"), 1)

            split_hi(act, 0, 2, JB["DQK"] + 1)
            qk2_hi(0, 0)
            qk2_hi(0, 1)

            def extra2(fox):
                def extra(it, pc, i):
                    n = pc + 4 * fox + 1
                    if i == 1:
                        act.wait_ge(s_("acc_ready"), GB["DQK"] + 2 * n)
                        if n < 8:
                            split_hi(act, 0, 2, JB["DQK"] + n + 1)
                    if i == 3 and n < 8:
                        qk2_hi(n, 0)
                    if i == 6 and n < 8:
                        qk2_hi(n, 1)
                    if not fox and i == 0 and pc in (1, 2):
                        act.wait_ge(s_("bias_done"), DF.g0 + 8 * pc)
                        load_strip2(pc + 1)
                return extra

            for pc in range(4):
                attend(DF, 0, pc, pc == 0, pc == 3, extra2(0))
            for pc in range(4):
                attend(FX, 0, pc, pc == 0, pc == 3, extra2(1))

            act.wait_ge(s_("o_free1"), step_half(DF, 0, 3, 7) + 1)
            for t in range(16):
                f(subsq, odiff[:, t], ACT.Square, accum_out=ssum[:, t:t + 1]).then_inc(s_("subsq_done"), 1)
                act.wait_ge(s_("subsq_done"), t + 1)
            f(srst, ssum, ACT.Sqrt, scale=1.0 / 128, bias=eps).then_inc(s_("srms_ready"), 1)
            for t in range(16):
                act.wait_ge(s_("subt_done"), t + 1)
                f(oa2[0][:, t % 4, 128 * (t // 4):128 * (t // 4) + 128], T[t % 2][:, 0:128], ACT.Copy)\
                    .then_inc(s_("subt_hi"), 1)

            with act.Fori(0, 2) as it:
                for c in range(6):
                    split_hi(act, it, 6, JB["GO2"] + c + 1)
                    mp, g = c // 3, GB["GO2"] + 8 * (c // 3) + 2 * (c % 3)
                    if c % 3 < 2:
                        for t in range(2):
                            acc_wait_ready(act, it, 16, g + t)
                            free_acc(f((ga_t, gb_t)[c % 3][:, t], acc[(g + t) % 2][:], ACT.Sigmoid), g + t)
                    else:
                        for t in range(2):
                            act.wait_ge(s_("mf2_ready"), it * 4 + (2 * mp + t + 1))
                            f(merged[0][:, bass.ds(it * 4 + (2 * mp + t), 1)].rearrange("p a n -> p (a n)"), ya_t[:, t], ACT.Copy)\
                                .then_inc(s_("merged2_hi"), 1)

            def stream(name, job, group, n, gain):
                if n % 2 == 0:
                    split_hi(act, 0, 2, JB[job] + n // 2 + 1)
                wait_evacuated(act, 0, 2, GB[group] + n)
                f(xg[0][:, n], y[:, n], ACT.Copy, scale=par[:, gain + n:gain + n + 1]).then_inc(s_("xg_hi"), 1)
                W(act, name, n)
                f(sq, y[:, n], ACT.Square).then_inc(s_("sqx_ready"), 1)

            act.wait_ge(s_("merged2_ready"), KT)
            act.dma_start(y, x_dram).then_inc(s_("x_back"), 16)
            act.dma_start(mkv_all, mkv_dram).then_inc(s_("mkv_back"), 16)
            for n in range(KT):
                stream("acc2_done", "WO2", "WO2", n, P_MQ)

            split_hi(act, 0, 2, JB["QM"] + 1)
            act.wait_ge(s_("sum2_done"), 1)
            f(rstd, S[0][:], ACT.Sqrt, scale=1.0 / D, bias=eps).then_inc(s_("rms_ready"), 1)

            def qm_hi(n, x):
                wait_evacuated(act, 0, 2, GB["QM"] + 2 * n + x)
                f(qm[n % 2][0][:, x], tmp, ACT.Copy).then_inc(s_("qm_hi"), 1)

            qm_hi(0, 0)
            qm_hi(0, 1)

            def extram(it, pc, i):
                if i == 0 and pc < 3:
                    act.wait_ge(s_("acc_ready"), GB["QM"] + 2 * pc + 2)
                    split_hi(act, 0, 2, JB["QM"] + pc + 2)
                if i == 2 and pc < 3:
                    qm_hi(pc + 1, 0)
                if i == 3 and pc < 3:
                    qm_hi(pc + 1, 1)

            for pc in range(4):
                attend(MM, 0, pc, pc == 0, pc == 3, extram)
            for n in range(KT):
                stream("acc3_done", "OM", "OM", n, P_MLP)

            def up(it, per, gper, c, jb, gb, done0):
                split_hi(act, it, per, jb + c + 1)
                if done0 == 0 and c == 0:
                    act.wait_ge(s_("sum3_done"), 1)
                    f(rstd, S[0][:], ACT.Sqrt, scale=1.0 / D, bias=eps).then_inc(s_("rms_ready"), 1)
                for t in range(2):
                    act.wait_ge(s_("actf_ready"), it * 8 + (done0 + 2 * c + t + 1))
                    f(act2[0][:, 2 * c + t], mt[t], ACT.Copy).then_inc(s_("act_hi"), 1)

            def down(it, per, gper, c, jb, gb):
                split_hi(act, it, per, jb + c + 1)
                for t in range(2):
                    acc_wait_ready(act, it, gper, gb + 2 * c + t)

            for c in range(4):
                up(0, 8, 16, c, JB["MLP"], GB["MLP"], 0)
            for c in range(4, 8):
                down(0, 8, 16, c, JB["MLP"], GB["MLP"])
            with act.Fori(0, 2) as it:
                for c in range(4):
                    up(it, 8, 16, c, JB["MLP"] + 8, GB["MLP"] + 16, 8)
                for c in range(4, 8):
                    down(it, 8, 16, c, JB["MLP"] + 8, GB["MLP"] + 16)
            for c in range(4):
                up(0, 8, 16, c, JB["MLP"] + 24, GB["MLP"] + 48, 24)
            for n in range(KT):
                if n % 2 == 0 and n < 6:
                    split_hi(act, 0, 2, JB["MLP"] + 24 + 4 + n // 2 + 1)
                wait_evacuated(act, 0, 2, GB["MLP"] + 56 + n)
                W(act, "acc4_done", n)
                f(sq, y[:, n], ACT.Square).then_inc(s_("sqx_ready"), 1)
            act.wait_ge(s_("sum4_done"), 1)
            f(rstd, S[0][:], ACT.Sqrt, scale=1.0 / D, bias=eps).then_inc(s_("rms_ready"), 1)

        @block.vector
        def _(v):
            own = Chain(v, s_("dve_own"))
            link = own.link
            tt, stt, ts = nc.vector.tensor_tensor, nc.vector.scalar_tensor_tensor, nc.vector.tensor_scalar
            MUL, ADD, SUB, MAX, MIN = ALU.mult, ALU.add, ALU.subtract, ALU.max, ALU.min

            def lo(dst, src, hi):
                return tt(dst, src, hi.bitcast(f32), SUB)

            def vec(col, n=1):
                return par[:, col:col + n]

            def reciprocal_of(sem_value, t):
                v.wait_ge(s_("rms_ready"), sem_value)
                link(nc.vector.reciprocal(t, t))

            v.sem_inc(s_("acc_free0"), 1)
            v.sem_inc(s_("acc_free1"), 1)
            v.wait_ge(s_("par_in"), 16)
            v.wait_ge(s_("sigc_ready"), 1)
            tt(silc, silc, par[:, P_C:P_C + 16], MUL).then_inc(s_("silc_ready"), 1)
            v.wait_ge(s_("silr_hi"), 1)
            lo(silr[:, 1], silc, silr[:, 0]).then_inc(s_("silr_ready"), 1)
            v.wait_ge(s_("rms0_ready"), 1)
            link(nc.vector.reciprocal(rstd_c, rstd_c))
            for k in range(KT):
                last = tt(ctx0[:, k], ctx0[:, k], rstd_c, MUL)
            link(last)
            v.wait_ge(s_("rms0_ready"), 2)
            link(nc.vector.reciprocal(rstd_x, rstd_x))
            for k in range(KT):
                last = tt(x0[:, k], x0[:, k], rstd_x, MUL)
            link(last)
            v.wait_ge(s_("mod_done"), 1)
            modp = T[0][:, 0:48].rearrange("p (m s) -> p m s", s=2)
            for s in range(2):
                last = tt(mods[:, 0:16, s], modp[:, 0:16, s], vec(P_BMOD, 16), ADD)
            link(last)
            for s, ax in ((1, mod_ac), (0, mod_ax)):
                last = stt(ax, mods[:, 8:16, s], 1.0, vec(P_PRE, 8), ADD, MUL)
            link(last)
            for k in range(KT):
                ts(ctx0[:, k], ctx0[:, k], mod_ac[:, k:k + 1], mods[:, k, 1:2], MUL, ADD).then_inc(s_("hcf_ready"), 1)
            for k in range(KT):
                v.wait_ge(s_("hc_hi"), k + 1)
                lo(hc[1][:, k], ctx0[:, k], hc[0][:, k]).then_inc(s_("hc_ready"), 1)
            split_job(v, 0, 2, 0)
            ts(x0[:, 0], x0[:, 0], mod_ax[:, 0:1], mods[:, 0, 0:1], MUL, ADD).then_inc(s_("hf_ready"), 1)
            for k in range(KT):
                if k + 1 < KT:
                    ts(x0[:, k + 1], x0[:, k + 1], mod_ax[:, k + 1:k + 2], mods[:, k + 1, 0:1], MUL, ADD)\
                        .then_inc(s_("hf_ready"), 1)
                v.wait_ge(s_("h_hi"), k + 1)
                lo(h[1][:, k], x0[:, k], h[0][:, k]).then_inc(s_("h_ready"), 1)

            with v.Fori(0, 2) as it:
                for c in range(2):
                    split_job(v, it, 2, JB["V"] + c + 1)
                    for gi in range(6):
                        g = GB["V"] + 6 * c + gi
                        t = Vc if gi < 2 else V
                        b = gi if gi < 2 else gi - 2
                        cols = bass.ds(it * 512 + 256 * c, 256)
                        v.wait_ge(s_("v_hi"), it * 12 + (6 * c + gi + 1))
                        free_acc(lo(t[1][:, b][:, cols], acc[g % 2][:, 0:256], t[0][:, b][:, cols]), g)

            v.wait_ge(s_("lam_in"), 16)
            link(tt(lamv[:, 0:2], lamv[:, 0:2], lamv[:, 2:4], MUL))
            nc.vector.tensor_reduce(lamt[:, 0:2], lamv[:, 0:2], axis=AX.X, op=ADD).then_inc(s_("lam_sum"), 1)
            v.wait_ge(s_("lam_exp"), 1)
            link(stt(nlam, lamt[:, 3:4], LAMBDA_INIT, lamt[:, 2:3], SUB, SUB))
            v.wait_ge(s_("relt_done"), 1)
            v.wait_ge(s_("relt_in"), 16)
            tt(relt[0:4, 0:SEQ], S[0][0:4, :], relt[0:4, 0:SEQ], ADD)
            tt(relt[0:4, SEQ:NDIST], S[1][0:4, 0:128], relt[0:4, SEQ:NDIST], ADD).then_inc(s_("relt_sum"), 1)

            split_job(v, 0, 2, JB["QK"] + 1)
            v.wait_ge(s_("relt_out"), 16)
            v.wait_ge(s_("rope_in"), 48)
            swap = [(n + 16) % 32 for n in range(32)]

            def rope(it, pc, x):
                g = GB["QK"] + 4 * pc + x
                W(v, "rope_lo", it * 4 + (2 * pc + x))
                acc_wait_ready(v, it, 8, g)
                stt(rope_a, acc[g % 2][:], (0.125, 1.0)[x], cos_t, MUL, MUL).then_inc(s_("rope_cos"), 1)
                free_acc(nc.vector.stream_shuffle(rope_b, acc[g % 2][:], swap), g)

            def kc_lo(it, pc, x):
                g = GB["QK"] + 4 * pc + 2 + x
                v.wait_ge(s_("kc_hi"), it * 4 + (2 * pc + x) + 1)
                cols = slice(128 * x, 128 * x + 128)
                free_acc(lo(kcs[pc % 2][1][:, cols], acc[g % 2][:, 0:128], kcs[pc % 2][0][:, cols]), g)

            rope(0, 0, 0)
            rope(0, 0, 1)
            kc_lo(0, 0, 0)
            kc_lo(0, 0, 1)

            def attend(s, it, pc, first, last_pair, extra=None):
                def made(j):
                    return (j >= 0 or not first) and j < s.n
                for i in range(s.n + (4 if last_pair else 0)):
                    g = step_no(s, it, pc, i)
                    a, b = i % 2, 1 - i % 2
                    if i < s.n:
                        n, cc = s.cols(i), i % 8
                        v.wait_ge(s_("qk_done"), g + 1)
                        if s is NB:
                            v.wait_ge(s_("bm_done"), g + 1)
                            tt(S[a][:, 0:256], S[a][:, 0:256], bm[a], ADD).then_inc(s_("bias_done"), 1)
                        if s is DF:
                            v.wait_ge(s_(f"strip2_in{pc % 2}"), 16 * (pc // 2 + 1))
                            rev = strip2[pc % 2][:, n - 1::-1] if n == SEQ else strip2[pc % 2][:, 0:n][:, ::-1]
                            tt(S[a][:, 0:n], S[a][:, 0:n], rev, ADD).then_inc(s_("bias_done"), 1)
                        if s is FX:
                            v.wait_ge(s_("cmask_in"), 16)
                            tt(S[a][:, n - 128:n], S[a][:, n - 128:n], cmask, ADD).then_inc(s_("bias_done"), 1)
                        if s is not MM:
                            v.wait_ge(s_("bias_done"), g + 1)
                        nc.vector.tensor_reduce(negmax[:, cc:cc + 1], S[a][:, 0:n], axis=AX.X, op=MAX, negate=True)\
                            .then_inc(s_("max_done"), 1)
                    if made(i - 1):
                        n, cc = s.cols((i - 1) % s.n), (i - 1) % s.n % 8
                        v.wait_ge(s_("exp_done"), g)
                        if s is DF and b == 1:
                            link(nc.vector.reciprocal(rinv[:, cc:cc + 1], rowsum[:, cc:cc + 1]))
                            tt(rinv[:, cc:cc + 1], rinv[:, cc:cc + 1], nlam, MUL).then_inc(s_("rinv_done"), 1)
                        else:
                            nc.vector.reciprocal(rinv[:, cc:cc + 1], rowsum[:, cc:cc + 1]).then_inc(s_("rinv_done"), 1)
                        v.wait_ge(s_("phi_done"), g)
                        lo(s.pt[b][1][:, 0:n], T[b][:, 0:n], s.pt[b][0][:, 0:n]).then_inc(s_("plo_done"), 1)
                    if s is FX and a == 0 and made(i - 4) and made(i - 3):
                        qb, pr = (i // 2 - 2) % 4, pc - 1 if i < 4 else pc
                        v.wait_ge(s_("ot_hi"), ot_no(s, it, pc, i) - 32 + 1)
                        cols = slice(128 * qb, 128 * qb + 128)
                        lo(ob2[1][:, pr, cols], O[1][:, 256:384], ob2[0][:, pr, cols]).then_inc(s_("ot_free"), 1)
                    if s is MM and made(i - 3):
                        j, pr = (i - 3) % 4, pc - 1 if i < 3 else pc
                        v.wait_ge(s_("ot_hi"), 16 + 4 * pc + i - 3 + 1)
                        cols = slice(128 * j, 128 * j + 128)
                        lo(om[1][:, 2 * pr:2 * pr + 2, cols], O[b][:, 256:512].rearrange("p (t n) -> p t n", t=2),
                           om[0][:, 2 * pr:2 * pr + 2, cols]).then_inc(s_("ot_free"), 1)
                    if s is DF and a == 1 and made(i - 2):
                        j = (i - 2) % 8
                        pr = pc - 1 if i < 2 else pc
                        v.wait_ge(s_("pv_done"), g - 1)
                        v.wait_ge(s_("o_free0"), step_half(s, it, pc, i - 3) + 1)
                        stt(odiff[:, 4 * (j // 2) + pr], O[1][:, 0:128], rinv[:, j:j + 1], osb2[(j // 2) % 2], MUL, ADD)\
                            .then_inc(s_("o_free1"), 1)
                    if extra:
                        extra(it, pc, i)

            def nb_extra(it, pc, i):
                if i == 2:
                    rope(it, pc + 1, 0)
                if i == 4:
                    rope(it, pc + 1, 1)
                if i == 6:
                    kc_lo(it, pc + 1, 0)
                    kc_lo(it, pc + 1, 1)

            attend(NB, 0, 0, True, False, nb_extra)
            with v.Fori(0, 3) as it:
                for pc in (1, 2):
                    attend(NB, it, pc, False, False, nb_extra)
            attend(NB, 0, 7, False, True)

            v.wait_ge(s_("lo_done"), JB["CONV"] + 1)
            with v.Fori(0, 4) as it:
                own.loop(it, 4)
                for c in range(4):
                    split_job(v, it, 4, JB["CONV"] + c + 1)
                    g = GB["CONV"] + 2 * c
                    if c == 0:
                        acc_wait_ready(v, it, 8, g + 1)
                    for t in range(2):
                        if c == 1:
                            wait_evacuated(v, it, 8, g - 2 + t)
                            acc_wait_ready(v, it, 8, g + t)
                            free_acc(tt(u_t[:, t], acc[(g + t) % 2][:], c_t[:, t], MUL), g + t)
                        if c == 2:
                            v.wait_ge(s_("tap_ready"), it * 2 + (t + 1))
                            u, yy = u_t[:, t], y_t[:, t]
                            w0 = par[:, bass.ds(it * 2 + (P_CW + t), 1)]
                            w2 = par[:, bass.ds(it * 2 + (P_CW + 16 + t), 1)]
                            stt(yy[:, GR:], u[:, 0:SEQ - GR], w0, yy[:, GR:], MUL, ADD)
                            link(stt(yy[:, 1:GR], u[:, SEQ - GR:SEQ - 1], w0, yy[:, 1:GR], MUL, ADD))
                            stt(yy[:, 0:SEQ - GR], u[:, GR:], w2, yy[:, 0:SEQ - GR], MUL, ADD)
                            link(stt(yy[:, SEQ - GR:SEQ - 1], u[:, 1:GR], w2, yy[:, SEQ - GR:SEQ - 1], MUL, ADD))
                            acc_wait_ready(v, it, 8, g + t)
                            free_acc(tt(yy, acc[(g + t) % 2][:], yy, MUL), g + t)
                        if c == 3:
                            v.wait_ge(s_("zsig_ready"), it * 2 + (t + 1))
                            free_acc(tt(sg_t[:, t], acc[(g + t) % 2][:], sg_t[:, t], MUL), g + t)
                            wait_evacuated(v, it, 8, g + t)
                            tt(y_t[:, t], y_t[:, t], sg_t[:, t], MUL).then_inc(s_("cinf_ready"), 1)
                for t in range(2):
                    v.wait_ge(s_("cin_hi"), it * 2 + (t + 1))
                    m = bass.ds(it * 2 + t, 1)
                    lo(cin[1][:, m].rearrange("p a n -> p (a n)"), y_t[:, t], cin[0][:, m].rearrange("p a n -> p (a n)"))\
                        .then_inc(s_("cin_ready"), 1)
            own.done(4)

            for c in range(4):
                split_job(v, 0, 2, JB["ZB"] + c + 1)
                for t in range(2):
                    g = GB["ZB"] + 2 * c + t
                    v.wait_ge(s_("bsig_ready"), 2 * c + t + 1)
                    free_acc(tt(sg_t[:, t], acc[g % 2][:], sg_t[:, t], MUL), g)
                    v.wait_ge(s_(f"o_in{c % 2}"), 16 * (c // 2 + 1))
                    wait_evacuated(v, 0, 2, g)
                    tt(y_t[:, t], sg_t[:, t], o_in[c % 2][:, t], MUL).then_inc(s_("ogf_ready"), 1)
                for t in range(2):
                    m = 2 * c + t
                    v.wait_ge(s_("og_hi"), m + 1)
                    lo(og[1][:, m], y_t[:, t], og[0][:, m]).then_inc(s_("og_ready"), 1)

            with v.Fori(0, 4) as it:
                for c in range(4):
                    split_job(v, it, 4, JB["GO"] + c + 1)
                    g = GB["GO"] + 2 * c
                    if c % 2 == 0:
                        acc_wait_ready(v, it, 8, g + 1)
                        continue
                    for t in range(2):
                        wait_evacuated(v, it, 8, g - 2 + t)
                        acc_wait_ready(v, it, 8, g + t)
                        free_acc(tt((ya_t, yb_t)[c // 2][:, t], acc[(g + t) % 2][:], (ga_t, gb_t)[c // 2][:, t], MUL), g + t)
                for t in range(2):
                    wait_evacuated(v, it, 8, GB["GO"] + 6 + t)
                    tt(ya_t[:, t], ya_t[:, t], yb_t[:, t], ADD).then_inc(s_("mf_ready"), 1)
                for t in range(2):
                    v.wait_ge(s_("merged_hi"), it * 2 + (t + 1))
                    m = bass.ds(it * 2 + t, 1)
                    lo(merged[1][:, m].rearrange("p a n -> p (a n)"), ya_t[:, t],
                       merged[0][:, m].rearrange("p a n -> p (a n)")).then_inc(s_("merged_ready"), 1)

            for c in range(4):
                split_job(v, 0, 2, JB["WO"] + 2 * c + 1)
                if c == 2:
                    v.wait_ge(s_("rmsm_ready"), 1)
                    link(nc.vector.reciprocal(rstd_m, rstd_m))
                    for k in range(KT):
                        stt(mem[:, k], mem[:, k], vec(P_MKV + k), rstd_m, MUL, MUL).then_inc(s_("hmf_ready"), 1)
                if c == 3:
                    for k in range(KT):
                        v.wait_ge(s_("hm_hi"), k + 1)
                        lo(hm[1][:, k], mem[:, k], hm[0][:, k]).then_inc(s_("hm_ready"), 1)
                acc_wait_ready(v, 0, 2, GB["WO"] + 4 * c + 1)
                split_job(v, 0, 2, JB["WO"] + 2 * c + 2)
                for t in range(2):
                    m, g = 2 * c + t, GB["WO"] + 4 * c + 2 + t
                    acc_wait_ready(v, 0, 2, g)
                    free_acc(stt(gtp[:, m:m + 1], acc[g % 2][:, 0:1], vec(P_BMOD + 16 + m), vec(P_POST + m), ADD, MUL), g)
                    wait_evacuated(v, 0, 2, g)

            for c in range(8):
                split_job(v, 0, 2, JB["MKV"] + c + 1)
                for t in range(2):
                    g = GB["MKV"] + 2 * c + t
                    v.wait_ge(s_("mkv_hi"), 2 * c + t + 1)
                    d = (mk[0][:, 2 * c + t], mk[1][:, 2 * c + t]) if c < 4 else \
                        tuple(p[:, t, 256 * (c - 4):256 * (c - 4) + 256] for p in mv)
                    free_acc(lo(d[1], acc[g % 2][:, 0:256], d[0]), g)
                if c == 0:
                    reciprocal_of(1, rstd)
                if c < 4:
                    for k in (2 * c, 2 * c + 1):
                        link(tt(y[:, k], y[:, k], rstd, MUL))
                        v.wait_ge(s_(f"xin{k % 2}"), 16 * (k // 2 + 1))
                        stt(y[:, k], y[:, k], gtp[:, k:k + 1], xin[k % 2], MUL, ADD).then_inc(s_("x1_ready"), 1)
                if c == 4:
                    reciprocal_of(2, rstd)
                if c in (5, 6):
                    for k in range(4 * (c - 5), 4 * (c - 5) + 4):
                        stt(h2f[k % 2], y[:, k], vec(P_MIX + k), rstd, MUL, MUL).then_inc(s_("h2f_ready"), 1)
                        v.wait_ge(s_("h2_hi"), k + 1)
                        lo(h2[1][:, k], h2f[k % 2], h2[0][:, k]).then_inc(s_("h2_ready"), 1)

            split_job(v, 0, 2, JB["FL"] + 1)
            z, m0, cum = fl_t[0][0:8], fl_t[2][0:8], fl_t[3][0:8]
            for x in range(2):
                g = GB["FL"] + x
                acc_wait_ready(v, 0, 2, g)
                free_acc(ts(z[:, 256 * x:256 * x + 256], acc[g % 2][0:8, 0:256], par[0:8, P_BF:P_BF + 1], None, ADD), g)
                wait_evacuated(v, 0, 2, g)
            ts(m0, z, 0.0, None, MIN).then_inc(s_("fl_ready"), 1)
            v.wait_ge(s_("lnf_ready"), 1)
            v.wait_ge(s_("fl_ready"), 1)
            tt(m0, m0, fl_t[1][0:8], SUB)
            link(nc.vector.memset(z, 1.0))
            nc.vector.tensor_tensor_scan(cum, z, m0, 0.0, MUL, ADD).then_inc(s_("cum_ready"), 1)
            v.wait_ge(s_("cum_hi"), 2)
            lo(cumst[1][0:8], cum, cumst[0][0:8]).then_inc(s_("cum_lo"), 1)
            stt(cumst[3][0:8], cum, -1.0, cumst[2][0:8].bitcast(f32), MUL, SUB).then_inc(s_("cum_lo"), 1)

            for c in range(4):
                split_job(v, 0, 2, JB["V2"] + c + 1)
                for b in range(4):
                    g = GB["V2"] + 4 * c + b
                    v.wait_ge(s_("v2_hi"), 4 * c + b + 1)
                    cols = slice(256 * c, 256 * c + 256)
                    free_acc(lo(v2[1][:, b, cols], acc[g % 2][:, 0:256], v2[0][:, b, cols]), g)

            def qk2_lo(n, x):
                g = GB["DQK"] + 2 * n + x
                v.wait_ge(s_("qk2_hi"), 2 * n + x + 1)
                p = (q2, k2)[x][n % 2]
                free_acc(stt(p[1], acc[g % 2][:], (0.125, 1.0)[x], p[0].bitcast(f32), MUL, SUB), g)

            split_job(v, 0, 2, JB["DQK"] + 1)
            qk2_lo(0, 0)
            qk2_lo(0, 1)

            def extra2(fox):
                def extra(it, pc, i):
                    n = pc + 4 * fox + 1
                    if i == 3 and n < 8:
                        qk2_lo(n, 0)
                    if i == 6 and n < 8:
                        qk2_lo(n, 1)
                return extra

            for pc in range(4):
                attend(DF, 0, pc, pc == 0, pc == 3, extra2(0))
            for pc in range(4):
                attend(FX, 0, pc, pc == 0, pc == 3, extra2(1))

            v.wait_ge(s_("srms_ready"), 1)
            v.wait_ge(s_("gsub_in"), 16)
            link(nc.vector.reciprocal(srst, srst))
            link(ts(srst, srst, 1.0 - LAMBDA_INIT, None, MUL))
            for t in range(16):
                stt(odiff[:, t], odiff[:, t], srst[:, t:t + 1], gsub, MUL, MUL).then_inc(s_("sub_ready"), 1)
            for t in range(16):
                v.wait_ge(s_("subt_hi"), t + 1)
                cols = slice(128 * (t // 4), 128 * (t // 4) + 128)
                lo(oa2[1][:, t % 4, cols], T[t % 2][:, 0:128], oa2[0][:, t % 4, cols]).then_inc(s_("subt_lo"), 1)

            v.wait_ge(s_("lo_done"), JB["GO2"] + 1)
            with v.Fori(0, 2) as it:
                for c in range(6):
                    split_job(v, it, 6, JB["GO2"] + c + 1)
                    mp, g = c // 3, GB["GO2"] + 8 * (c // 3) + 2 * (c % 3)
                    if c % 3 < 2:
                        acc_wait_ready(v, it, 16, g + 1)
                        continue
                    for u in range(4):
                        e, t = u % 2, u // 2
                        wait_evacuated(v, it, 16, GB["GO2"] + 8 * mp + 2 * e + t)
                        acc_wait_ready(v, it, 16, g + u)
                        free_acc(tt((ya_t, yb_t)[e][:, t], acc[(g + u) % 2][:], (ga_t, gb_t)[e][:, t], MUL), g + u)
                    for t in range(2):
                        wait_evacuated(v, it, 16, g + 2 + t)
                        tt(ya_t[:, t], ya_t[:, t], yb_t[:, t], ADD).then_inc(s_("mf2_ready"), 1)
                    for t in range(2):
                        v.wait_ge(s_("merged2_hi"), it * 4 + (2 * mp + t + 1))
                        m = bass.ds(it * 4 + (2 * mp + t), 1)
                        lo(merged[1][:, m].rearrange("p a n -> p (a n)"), ya_t[:, t],
                           merged[0][:, m].rearrange("p a n -> p (a n)")).then_inc(s_("merged2_ready"), 1)

            def add_stream(it, gper, g, n):
                acc_wait_ready(v, it, gper, g)
                free_acc(tt(y[:, n], acc[g % 2][:], y[:, n], ADD), g)

            def stream(name, n, gain, made0):
                if n % 2 == 0:
                    split_job(v, 0, 2, JB[name] + n // 2 + 1)
                g = GB[name] + n
                add_stream(0, 2, g, n)
                wait_evacuated(v, 0, 2, g)
                v.wait_ge(s_("xg_hi"), made0 + n + 1)
                stt(xg[1][:, n], y[:, n], vec(gain + n), xg[0][:, n].bitcast(f32), MUL, SUB).then_inc(s_("xg_ready"), 1)

            v.wait_ge(s_("x_back"), 16)
            for n in range(KT):
                stream("WO2", n, P_MQ, 0)

            split_job(v, 0, 2, JB["QM"] + 1)
            reciprocal_of(3, rstd)

            def qm_tile(n, x):
                g = GB["QM"] + 2 * n + x
                acc_wait_ready(v, 0, 2, g)
                W(v, "qm_lo", 2 * n + x)
                free_acc(stt(tmp, acc[g % 2][:], 1.0 / 16, rstd, MUL, MUL), g)
                v.wait_ge(s_("qm_hi"), 2 * n + x + 1)
                lo(qm[n % 2][1][:, x], tmp, qm[n % 2][0][:, x]).then_inc(s_("qm_lo"), 1)

            qm_tile(0, 0)
            qm_tile(0, 1)

            def extram(it, pc, i):
                if i == 0 and pc < 3:
                    v.wait_ge(s_("acc_ready"), GB["QM"] + 2 * pc + 2)
                    split_job(v, 0, 2, JB["QM"] + pc + 2)
                if i in (2, 3) and pc < 3:
                    qm_tile(pc + 1, i - 2)

            for pc in range(4):
                attend(MM, 0, pc, pc == 0, pc == 3, extram)
            for n in range(KT):
                stream("OM", n, P_MLP, KT)

            def up(it, per, gper, c, jb, gb, done0):
                split_job(v, it, per, jb + c + 1)
                if done0 == 0 and c == 0:
                    reciprocal_of(4, rstd)
                for t in range(2):
                    g = gb + 2 * c + t
                    W(v, "act_ready", it * 8 + (done0 + 2 * c + t) - 1)
                    acc_wait_ready(v, it, gper, g)
                    free_acc(tt(mt[t], acc[g % 2][:], rstd, MUL), g)
                    wait_evacuated(v, it, gper, g)
                    stt(mt[t], mt[t], 0.0, mt[t], MAX, MUL).then_inc(s_("actf_ready"), 1)
                for t in range(2):
                    v.wait_ge(s_("act_hi"), it * 8 + (done0 + 2 * c + t + 1))
                    lo(act2[1][:, 2 * c + t], mt[t], act2[0][:, 2 * c + t]).then_inc(s_("act_ready"), 1)

            def down(it, per, gper, c, jb, gb, split=True):
                if split:
                    split_job(v, it, per, jb + c + 1)
                for t in range(2):
                    add_stream(it, gper, gb + 2 * c + t, 2 * (c - 4) + t)

            def quarter(it, jb, gb, done0, final=False):
                for c in range(4):
                    up(it, 8, 16, c, jb, gb, done0)
                for c in range(4, 8):
                    down(it, 8, 16, c, jb, gb, not (final and c == 7))
            quarter(0, JB["MLP"], GB["MLP"], 0)
            with v.Fori(0, 2) as it:
                quarter(it, JB["MLP"] + 8, GB["MLP"] + 16, 8)
            quarter(0, JB["MLP"] + 24, GB["MLP"] + 48, 24, True)

            v.wait_ge(s_("rms_ready"), 5)
            link(nc.vector.reciprocal(rstd, rstd))
            for k in range(KT):
                stt(y[:, k], y[:, k], vec(P_FIN + k), rstd, MUL, MUL).then_inc(s_("final_ready"), 1)

        @block.gpsimd
        def _(gp):
            gt = nc.gpsimd.tensor_tensor
            MUL, ADD, SUB = ALU.mult, ALU.add, ALU.subtract
            nc.gpsimd.memset(ones[:], 1.0).then_inc(s_("consts_ready"), 1)
            nc.gpsimd.memset(eps, EPS).then_inc(s_("consts_ready"), 1)
            gp.wait_ge(s_("consts_ready"), 1)
            gp.wait_ge(s_("consts_ready"), 2)
            nc.gpsimd.affine_select(out=ident[:], in_=ones[:], compare_op=ALU.is_equal, fill=0.0, base=0,
                                    pattern=[[-1, 128]], channel_multiplier=1).then_inc(s_("consts_ready"), 1)
            gp.wait_ge(s_("h_ready"), KT)
            for n in range(2):
                for dst, src in ((slice(0, 64), slice(SEQ - 64, SEQ)), (slice(64, 128), slice(0, 64))):
                    nc.gpsimd.tensor_copy(hseam[n][:, :, dst], h[n][:, :, src]).then_inc(s_("seam_ready"), 1)
            nc.gpsimd.memset(relb[0:32], 0.0).then_inc(s_("relb_ready"), 1)

            def rope_sum(it, pc, x):
                r = it * 4 + (2 * pc + x)
                g = GB["QK"] + 4 * pc + x
                gp.wait_ge(s_("rope_cos"), r + 1)
                wait_evacuated(gp, it, 8, g)
                gt(rope_b, rope_b, sin_q if x == 0 else sin_t, MUL).then_inc(s_("rope_sin"), 1)
                gp.wait_ge(s_("rope_sin"), r + 1)
                gt(rope_a, rope_a, rope_b, ADD).then_inc(s_("rope_sum"), 1)

            def rope_lo(it, pc, x):
                gp.wait_ge(s_("rope_hi"), it * 4 + (2 * pc + x) + 1)
                p = (qs, ks)[x][pc % 2]
                gt(p[1], rope_a, p[0].bitcast(f32), SUB).then_inc(s_("rope_lo"), 1)

            def bias(it, pc, i):
                if i == 8:
                    pc, i = pc + 1, 0
                qb, e, a = i // 2, i % 2, i % 2
                if i == 0:
                    gp.wait_ge(s_(f"strip_in{pc % 2}"), it * 32 + 32 * (pc // 2 + 1))
                W(gp, "bias_done", step_no(NB, it, pc, i) - 1)
                kind = (0, 1, 1, 2)[qb]
                rev = strip[:, 2 * (pc % 2) + e].rearrange("p (u v) -> p u v", v=15)[:, ::-1, 7::-1]
                gt(bm[a].rearrange("p (u v) -> p u v", v=GR), rev, wmask[:, kind].rearrange("p (u v) -> p u v", v=GR), ADD)\
                    .then_inc(s_("bm_done"), 1)

            gp.wait_ge(s_("rope_in"), 48)
            for x in range(2):
                rope_sum(0, 0, x)
                rope_lo(0, 0, x)
            gp.wait_ge(s_("wmask_in"), 16)
            gp.wait_ge(s_("lam_sum"), 1)
            bias(0, 0, 0)
            gp.wait_ge(s_("lo_done"), JB["QK"] + 2)

            def body(it, pc, last):
                for i in range(8):
                    if not (last and i == 7):
                        bias(it, pc, i + 1)
                    if last:
                        continue
                    if i == 1:
                        gp.wait_ge(s_("acc_ready"), it * 8 + (GB["QK"] + 4 * (pc + 1)))
                        split_job(gp, it, 2, JB["QK"] + pc + 2)
                    if i in (2, 4):
                        rope_sum(it, pc + 1, i // 2 - 1)
                    if i in (3, 5):
                        rope_lo(it, pc + 1, i // 2 - 1)

            body(0, 0, False)
            with gp.Fori(0, 3) as it:
                for pc in (1, 2):
                    body(it, pc, False)
            body(0, 7, True)

            def add_square(name, n, dst, src):
                if n == 0:
                    nc.gpsimd.tensor_copy(dst, src).then_inc(s_(name), 1)
                else:
                    gp.wait_ge(s_(name), n)
                    gt(dst, dst, src, ADD).then_inc(s_(name), 1)

            for n in range(KT):
                if n == 2:
                    for k in range(KT):
                        gp.wait_ge(s_("sqm_ready"), k + 1)
                        add_square("accm_done", k, rstd_m, sqm)
                wait_evacuated(gp, 0, 2, GB["WO"] + 4 * (n // 2) + n % 2)
                add_square("accy_done", n, acc_sq, sq)
            gp.wait_ge(s_("sumy_done"), 1)
            for n in range(KT):
                gp.wait_ge(s_("sq1_ready"), n + 1)
                add_square("acc1_done", n, acc_sq, sq)

            gp.wait_ge(s_("lo_done"), JB["DQK"] + 2)
            for n in range(1, 8):
                gp.wait_ge(s_("acc_ready"), GB["DQK"] + 2 * n)
                split_job(gp, 0, 2, JB["DQK"] + n + 1)

            for i, name in enumerate(("acc2_done", "acc3_done", "acc4_done")):
                gp.wait_ge(s_(f"sum{i + 1}_done"), 1)
                for n in range(KT):
                    gp.wait_ge(s_("sqx_ready"), KT * i + n + 1)
                    add_square(name, n, acc_sq, sq)


def _pair_cols(w, cols):
    w = w.reshape(KT, 128, -1, 128)
    return [np.concatenate([w[:, :, a], w[:, :, b]], axis=-1).transpose(1, 0, 2) for a, b in cols]


def _layout(i):
    win, win2 = np.asarray(i["w_in"][0]), np.asarray(i["w_in_2"][0])

    def seq(first, n):
        return [(first + 2 * j, first + 2 * j + 1) for j in range(n)]

    def square(w, n=4):
        return _pair_cols(np.asarray(w), seq(0, n))

    jobs = []
    jobs += _pair_cols(win, seq(48, 4))
    jobs += _pair_cols(win, [(32 + p, 40 + p) for p in range(8)])
    for p in range(4):
        jobs += _pair_cols(win, [(t + 2 * p, t + 2 * p + 1) for t in (8, 16, 0, 24)])
    jobs += _pair_cols(win, seq(56, 4))
    oc, oa = square(i["w_out_conv"][0]), square(i["w_out_attn"][0])
    ga, gb = _pair_cols(win, seq(64, 4)), _pair_cols(win, seq(72, 4))
    for p in range(4):
        jobs += [ga[p], oc[p], gb[p], oa[p]]
    gate = square(np.asarray(i["w_mod"][0])[:, 2 * D:])
    for p, job in enumerate(square(i["w_o"][0])):
        jobs += [job, gate[p]]
    jobs += square(i["w_kv_mem_2"][0], 8)
    fl = np.zeros((KT, 128, JW), np.float32)
    fl[:, :, 0:8] = win2[:, 3072:3080].reshape(KT, 128, 8)
    jobs += [fl.transpose(1, 0, 2)]
    jobs += _pair_cols(win2[:, :3072], seq(8, 2)) + _pair_cols(win2[:, :3072], seq(20, 2))
    jobs += _pair_cols(win2[:, :3072], [(p, 4 + p) for p in range(4)] + [(12 + p, 16 + p) for p in range(4)])
    gates = np.ascontiguousarray(win2[:, 3080:])
    ga, gb = _pair_cols(gates, seq(0, 4)), _pair_cols(gates, seq(8, 4))
    both = np.concatenate([np.asarray(i["w_diff_out_2"][0]), np.asarray(i["w_fox_out_2"][0])], axis=0)
    both = square(both)
    for p in range(4):
        jobs += [ga[p], gb[p], both[p]]
    jobs += square(i["w_o_2"][0]) + square(i["w_q_mem_2"][0]) + square(i["w_o_mem_2"][0])
    w1, w2 = np.asarray(i["w1_2"][0]), np.asarray(i["w2_2"][0])
    for q in range(4):
        jobs += _pair_cols(w1, seq(8 * q, 4)) + square(w2[1024 * q:1024 * q + 1024])
    assert len(jobs) == NJ, (len(jobs), NJ)

    def feat(t):
        return np.asarray(t).T.reshape(KT, 128, -1).transpose(1, 0, 2)

    def vecs(t):
        return np.asarray(t).reshape(-1, 128).T

    x = np.asarray(i["x"][0])
    grid = x.reshape(GR, GW, D).transpose(1, 0, 2).reshape(SEQ, D)
    par = np.zeros((128, NPAR), np.float32)
    for col, t in ((P_PRE, i["pre_g"]), (P_POST, i["post_g"]), (P_BMOD, i["b_mod"]), (P_CW, i["conv_w"]),
                   (P_CB, i["conv_b"]), (P_MIX, i["g_mix_2"]), (P_MQ, i["g_mem_q_2"]), (P_MKV, i["g_mem_kv_2"]),
                   (P_MLP, i["g_mlp_2"]), (P_FIN, i["g_final_2"])):
        t = vecs(t)
        par[:, col:col + t.shape[1]] = t
    par[:, P_C:P_C + 16:2] = vecs(i["c"])
    par[:, P_C + 1:P_C + 16:2] = vecs(i["c_ctx"])
    par[0:8, P_BF] = np.asarray(i["b_forget_2"][0])

    rpb = np.asarray(i["rpb"][0])
    strips = np.zeros((16, 48, 15), np.float32)
    strips[:, 8:39, :] = rpb[:, ::-1, ::-1].transpose(0, 2, 1)
    lam = np.concatenate([np.asarray(i[n][0]) for n in ("lambda_q1_2", "lambda_q2_2", "lambda_k1_2", "lambda_k2_2")])

    f = np.float32
    inv = (f(10000.0) ** (-np.arange(0, 32, 2, dtype=f) / f(32))).astype(f)
    col, row = np.repeat(np.arange(GW), GR).astype(f), np.tile(np.arange(GR), GW).astype(f)
    ang = np.concatenate([row[:, None] * inv] * 2 + [col[:, None] * inv] * 2, axis=1).astype(f)
    sign = np.tile(np.repeat(np.array([-1.0, 1.0], f), 16), 2)
    cos, sin = np.cos(ang).astype(f), (np.sin(ang) * sign).astype(f)
    cos, sin = (np.tile(t.T, (2, 1)) for t in (cos, sin))
    wmask = np.zeros((128, 3, 256), f)
    for n, qb in enumerate((0, 1, 3)):
        qc = 16 * qb + np.arange(128) // GR
        kc = 16 * qb - 8 + np.arange(256) // GR
        start = np.clip(qc - WIN // 2, 0, GW - WIN)
        ok = (kc >= 0) & (kc < GW) & (kc >= start[:, None]) & (kc < start[:, None] + WIN)
        wmask[:, n] = np.where(ok, 0.0, MASKED)
    dist = np.arange(NDIST) - 127
    d = np.maximum(dist, 1).astype(f)
    large = 16 + (np.log(d / f(16)) / f(math.log(128 / 16)) * f(16)).astype(np.int32)
    bucket = np.where(dist < 16, np.maximum(dist, 0), np.minimum(large, 31))
    onehot = ((bucket == np.arange(32)[:, None]) & (dist >= 0)).astype(f)
    masked_rows = np.tile(np.where(dist < 0, MASKED, 0.0).astype(f), (4, 1))
    cmask = np.where(np.arange(128) <= np.arange(128)[:, None], 0.0, MASKED).astype(f)
    sel = np.zeros((16, 8, 128), f)
    sel[np.arange(16), np.arange(16) % 8] = 1.0

    arrays = {
        "w": np.stack(jobs), "par": par, "ctx": feat(i["ctx"][0]), "x_grid": feat(grid), "x_natural": feat(x),
        "mem": feat(i["mem_2"][0]), "wmod": np.asarray(i["w_mod"][0])[:, :2 * D].reshape(KT, 128, -1).transpose(1, 0, 2),
        "rpb": strips.reshape(16, 720), "lam": np.broadcast_to(lam, (128, 256)), "rel_bias": np.asarray(i["rel_bias_2"]),
        "gsub": np.broadcast_to(np.asarray(i["g_subln_2"][0]), (128, 128)),
        "onehot": onehot, "masked_rows": masked_rows, "cos": cos, "sin": sin, "sin_eighth": sin / 8, "wmask": wmask, "cmask": cmask, "sel": sel,
    }
    return {"in_" + k: np.ascontiguousarray(t) for k, t in arrays.items()}


def kernel(**inputs):
    import concourse.bacc as bacc
    from concourse.bass_utils import run_bass_kernel_spmd

    nc = bacc.Bacc("TRN2", target_bir_lowering=False, num_devices=1)
    arrays = _layout(inputs)
    A = {k[3:]: nc.dram_tensor(k, t.shape, mybir.dt.from_np(t.dtype), kind="ExternalInput").ap()
         for k, t in arrays.items()}
    out = nc.dram_tensor("out", (128, KT, SEQ), mybir.dt.float32, kind="ExternalOutput").ap()
    build(nc, A, out)
    got = run_bass_kernel_spmd(nc, [arrays], core_ids=[0]).results[0]["out"]
    return np.ascontiguousarray(got.transpose(2, 1, 0).reshape(1, SEQ, D))
```

```python
import concourse.bass as bass
from concourse import mybir
from contextlib import ExitStack
import math
import numpy as np

D = 1024
SEQ = 512
KT = D // 128
GW, GR = 64, 8
CTX = 256
WIN = 16
JW = 256
MASKED = -1e30
EPS = 1e-6
LAMBDA_INIT = 0.8 - 0.6 * float(np.exp(-0.3 * 0))
DVE_LAST = 5
STRIP = 32 * 15
NDIST = 640

PHASES = [("V", 4, 24), ("QK", 8, 24), ("CONV", 16, 32), ("ZB", 8, 12), ("GO", 16, 32),
          ("WO", 4, 8), ("MKV", 8, 16), ("FL", 1, 1), ("V2", 4, 16), ("DQK", 4, 8), ("FQK", 4, 8),
          ("GO2", 12, 32), ("WO2", 4, 8), ("QM", 4, 8), ("OM", 4, 8), ("MLP", 32, 64)]
JB, GB = {}, {}
_j = _g = 0
for _name, _n, _groups in PHASES:
    JB[_name], GB[_name] = _j, _g
    _j, _g = _j + _n, _g + _groups
NJ, NG = _j, _g

P_PRE, P_POST, P_BMOD, P_CW, P_CB = 0, 8, 16, 40, 64
P_MIX, P_MQ, P_MKV, P_MLP, P_FIN, P_C = 72, 80, 88, 96, 104, 112
P_BF = 128
NPAR = 129


class Chain:

    def __init__(self, eng, sem):
        self.eng, self.sem, self.n, self.off = eng, sem, 0, 0

    def link(self, ins):
        self.n += 1
        ins.then_inc(self.sem, 1)
        self.eng.wait_ge(self.sem, self.off + self.n)

    def loop(self, it, per):
        self.off, self.start, self.per = it * per, self.n, per

    def done(self, iterations):
        assert self.n - self.start == self.per, (self.n - self.start, self.per)
        self.n, self.off = self.start + self.per * iterations, 0


class Stage:

    def __init__(self, n, g0, ot0, cols, P, osb, pt):
        self.n, self.g0, self.ot0, self.cols, self.P, self.osb, self.pt = n, g0, ot0, cols, P, osb, pt


def build(nc, A, out):
    f32, f32r = mybir.dt.float32, mybir.dt.float32r
    ALU, ACT, AX = mybir.AluOpType, mybir.ActivationFunctionType, mybir.AxisListType
    ctx = ExitStack()
    with ctx:
        def sb(name, shape, dt=f32):
            return ctx.enter_context(nc.sbuf_tensor(name, shape, dt))

        def sem(name):
            return ctx.enter_context(nc.semaphore(name))

        raw = sb("raw", [128, 2, KT, JW])
        wh = sb("wh", [128, 2, KT, JW], f32r)
        wl = sb("wl", [128, 2, KT, JW], f32r)
        par = sb("par", [128, NPAR])
        ident = sb("ident", [128, 128])
        ones = sb("ones", [128, 128])
        small = sb("small", [128, 168])
        silr = sb("silr", [128, 2, 16], f32r)
        F_KB, R_KB = 29.5, 128
        farena = sb("farena", [128, int(F_KB * 256)])
        with nc.sbuf_tensor("early", [128, 75 * 256], f32) as early:
            pass
        rarena = sb("rarena", [128, R_KB * 256], f32r)

        def view(arena, kb, shape):
            n = int(np.prod(shape))
            ap = arena[:, int(kb * 256):int(kb * 256) + n]
            if len(shape) == 1:
                return ap
            names = "abcd"[:len(shape)]
            return ap.rearrange("p (%s) -> p %s" % (" ".join(names), " ".join(names)),
                                **{c: s for c, s in zip(names, shape)})

        def R(kb, *shape):
            n = int(np.prod(shape)) / 256
            return view(rarena, kb, shape), view(rarena, kb + n, shape)

        def F(kb, *shape):
            return view(farena, kb, shape)

        h = R(0, KT, SEQ)
        V, Vc = view(rarena, 32, (4, 2 * D)), view(rarena, 64, (2, 2 * D))
        hc = R(80, KT, CTX)
        hseam = R(96, KT, 128)
        qs = [R(96, SEQ), R(100, SEQ)]
        ks = [R(104, SEQ), R(108, SEQ)]
        kcs = [R(112, CTX), R(114, CTX)]
        pt = [R(116, SEQ), R(120, SEQ)]
        cin = R(32, KT, SEQ)
        og = R(64, KT, SEQ)
        merged = R(96, KT, SEQ)
        wmod_a = view(early, 0, (KT, 2 * D))
        mrow = view(early, 64, (2 * D,))
        acc_x, acc_c = view(early, 72, (SEQ,)), view(early, 74, (CTX,))
        hm = R(0, KT, CTX)
        mk, mv = R(32, KT, CTX), R(48, 2, D)
        mkv_all = rarena[:, 32 * 256:64 * 256].bitcast(f32)
        h2 = R(64, KT, SEQ)
        v2 = view(rarena, 0, (4, 2 * D))
        cumst = [view(rarena, 48 + 2 * n, (SEQ,)) for n in range(4)]
        cum16, ncum16 = view(rarena, 120, (SEQ,)), view(rarena, 122, (SEQ,))
        sel16 = view(rarena, 124, (8, 128))
        q2, k2, pt2 = qs, ks, [R(112, SEQ), R(116, SEQ)]
        oa2, ob2 = R(32, 4, SEQ), R(48, 4, SEQ)
        oab2 = view(rarena, 32, (2, 2, 4, SEQ))
        xg = R(0, KT, SEQ)
        qm = [R(64, 2, SEQ), R(72, 2, SEQ)]
        ptm = [R(80, CTX), R(82, CTX)]
        om = R(96, KT, SEQ)
        act2 = R(32, KT, SEQ)

        x0, ctx0 = F(0, KT, SEQ), F(16, KT, CTX)
        sq0 = [F(24, SEQ), F(26, SEQ)]
        rstd_x, rstd_c = F(24, SEQ), F(28, CTX)
        cos_t, sin_t, ptile = F(0, SEQ), F(2, SEQ), [F(4, SEQ), F(6, SEQ)]
        rope_a, rope_b = F(8, SEQ), F(10, SEQ)
        strip = F(12, 4, STRIP)
        bm = [F(19.5, 256), F(20.5, 256)]
        wmask = F(21.5, 3, 256)
        osb = [F(24.5, 128), F(25, 128)]
        stage, sin_q = F(25.5, SEQ), F(27.5, SEQ)
        c_t, u_t, y_t, sg_t = F(0, 2, SEQ), F(4, 2, SEQ), F(8, 2, SEQ), F(12, 2, SEQ)
        o_in = [F(16, 2, SEQ), F(20, 2, SEQ)]
        onehot, relb, relt, lamv = F(4, NDIST), F(8, 128), F(9, NDIST), F(19.5, 4, 64)
        fl_sel = view(early, 56, (8, 128))
        grow = F(28.5, JW)
        ga_t, gb_t, ya_t, yb_t = F(0, 2, SEQ), F(4, 2, SEQ), F(8, 2, SEQ), F(12, 2, SEQ)
        sqm, mem, rstd_m = F(14, CTX), F(20, KT, CTX), F(28, CTX)
        y = F(0, KT, SEQ)
        sq, acc_sq = F(16, SEQ), F(18, SEQ)
        xin, rstd, tmp = [F(20, SEQ), F(22, SEQ)], F(24, SEQ), F(26, SEQ)
        fl_t = [F(16 + 2 * n, SEQ) for n in range(4)]
        ptile2, strip2, odiff = [F(0, SEQ), F(2, SEQ)], [F(4, SEQ), F(6, SEQ)], F(8, 16, 128)
        osb2 = [F(16, 128), F(16.5, 128)]
        cmask, subsq, gsub = F(17, 128), F(17.5, 128), F(18, 128)
        ptilem, osbm = [F(20, CTX), F(21, CTX)], [F(22, 256), F(23, 256)]
        mt = [F(20, SEQ), F(22, SEQ)]

        eps = small[:, 0:1]
        mod_ax, mod_bx, mod_ac, mod_bc = (small[:, 1 + 8 * n:9 + 8 * n] for n in range(4))
        gtp = small[:, 33:41]
        negmax, rowsum, rinv = small[:, 41:49], small[:, 49:57], small[:, 57:65]
        mods = small[:, 65:97].rearrange("p (m s) -> p m s", s=2)
        rcol = small[:, 97:101]
        nlam = small[:, 113:114]
        lamt = small[:, 114:118]
        ssum, srst = small[:, 118:134], small[:, 134:150]
        silc = small[:, 150:166]
        one1 = ones[:, 0:1]

        acc = [ctx.enter_context(nc.psum_tensor(f"acc{n}", [128, SEQ], f32)) for n in range(2)]
        S = [ctx.enter_context(nc.psum_tensor(f"S{n}", [128, SEQ], f32)) for n in range(2)]
        T = [ctx.enter_context(nc.psum_tensor(f"T{n}", [128, SEQ], f32)) for n in range(2)]
        O = [ctx.enter_context(nc.psum_tensor(f"O{n}", [128, SEQ], f32)) for n in range(2)]

        def head_parts(t, n, part):
            return t.rearrange("p (h x n) -> p h x n", x=2, n=n)[:, :, part]

        o_dram = nc.dram_tensor("o_scratch", (KT // 2, 2, 128, SEQ), f32, kind="Internal").ap()
        x_dram = nc.dram_tensor("x_scratch", (128, KT, SEQ), f32, kind="Internal").ap()
        mkv_dram = nc.dram_tensor("mkv_scratch", (128, 32 * 256), f32, kind="Internal").ap()
        t_dram = nc.dram_tensor("t_scratch", (4, NDIST), f32, kind="Internal").ap()

        sems = {}

        def s_(name):
            if name not in sems:
                sems[name] = sem(name)
            return sems[name]

        def W(eng, name, value):
            if not (isinstance(value, int) and value <= 0):
                eng.wait_ge(s_(name), value)

        def job_no(it, per, base):
            return it * per + base

        def half(it, per, base):
            return it * (per // 2) + base // 2

        def split_hi(act, it, per, base):
            s = base % 2
            act.wait_ge(s_(f"raw_loaded{s}"), half(it, per, base) * 16 + 16)
            nc.scalar.activation(wh[:, s], raw[:, s], ACT.Copy).then_inc(s_("hi_done"), 1)

        def split_job(eng, it, per, base):
            s = base % 2
            eng.wait_ge(s_("hi_done"), job_no(it, per, base) + 1)
            eng.tensor_tensor(wl[:, s], raw[:, s], wh[:, s].bitcast(f32), ALU.subtract)\
               .then_inc(s_("lo_done"), 1)

        def acc_wait_free(pe, it, per, base):
            pe.wait_ge(s_(f"acc_free{base % 2}"), half(it, per, base) + 1)

        def acc_wait_ready(eng, it, per, base):
            eng.wait_ge(s_("acc_ready"), job_no(it, per, base) + 1)

        def wait_evacuated(eng, it, per, base):
            eng.wait_ge(s_(f"acc_free{base % 2}"), half(it, per, base) + 2)

        def free_acc(ins, base):
            ins.then_inc(s_(f"acc_free{base % 2}"), 1)

        block = ctx.enter_context(nc.Block())

        NB = Stage(8, 0, 0, lambda i: SEQ, ptile, osb, pt)
        DF = Stage(8, 64, 32, lambda i: 128 * (i // 2 + 1), ptile2, osb2, pt2)
        FX = Stage(8, 96, 32, lambda i: 128 * (i // 2 + 1), ptile2, osb2, pt2)
        MM = Stage(4, 128, 48, lambda i: CTX, ptilem, osbm, ptm)

        def step_no(s, it, pc, i):
            return it * (2 * s.n) + (s.g0 + s.n * pc + i)

        def step_half(s, it, pc, i):
            return it * s.n + (s.g0 + s.n * pc + i) // 2

        def ot_no(s, it, pc, i):
            return it * 8 + (s.ot0 + 4 * pc + i // 2 - 2)

        @block.sync
        def _(sp):
            sp.dma_start(par[:], A["par"]).then_inc(s_("par_in"), 16)

            def load_job(j):
                if j >= 2:
                    sp.wait_ge(s_("hi_done"), j - 1)
                    sp.wait_ge(s_("lo_done"), j - 1)
                sp.dma_start(raw[:, j % 2], A["w"][j]).then_inc(s_(f"raw_loaded{j % 2}"), 16)

            for n in range(2):
                sp.dma_start(ctx0[:, 4 * n:4 * n + 4], A["ctx"][:, 4 * n:4 * n + 4]).then_inc(s_(f"ctx_in{n}"), 16)
            for n in range(4):
                sp.dma_start(x0[:, 2 * n:2 * n + 2], A["x_grid"][:, 2 * n:2 * n + 2]).then_inc(s_(f"x_in{n}"), 16)
            for n in range(8):
                sp.dma_start(wmod_a[:, :, 256 * n:256 * n + 256], A["wmod"][:, :, 256 * n:256 * n + 256])\
                  .then_inc(s_(f"wmod_in{n}"), 16)
            load_job(0)
            load_job(1)
            sp.wait_ge(s_("h_ready"), KT)
            sp.wait_ge(s_("relb_ready"), 1)
            sp.dma_start(relb[0:32, 0:4], A["rel_bias"]).then_inc(s_("relb_in"), 16)
            sp.dma_start(onehot[0:32], A["onehot"]).then_inc(s_("relb_in"), 16)
            sp.dma_start(relt[0:4], A["masked_rows"]).then_inc(s_("relt_in"), 16)
            sp.dma_start(cos_t, A["cos"]).then_inc(s_("rope_in"), 16)
            sp.dma_start(sin_t, A["sin"]).then_inc(s_("rope_in"), 16)
            sp.dma_start(sin_q, A["sin_eighth"]).then_inc(s_("rope_in"), 16)
            sp.dma_start(wmask, A["wmask"]).then_inc(s_("wmask_in"), 16)
            sp.dma_start(lamv, A["lam"]).then_inc(s_("lam_in"), 16)
            with sp.Fori(0, (NJ - 2) // 2) as it:
                for c in range(2):
                    sp.wait_ge(s_("hi_done"), it * 2 + (c + 1))
                    sp.wait_ge(s_("lo_done"), it * 2 + (c + 1))
                    sp.dma_start(raw[:, c], A["w"][bass.ds(it * 2 + (c + 2), 1)].rearrange("a p k n -> (a p) k n"))\
                      .then_inc(s_(f"raw_loaded{c}"), 16)
            for j in range(2 + (NJ - 2) // 2 * 2, NJ):
                load_job(j)
            for k in sorted(range(KT), key=lambda k: (k % DVE_LAST, k)):
                if k < DVE_LAST:
                    sp.wait_ge(s_("final_ready"), k + 1)
                else:
                    sp.wait_ge(s_("final_ready_gp"), k - DVE_LAST + 1)
                sp.dma_start(out[:, k], y[:, k]).then_inc(s_("out_stored"), 16)
            sp.wait_ge(s_("out_stored"), 16 * KT)

        @block.tensor
        def _(pe):
            mm = nc.tensor.matmul

            def mm3(o, w, m, start, stop):
                mm(o, w[0], m[0], start=start, stop=False)
                mm(o, w[0], m[1], start=False, stop=False)
                return mm(o, w[1], m[0], start=False, stop=stop)

            def at(pair, *idx):
                return tuple(t.__getitem__(idx) for t in pair)

            def wt(s, k, t):
                return wh[:, s, k, 128 * t:128 * t + 128], wl[:, s, k, 128 * t:128 * t + 128]

            def tiles_job(it, per, base, gper, gbase, x, n=SEQ, k_ready=None, between=None):
                s = base % 2
                pe.wait_ge(s_("lo_done"), job_no(it, per, base) + 1)
                for t in range(2):
                    acc_wait_free(pe, it, gper, gbase + t)
                    for k in range(KT):
                        if k_ready and t == 0:
                            pe.wait_ge(s_(k_ready[0]), k_ready[1] + k + 1)
                        last = mm3(acc[(gbase + t) % 2][:, 0:n], wt(s, k, t), at(x, slice(None), k),
                                   k == 0, k == KT - 1)
                    last.then_inc(s_("acc_ready"), 1)
                    if between and t == 0:
                        between()

            def token_group(base, gbase, it, gper, stat, ready=None):
                s = base % 2
                acc_wait_free(pe, it, gper, gbase)
                for k in range(KT):
                    if ready:
                        pe.wait_ge(s_(ready), k + 1)
                    st = stat(k)
                    o = acc[gbase % 2][:, 0:JW]
                    mm(o, st[0], wh[:, s, k], start=k == 0, stop=False)
                    mm(o, st[0], wl[:, s, k], start=False, stop=False)
                    last = mm(o, st[1], wh[:, s, k], start=False, stop=k == KT - 1)
                last.then_inc(s_("acc_ready"), 1)

            def norm_sum(bank, src, n=SEQ):
                return mm(bank[:, 0:n], ones[:], src, start=True, stop=True)

            pe.wait_ge(s_("consts_ready"), 3)
            pe.wait_ge(s_("acc0_done"), KT)
            norm_sum(S[1], acc_c, CTX).then_inc(s_("sum0_done"), 1)
            pe.wait_ge(s_("silc_ready"), 1)
            for n in range(9):
                if n < 8:
                    pe.wait_ge(s_(f"wmod_in{n}"), 16)
                    W(pe, "mrow_ready", n - 1)
                    for k in range(KT):
                        last = mm(O[n % 2][0:2, 0:256], silc[:, 2 * k:2 * k + 2], wmod_a[:, k, 256 * n:256 * n + 256],
                                  start=k == 0, stop=k == KT - 1)
                    last.then_inc(s_("mrow_done"), 1)
                if n == 1:
                    pe.wait_ge(s_("acc0_done"), 2 * KT)
                    norm_sum(S[0], acc_x).then_inc(s_("sum0_done"), 1)
                if n > 0:
                    pe.wait_ge(s_("mrow_ready"), n)
                    for m in (2 * n - 2, 2 * n - 1):
                        last = nc.tensor.transpose(T[0][:, 2 * m:2 * m + 2], mrow[0:2, 128 * m:128 * m + 128], ident[0:2, 0:2])
            last.then_inc(s_("mod_done"), 1)

            def h_block(b):
                if b < 3:
                    return lambda k: at(h, slice(None), k, slice(64 + 128 * b, 192 + 128 * b))
                return lambda k: at(hseam, slice(None), k)

            with pe.Fori(0, 2) as it:
                for c in range(2):
                    base, g = JB["V"] + c, GB["V"] + 6 * c
                    pe.wait_ge(s_("lo_done"), it * 2 + (base + 1))
                    for b in range(2):
                        token_group(base, g + b, it, 12,
                                    lambda k, b=b: at(hc, slice(None), k, slice(128 * b, 128 * b + 128)),
                                    ready="hc_ready" if c == b == 0 else None)
                    for b in range(4):
                        if c == 0 and b == 3:
                            pe.wait_ge(s_("seam_ready"), 4)
                        token_group(base, g + 2 + b, it, 12, h_block(b), ready="h_ready" if c == b == 0 else None)
            pe.wait_ge(s_("relb_in"), 32)
            pe.wait_ge(s_("relb_ready"), 1)
            mm(S[0][:], relb[0:32], onehot[0:32, 0:SEQ], start=True, stop=True)
            mm(S[1][:, 0:128], relb[0:32], onehot[0:32, SEQ:NDIST], start=True, stop=True)\
                .then_inc(s_("relt_done"), 1)

            def chunk(it, pc, i):
                n = pc + 2 if i == 7 else pc + 1
                base, g = JB["QK"] + n, GB["QK"] + 3 * n
                gi, k0, k1 = ((0, 3, 6), (0, 6, 8), (1, 0, 3), (1, 3, 6), (1, 6, 8), (2, 0, 4), (2, 4, 8), (0, 0, 3))[i]
                if i == 7:
                    pe.wait_ge(s_("lo_done"), it * 2 + (base + 1))
                if k0 == 0:
                    acc_wait_free(pe, it, 6, g + gi)
                x, w = (h, SEQ) if gi < 2 else (hc, CTX)
                for k in range(k0, k1):
                    last = mm3(acc[(g + gi) % 2][:, 0:w], wt(base % 2, k, min(gi, 1)), at(x, slice(None), k),
                               k == 0, k == KT - 1)
                if k1 == KT:
                    last.then_inc(s_("acc_ready"), 1)

            def scores_nb(it, pc, i, o):
                qb, e, sl = i // 2, i % 2, pc % 2
                if i == 0:
                    pe.wait_ge(s_("rope_lo"), it * 4 + 2 * pc + 2)
                    wait_evacuated(pe, it, 6, GB["QK"] + 3 * pc + 2)
                r = slice(64 * e, 64 * e + 64)
                q = at(qs[sl], r, slice(128 * qb, 128 * qb + 128))
                kk = at(ks[sl], r)
                seam = tuple(t.rearrange("p (c n) -> p c n", n=64)[:, 7::-7, :] for t in kk)
                if qb == 0:
                    sets = [(0, 128, seam), (128, 128, at(kk, slice(None), slice(64, 192)))]
                elif qb == 3:
                    sets = [(0, 128, at(kk, slice(None), slice(320, 448))), (128, 128, seam)]
                else:
                    sets = [(0, 256, at(kk, slice(None), slice(128 * qb - 64, 128 * qb + 192)))]
                for c0, n, m in sets + [(256, 256, at(kcs[sl], r))]:
                    last = mm3(o[:, c0:c0 + n], q, m, True, True)
                return last

            def weighted(o, p, v, w, first, last_block):
                if not first:
                    mm(o[:, 0:w], p[1], v[:, 0:w], start=False, stop=False)
                last = mm(o[:, 0:2 * w], p[0], v, start=first, stop=last_block and not first)
                if first:
                    last = mm(o[:, 0:w], p[1], v[:, 0:w], start=False, stop=last_block)
                return last

            def values_nb(it, pc, i, o, p):
                if i < 0:
                    pc, i = pc - 1, i + 8
                qb, e = i // 2, i % 2
                c0 = it * 512 + (256 * pc + 128 * e)
                for b in range(4):
                    vb = V[:, (qb - 1) % 4 if b == 0 else qb] if b < 2 else Vc[:, b - 2]
                    last = weighted(o, at(p, slice(None), slice(128 * b, 128 * b + 128)),
                                    vb[:, bass.ds(c0, 128)], 64, b == 0, b == 3)
                return last

            def scores_causal(fox):
                def scores(it, pc, i, o):
                    qb, e, sl = i // 2, i % 2, pc % 2
                    n = 128 * (qb + 1)
                    if i == 0:
                        pe.wait_ge(s_("qk2_lo"), 2 * (pc + 4 * fox) + 2)
                    r = slice(64 * e, 64 * e + 64)
                    last = mm3(o[:, 0:n], at(q2[sl], r, slice(128 * qb, n)), at(k2[sl], r, slice(0, n)), True, not fox)
                    if fox:
                        hd = 2 * pc + e
                        mm(o[:, 0:n], sel16[0:16, hd], ncum16[0:16, 0:n], start=False, stop=False)
                        last = mm(o[:, 0:n].rearrange("p (b n) -> p b n", n=128), cum16[0:16, 128 * qb:n],
                                  sel16[0:16, hd:hd + 1].broadcast_to([16, qb + 1, 128]), start=False, stop=True)
                    return last
                return scores

            def values_causal(fox):
                def values(it, pc, i, o, p):
                    if i < 0:
                        pc, i = pc - 1, i + 8
                    qb, e = i // 2, i % 2
                    c0, w = (D + 256 * pc + 128 * e, 64) if fox else (256 * pc, 128)
                    for b in range(qb + 1):
                        last = weighted(o, at(p, slice(None), slice(128 * b, 128 * b + 128)),
                                        v2[:, b, c0:c0 + 2 * w], w, b == 0, b == qb)
                    return last
                return values

            def scores_mm(it, pc, i, o):
                if i == 0:
                    pe.wait_ge(s_("qm_lo"), 2 * pc + 2)
                if i == 0 and pc == 0:
                    pe.wait_ge(s_("mkv_back"), 16)
                for t in range(2):
                    last = mm3(o[:, 0:CTX], at(qm[pc % 2], slice(None), t, slice(128 * i, 128 * i + 128)),
                               at(mk, slice(None), 2 * pc + t), t == 0, t == 1)
                return last

            def values_mm(it, pc, i, o, p):
                if i < 0:
                    pc, i = pc - 1, i + 4
                for b in range(2):
                    last = mm3(o[:, 0:256], at(p, slice(None), slice(128 * b, 128 * b + 128)),
                               at(mv, slice(None), b, slice(256 * pc, 256 * pc + 256)), b == 0, b == 1)
                return last

            def attend(s, it, pc, first, last_pair, scores, values, part=None):
                def made(j):
                    return (j >= 0 or not first) and j < s.n
                for i in range(s.n + (4 if last_pair else 0)):
                    g, gh = step_no(s, it, pc, i), step_half(s, it, pc, i)
                    a = i % 2
                    if i < s.n:
                        W(pe, "exp_done", g - 1)
                        scores(it, pc, i, S[a]).then_inc(s_("qk_done"), 1)
                    if made(i - 1):
                        pe.wait_ge(s_("exp_done"), g)
                        W(pe, "plo_done", g - 2)
                        b = 1 - a
                        for c0 in range(0, s.cols((i - 1) % s.n), 128):
                            tr = nc.tensor.transpose(T[b][:, c0:c0 + 128], s.P[b][:, c0:c0 + 128], ident[:])
                        tr.then_inc(s_("t_done"), 1)
                    if s is MM and made(i - 3):
                        b = 1 - a
                        pe.wait_ge(s_(f"o_free{b}"), step_half(s, it, pc, i - 3) + 1)
                        for c0 in range(0, 256, 128):
                            tr = nc.tensor.transpose(O[b][:, 256 + c0:384 + c0], osbm[b][:, c0:c0 + 128], ident[:])
                        tr.then_inc(s_("ot_done"), 1)
                    if s in (NB, FX) and a == 0 and made(i - 4) and made(i - 3):
                        for b in range(2):
                            pe.wait_ge(s_(f"o_free{b}"), step_half(s, it, pc, i - 4) + 1)
                        W(pe, "ot_free", ot_no(s, it, pc, i))
                        if s is FX:
                            u = ot_no(s, it, pc, i) - s.ot0
                            pe.wait_ge(s_("sub_ready"), u + 1)
                            nc.tensor.transpose(O[1][:, 256:384], odiff[:, 4 * (u % 4) + u // 4], ident[:])
                        c0 = 384 if s is FX else 256
                        nc.tensor.transpose(O[1][:, c0:c0 + 128], s.osb[(i // 2) % 2][:], ident[:])\
                            .then_inc(s_("ot_done"), 1)
                    if part and i < s.n:
                        part(it, pc, i)
                    if made(i - 2):
                        pe.wait_ge(s_("plo_done"), g - 1)
                        W(pe, f"o_free{a}", gh - 1)
                        if s in (NB, FX) and a == 1:
                            W(pe, "ot_free", ot_no(s, it, pc, i - 1) + 1)
                        if s is MM:
                            W(pe, "ot_free", s.ot0 + s.n * pc + i - 3)
                        values(it, pc, i - 2, O[a], s.pt[a]).then_inc(s_("pv_done"), 1)

            base, g = JB["QK"], GB["QK"]
            pe.wait_ge(s_("lo_done"), base + 1)
            for gi in range(3):
                acc_wait_free(pe, 0, 2, g + gi)
                x, n = (h, SEQ) if gi < 2 else (hc, CTX)
                for k in range(KT):
                    last = mm3(acc[(g + gi) % 2][:, 0:n], wt(base % 2, k, min(gi, 1)), at(x, slice(None), k),
                               k == 0, k == KT - 1)
                last.then_inc(s_("acc_ready"), 1)

            def chunk_or_none(it, pc, i):
                if i < 7:
                    chunk(it, pc, i)

            chunk(0, -1, 7)
            attend(NB, 0, 0, True, False, scores_nb, values_nb, chunk)
            with pe.Fori(0, 2) as it:
                for pc in (1, 2):
                    attend(NB, it, pc, False, False, scores_nb, values_nb, chunk)
            attend(NB, 0, 5, False, False, scores_nb, values_nb, chunk)
            attend(NB, 0, 6, False, False, scores_nb, values_nb, chunk_or_none)
            attend(NB, 0, 7, False, True, scores_nb, values_nb)

            with pe.Fori(0, 4) as it:
                for c in range(4):
                    tiles_job(it, 4, JB["CONV"] + c, 8, GB["CONV"] + 2 * c, h)

            def gate_columns(c):
                wait_evacuated(pe, 0, 2, GB["ZB"] + 3 * c + 2)
                for t in range(2):
                    m = 2 * c + t
                    last = nc.tensor.transpose(T[0][:, 2 * m:2 * m + 2], grow[0:2, 128 * t:128 * t + 128], ident[0:2, 0:2])
                last.then_inc(s_("gcol_done"), 1)

            for c in range(4):
                base, g = JB["ZB"] + 2 * c, GB["ZB"] + 3 * c
                tiles_job(0, 2, base, 2, g, h)
                if c:
                    gate_columns(c - 1)
                pe.wait_ge(s_("lo_done"), base + 2)
                acc_wait_free(pe, 0, 2, g + 2)
                for k in range(KT):
                    s, o = (base + 1) % 2, acc[(g + 2) % 2][0:2, 0:JW]
                    mm(o, silr[:, 0, 2 * k:2 * k + 2], wh[:, s, k], start=k == 0, stop=False)
                    mm(o, silr[:, 0, 2 * k:2 * k + 2], wl[:, s, k], start=False, stop=False)
                    last = mm(o, silr[:, 1, 2 * k:2 * k + 2], wh[:, s, k], start=False, stop=k == KT - 1)
                last.then_inc(s_("acc_ready"), 1)

            gate_columns(3)

            with pe.Fori(0, 4) as it:
                for c in range(4):
                    x = (h, cin, h, og)[c]
                    if c == 1:
                        pe.wait_ge(s_("cin_ready"), KT)
                    if c == 3:
                        pe.wait_ge(s_("og_ready"), KT)
                    tiles_job(it, 4, JB["GO"] + c, 8, GB["GO"] + 2 * c, x)

            for c in range(4):
                tiles_job(0, 2, JB["WO"] + c, 2, GB["WO"] + 2 * c, merged, k_ready=("merged_ready", 0) if c == 0 else None)
                if c == 1:
                    pe.wait_ge(s_("accm_done"), KT)
                    norm_sum(S[1], rstd_m[:], CTX).then_inc(s_("summ_done"), 1)

            pe.wait_ge(s_("hm_ready"), KT)
            for c in range(8):
                base, g = JB["MKV"] + c, GB["MKV"] + 2 * c
                if c < 4:
                    tiles_job(0, 2, base, 2, g, hm, CTX)
                else:
                    pe.wait_ge(s_("lo_done"), base + 1)
                    for b in range(2):
                        token_group(base, g + b, 0, 2,
                                    lambda k, b=b: at(hm, slice(None), k, slice(128 * b, 128 * b + 128)))
                if c == 0:
                    pe.wait_ge(s_("accy_done"), KT)
                    norm_sum(S[0], acc_sq[:]).then_inc(s_("sum_done"), 1)
                if c == 6:
                    pe.wait_ge(s_("acc1_done"), KT)
                    norm_sum(S[0], acc_sq[:])
                    for b in range(4):
                        last = mm(S[1][:, b:b + 1], acc_sq[:, 128 * b:128 * b + 128], one1, start=True, stop=True)
                    last.then_inc(s_("sum_done"), 1)

            base, g = JB["FL"], GB["FL"]
            pe.wait_ge(s_("lo_done"), base + 1)
            acc_wait_free(pe, 0, 2, g)
            for k in range(KT):
                pe.wait_ge(s_("h2_ready"), k + 1)
                last = mm3(acc[g % 2][:], wt(base % 2, k, 0), at(h2, slice(None), k), k == 0, k == KT - 1)
            last.then_inc(s_("acc_ready"), 1)

            for c in range(4):
                base, g = JB["V2"] + c, GB["V2"] + 4 * c
                pe.wait_ge(s_("lo_done"), base + 1)
                for b in range(4):
                    token_group(base, g + b, 0, 2,
                                lambda k, b=b: at(h2, slice(None), k, slice(128 * b, 128 * b + 128)))

            def part2(fox):
                def part(it, pc, i):
                    n = pc + 4 * fox + (1 if i < 6 else 2)
                    if n > 7:
                        return
                    base, g = JB["DQK"] + n, GB["DQK"] + 2 * n
                    t, k0 = divmod(2 * i + 4 if i < 6 else 2 * i - 12, KT)
                    if i == 6:
                        pe.wait_ge(s_("lo_done"), base + 1)
                    if k0 == 0:
                        acc_wait_free(pe, 0, 2, g + t)
                    for k in (k0, k0 + 1):
                        last = mm3(acc[(g + t) % 2][:], wt(base % 2, k, t), at(h2, slice(None), k), k == 0, k == KT - 1)
                    if k0 == KT - 2:
                        last.then_inc(s_("acc_ready"), 1)
                return part

            tiles_job(0, 2, JB["DQK"], 2, GB["DQK"], h2)
            for i in (6, 7):
                part2(0)(0, -1, i)
            for pc in range(4):
                attend(DF, 0, pc, pc == 0, pc == 3, scores_causal(0), values_causal(0), part2(0))
            pe.wait_ge(s_("cum_in"), 64)
            pe.wait_ge(s_("sel_ready"), 1)
            for pc in range(4):
                attend(FX, 0, pc, pc == 0, pc == 3, scores_causal(1), values_causal(1), part2(1))

            with pe.Fori(0, 2) as it:
                for c in range(6):
                    base, g = JB["GO2"] + c, GB["GO2"] + 8 * (c // 3) + 2 * (c % 3)
                    if c % 3 < 2:
                        tiles_job(it, 6, base, 16, g, h2)
                        continue
                    pe.wait_ge(s_("lo_done"), it * 6 + (base + 1))
                    pe.wait_ge(s_("ot_free"), 48)
                    for u in range(4):
                        acc_wait_free(pe, it, 16, g + u)
                        src, k0 = (oa2, 0) if u % 2 == 0 else (ob2, 4)
                        for k in range(4):
                            last = mm3(acc[(g + u) % 2][:], wt(base % 2, k0 + k, u // 2), at(src, slice(None), k),
                                       k == 0, k == 3)
                        last.then_inc(s_("acc_ready"), 1)

            for c in range(4):
                tiles_job(0, 2, JB["WO2"] + c, 2, GB["WO2"] + 2 * c, merged, k_ready=("merged2_ready", 0) if c == 0 else None)

            def sum2():
                pe.wait_ge(s_("acc2_done"), KT)
                norm_sum(S[0], acc_sq[:]).then_inc(s_("sum_done"), 1)

            tiles_job(0, 2, JB["QM"], 2, GB["QM"], xg, k_ready=("xg_ready", 0), between=sum2)

            def partm(it, pc, i):
                n = pc + (1 if i < 3 else 2)
                if n > 3:
                    return
                base, g = JB["QM"] + n, GB["QM"] + 2 * n
                t, k0 = ((0, 4), (1, 0), (1, 4), (0, 0))[i]
                if i == 3:
                    pe.wait_ge(s_("lo_done"), base + 1)
                if k0 == 0:
                    acc_wait_free(pe, 0, 2, g + t)
                for k in range(k0, k0 + 4):
                    last = mm3(acc[(g + t) % 2][:], wt(base % 2, k, t), at(xg, slice(None), k), k == 0, k == KT - 1)
                if k0:
                    last.then_inc(s_("acc_ready"), 1)

            partm(0, -1, 3)
            for pc in range(4):
                attend(MM, 0, pc, pc == 0, pc == 3, scores_mm, values_mm, partm)

            pe.wait_ge(s_("ot_free"), 64)
            for c in range(4):
                tiles_job(0, 2, JB["OM"] + c, 2, GB["OM"] + 2 * c, om)

            def sum3():
                pe.wait_ge(s_("acc3_done"), KT)
                norm_sum(S[0], acc_sq[:]).then_inc(s_("sum_done"), 1)

            def quarter(it, per, gper, base, g, q0, made):
                for c in range(8):
                    if c < 4:
                        start = q0 and c == 0
                        tiles_job(it, per, base + c, gper, g + 2 * c, xg,
                                  k_ready=("xg_ready", KT) if start else None, between=sum3 if start else None)
                    else:
                        tiles_job(it, per, base + c, gper, g + 2 * c, act2,
                                  k_ready=("act_ready", made) if c == 4 else None)

            quarter(0, 8, 16, JB["MLP"], GB["MLP"], True, 0)
            with pe.Fori(0, 2) as it:
                quarter(it, 8, 16, JB["MLP"] + 8, GB["MLP"] + 16, False, it * 8 + 8)
            quarter(0, 8, 16, JB["MLP"] + 24, GB["MLP"] + 48, False, 24)

            pe.wait_ge(s_("acc4_done"), KT)
            norm_sum(S[0], acc_sq[:]).then_inc(s_("sum_done"), 1)

        @block.scalar
        def _(act):
            f = nc.scalar.activation
            ex = Chain(act, s_("act_own"))

            def nat(t):
                return t.rearrange("p (c r) -> p c r", r=GR)

            def nat_out(t):
                return t.rearrange("p (r c) -> p c r", c=GW)

            def hi_of(name, it, gper, g, dst, src):
                acc_wait_ready(act, it, gper, g)
                f(dst, src, ACT.Copy).then_inc(s_(name), 1)

            act.wait_ge(s_("par_in"), 16)
            f(silc, par[:, P_C:P_C + 16], ACT.Sigmoid).then_inc(s_("sigc_ready"), 1)
            act.wait_ge(s_("silc_ready"), 1)
            f(silr[:, 0], silc, ACT.Copy).then_inc(s_("silr_hi"), 1)

            def squares(x):
                src, w, name, per = ((ctx0, CTX, "ctx_in", 4), (x0, SEQ, "x_in", 2))[x]
                for k in range(KT):
                    act.wait_ge(s_(f"{name}{k // per}"), 16)
                    W(act, "acc0_done", KT * x + k - 1)
                    f(sq0[k % 2][:, 0:w], src[:, k], ACT.Square).then_inc(s_("sq0_ready"), 1)

            def root(x):
                rms, bank, w = ((rstd_c, S[1], CTX), (rstd_x, S[0], SEQ))[x]
                act.wait_ge(s_("sum0_done"), x + 1)
                f(rms, bank[:, 0:w], ACT.Sqrt, scale=1.0 / D, bias=eps).then_inc(s_("rms0_ready"), 1)

            squares(0)
            squares(1)
            act.wait_ge(s_("consts_ready"), 3)
            root(0)
            for n in range(8):
                act.wait_ge(s_("mrow_done"), n + 1)
                f(mrow[0:2, 256 * n:256 * n + 256], O[n % 2][0:2, 0:256], ACT.Copy).then_inc(s_("mrow_ready"), 1)
                if n == 1:
                    root(1)
                if n == 6:
                    split_hi(act, 0, 2, 0)
            for k in range(KT):
                act.wait_ge(s_("hcf_ready"), k + 1)
                f(hc[0][:, k], ctx0[:, k], ACT.Copy).then_inc(s_("hc_hi"), 1)
            for k in range(KT):
                act.wait_ge(s_("hf_ready"), k + 1)
                f(h[0][:, k], x0[:, k], ACT.Copy).then_inc(s_("h_hi"), 1)

            with act.Fori(0, 2) as it:
                for c in range(2):
                    for gi in range(6):
                        if gi == 2:
                            split_hi(act, it, 2, JB["V"] + c + 1)
                        g = GB["V"] + 6 * c + gi
                        dst = Vc[:, gi] if gi < 2 else V[:, gi - 2]
                        hi_of("v_hi", it, 12, g, head_parts(dst[:, bass.ds(it * 1024 + 512 * c, 512)], 64, 0),
                              acc[g % 2][:, 0:256].rearrange("p (h n) -> p h n", n=64))
            act.wait_ge(s_("lam_sum"), 1)
            f(lamt[:, 2:4], lamt[:, 0:2], ACT.Exp).then_inc(s_("lam_exp"), 1)
            act.wait_ge(s_("relt_sum"), 1)
            act.dma_start(t_dram, relt[0:4]).then_inc(s_("relt_out"), 16)

            def load_strips(it, pc):
                for e in range(2):
                    hd = it * 4 + (2 * pc + e)
                    if isinstance(it, int):
                        src = A["rpb"][hd]
                    else:
                        src = A["rpb"][bass.ds(hd, 1)].rearrange("a n -> (a n)")
                    src = bass.AP(src.tensor, src.offset, [[15, 16], [1, 8], [1, STRIP]])
                    act.dma_start(strip[:, 2 * (pc % 2) + e], src).then_inc(s_(f"strip_in{pc % 2}"), 16)

            load_strips(0, 0)
            load_strips(0, 1)
            split_hi(act, 0, 2, JB["QK"] + 1)

            def rope_hi(it, pc, x):
                act.wait_ge(s_("rope_sum"), it * 4 + (2 * pc + x) + 1)
                f((qs, ks)[x][pc % 2][0], rope_a, ACT.Copy).then_inc(s_("rope_hi"), 1)

            def kc_hi(it, pc):
                g = GB["QK"] + 3 * pc + 2
                acc_wait_ready(act, it, 6, g)
                f(kcs[pc % 2][0], acc[g % 2][:, 0:CTX], ACT.Copy).then_inc(s_("kc_hi"), 1)

            rope_hi(0, 0, 0)
            rope_hi(0, 0, 1)
            kc_hi(0, 0)

            def attend(s, it, pc, first, last_pair, extra=None):
                def made(j):
                    return (j >= 0 or not first) and j < s.n
                for i in range(s.n + (4 if last_pair else 0)):
                    g = step_no(s, it, pc, i)
                    a, b = i % 2, 1 - i % 2
                    if made(i - 1):
                        n = s.cols((i - 1) % s.n)
                        act.wait_ge(s_("t_done"), g)
                        W(act, "pv_done", g - 2)
                        f(s.pt[b][0][:, 0:n], T[b][:, 0:n], ACT.Copy).then_inc(s_("phi_done"), 1)
                    if i < s.n:
                        act.wait_ge(s_("max_done"), g + 1)
                        W(act, "t_done", g - 1)
                        n, cc = s.cols(i), i % 8
                        f(s.P[a][:, 0:n], S[a][:, 0:n], ACT.Exp, bias=negmax[:, cc:cc + 1],
                          accum_out=rowsum[:, cc:cc + 1]).then_inc(s_("exp_done"), 1)
                    if s is NB and a == 0 and made(i - 4) and made(i - 3):
                        o = ot_no(s, it, pc, i)
                        act.wait_ge(s_("ot_done"), o + 1)
                        qb = (i // 2 - 2) % 4
                        if qb == 0:
                            W(act, "o_spilled", it * 32 + 16 * pc)
                        f(stage[:, 128 * qb:128 * qb + 128], O[1][:, 256:384], ACT.Copy).then_inc(s_("ot_free"), 1)
                        if qb == 3:
                            pr = pc - 1 if i < 4 else pc
                            act.wait_ge(s_("ot_free"), o + 1)
                            if isinstance(it, int):
                                dst = o_dram[pr // 2, pr % 2]
                            else:
                                dst = o_dram[bass.ds(it, 1), pc - 1].rearrange("a p n -> (a p) n")
                            act.dma_start(dst, stage).then_inc(s_("o_spilled"), 16)
                    if s is FX and a == 0 and made(i - 4) and made(i - 3):
                        o = ot_no(s, it, pc, i)
                        act.wait_ge(s_("ot_done"), o + 1)
                        qb, pr = (i // 2 - 2) % 4, pc - 1 if i < 4 else pc
                        f(oab2[:, :, 0, pr, 128 * qb:128 * qb + 128], O[1][:, 256:512].rearrange("p (x n) -> p x n", x=2), ACT.Copy)\
                            .then_inc(s_("ot_hi"), 1)
                    if s is MM and made(i - 3):
                        j = (i - 3) % 4
                        pr = pc - 1 if i < 3 else pc
                        act.wait_ge(s_("ot_done"), s.ot0 + 4 * pc + i - 3 + 1)
                        f(om[0][:, 2 * pr:2 * pr + 2, 128 * j:128 * j + 128],
                          O[b][:, 256:512].rearrange("p (t n) -> p t n", t=2), ACT.Copy).then_inc(s_("ot_hi"), 1)
                    if made(i - 2) and not (s is DF and a == 1):
                        j = (i - 2) % s.n
                        act.wait_ge(s_("pv_done"), g - 1)
                        act.wait_ge(s_("rinv_done"), g - 1)
                        cc = j % 8
                        if s in (NB, FX):
                            W(act, "ot_done", it * 8 + (s.ot0 + 4 * pc + (i - 2) // 2 - 1))
                            dst, w = s.osb[(j // 2) % 2][:, 64 * a:64 * a + 64], 64
                        elif s is DF:
                            W(act, "o_free1", step_half(s, it, pc, i - 5) + 1)
                            dst, w = s.osb[(j // 2) % 2], 128
                        else:
                            W(act, "ot_done", s.ot0 + 4 * pc + i - 3)
                            dst, w = s.osb[a], 256
                        f(dst, O[a][:, 0:w], ACT.Copy, scale=rinv[:, cc:cc + 1])\
                            .then_inc(s_(f"o_free{a}" if s is MM else f"o_main{a}"), 1)
                    if extra:
                        extra(it, pc, i)

            def nb_extra(it, pc, i):
                if i == 1:
                    act.wait_ge(s_("acc_ready"), it * 6 + (GB["QK"] + 3 * (pc + 1)))
                    split_hi(act, it, 2, JB["QK"] + pc + 2)
                if i == 3:
                    rope_hi(it, pc + 1, 0)
                if i == 6:
                    rope_hi(it, pc + 1, 1)
                    kc_hi(it, pc + 1)
                if i == 4 and not (isinstance(it, int) and pc == 0):
                    act.wait_ge(s_("bm_done"), it * 16 + 8 * pc)
                    load_strips(it, pc + 1)

            attend(NB, 0, 0, True, False, nb_extra)
            with act.Fori(0, 3) as it:
                for pc in (1, 2):
                    attend(NB, it, pc, False, False, nb_extra)
            attend(NB, 0, 7, False, True)

            with act.Fori(0, 4) as it:
                for c in range(4):
                    split_hi(act, it, 4, JB["CONV"] + c + 1)
                    for t in range(2):
                        g = GB["CONV"] + 2 * c + t
                        if c == 0:
                            acc_wait_ready(act, it, 8, g)
                            free_acc(f(c_t[:, t], acc[g % 2][:], ACT.Copy), g)
                        if c == 1:
                            wait_evacuated(act, it, 8, g)
                            f(y_t[:, t], u_t[:, t], ACT.Identity, bias=par[:, bass.ds(it * 2 + (P_CB + t), 1)],
                              scale=par[:, bass.ds(it * 2 + (P_CW + 8 + t), 1)]).then_inc(s_("tap_ready"), 1)
                        if c == 3:
                            acc_wait_ready(act, it, 8, g)
                            f(sg_t[:, t], acc[g % 2][:], ACT.Sigmoid).then_inc(s_("zsig_ready"), 1)
                    if c == 2:
                        acc_wait_ready(act, it, 8, GB["CONV"] + 5)
                for t in range(2):
                    act.wait_ge(s_("cinf_ready"), it * 2 + (t + 1))
                    f(cin[0][:, bass.ds(it * 2 + t, 1)].rearrange("p a n -> p (a n)"), y_t[:, t], ACT.Copy).then_inc(s_("cin_hi"), 1)

            def load_o(n):
                act.dma_start(o_in[n % 2], o_dram[n].rearrange("t p n -> p t n")).then_inc(s_(f"o_in{n % 2}"), 16)

            act.wait_ge(s_("o_spilled"), 16 * 8)
            load_o(0)
            load_o(1)
            for c in range(4):
                split_hi(act, 0, 2, JB["ZB"] + 2 * c + 1)
                for t in range(2):
                    g = GB["ZB"] + 3 * c + t
                    if t == 1:
                        acc_wait_ready(act, 0, 2, g)
                        split_hi(act, 0, 2, JB["ZB"] + 2 * c + 2)
                    acc_wait_ready(act, 0, 2, g)
                    W(act, "ogf_ready", 2 * c + t - 1)
                    f(sg_t[:, t], acc[g % 2][:], ACT.Sigmoid).then_inc(s_("bsig_ready"), 1)
                for t in range(2):
                    act.wait_ge(s_("ogf_ready"), 2 * c + t + 1)
                    f(og[0][:, 2 * c + t], y_t[:, t], ACT.Copy).then_inc(s_("og_hi"), 1)
                if c < 2:
                    act.wait_ge(s_("ogf_ready"), 2 * c + 2)
                    load_o(c + 2)
                acc_wait_ready(act, 0, 2, GB["ZB"] + 3 * c + 2)
                W(act, "gcol_done", c)
                free_acc(f(grow[0:2], acc[(GB["ZB"] + 3 * c + 2) % 2][0:2, 0:JW], ACT.Copy), GB["ZB"] + 3 * c + 2)

            with act.Fori(0, 4) as it:
                for c in range(4):
                    split_hi(act, it, 4, JB["GO"] + c + 1)
                    for t in range(2):
                        g = GB["GO"] + 2 * c + t
                        if c in (0, 2):
                            acc_wait_ready(act, it, 8, g)
                            free_acc(f((ga_t, gb_t)[c // 2][:, t], acc[g % 2][:], ACT.Sigmoid), g)
                    if c == 1:
                        acc_wait_ready(act, it, 8, GB["GO"] + 3)
                for t in range(2):
                    act.wait_ge(s_("mf_ready"), it * 2 + (t + 1))
                    f(merged[0][:, bass.ds(it * 2 + t, 1)].rearrange("p a n -> p (a n)"), ya_t[:, t], ACT.Copy).then_inc(s_("merged_hi"), 1)

            act.wait_ge(s_("merged_ready"), KT)
            act.dma_start(mem, A["mem"]).then_inc(s_("mem_in"), 16)
            act.wait_ge(s_("gtp_ready"), 1)
            for m in range(KT):
                if m % 2 == 0:
                    split_hi(act, 0, 2, JB["WO"] + m // 2 + 1)
                if m == 2:
                    act.wait_ge(s_("mem_in"), 16)
                    for k in range(KT):
                        W(act, "accm_done", k)
                        f(sqm, mem[:, k], ACT.Square).then_inc(s_("sqm_ready"), 1)
                if m == 4:
                    act.wait_ge(s_("summ_done"), 1)
                    f(rstd_m, S[1][:, 0:CTX], ACT.Sqrt, scale=1.0 / D, bias=eps).then_inc(s_("rmsm_ready"), 1)
                if m == 6:
                    for k in range(KT):
                        act.wait_ge(s_("hmf_ready"), k + 1)
                        f(hm[0][:, k], mem[:, k], ACT.Copy).then_inc(s_("hm_hi"), 1)
                if m == 7:
                    act.wait_ge(s_("accm_done"), KT)
                g = GB["WO"] + m
                acc_wait_ready(act, 0, 2, g)
                f(nat_out(y[:, m]), nat(acc[g % 2][:]), ACT.Copy, scale=gtp[:, m:m + 1]).then_inc(s_("y_ready"), 1)
                act.wait_ge(s_("y_ready"), m + 1)
                W(act, "accy_done", m)
                free_acc(f(nat_out(sq), nat(acc[g % 2][:]), ACT.Square), g)
            act.wait_ge(s_("hm_ready"), KT)
            for k in range(2):
                act.dma_start(xin[k], A["x_natural"][:, k]).then_inc(s_(f"xin{k}"), 16)

            def x1_tile(k):
                act.wait_ge(s_("x1_ready"), k + 1)
                f(h2[0][:, k], y[:, k], ACT.Copy, scale=par[:, P_MIX + k:P_MIX + k + 1]).then_inc(s_("h2_hi"), 1)
                W(act, "acc1_done", k)
                f(sq, y[:, k], ACT.Square).then_inc(s_("sq1_ready"), 1)
                if k < 6:
                    act.dma_start(xin[k % 2], A["x_natural"][:, k + 2]).then_inc(s_(f"xin{k % 2}"), 16)

            for c in range(8):
                split_hi(act, 0, 2, JB["MKV"] + c + 1)
                if 2 <= c < 6:
                    x1_tile(2 * c - 4)
                    x1_tile(2 * c - 3)
                for t in range(2):
                    g = GB["MKV"] + 2 * c + t
                    dst = mk[0][:, 2 * c + t] if c < 4 else mv[0][:, t, 256 * (c - 4):256 * (c - 4) + 256]
                    hi_of("mkv_hi", 0, 2, g, dst, acc[g % 2][:, 0:256])
                if c == 0:
                    act.wait_ge(s_("sum_done"), 1)
                    f(rstd, S[0][:], ACT.Sqrt, scale=1.0 / D, bias=eps).then_inc(s_("rms_ready"), 1)
                if c == 4:
                    wait_evacuated(act, 0, 2, GB["MKV"] + 7)
                    act.dma_start(mkv_dram[:, 0:16 * 256], mkv_all[:, 0:16 * 256]).then_inc(s_("mkv_spilled"), 16)
                if c == 5:
                    act.dma_start(x_dram, y).then_inc(s_("x_spilled"), 16)
                if c == 6:
                    act.wait_ge(s_("sum_done"), 2)
                    f(rstd, S[0][:], ACT.Sqrt, scale=1.0 / D, bias=eps).then_inc(s_("rms_ready"), 1)
                    f(rcol, S[1][:, 0:4], ACT.Sqrt, scale=1.0 / D, bias=eps).then_inc(s_("rms_ready"), 1)
            for t in range(2):
                wait_evacuated(act, 0, 2, GB["MKV"] + 14 + t)
            act.dma_start(mkv_dram[:, 16 * 256:], mkv_all[:, 16 * 256:]).then_inc(s_("mkv_spilled"), 16)

            split_hi(act, 0, 2, JB["FL"] + 1)
            z, az, lf = fl_t[0][0:8], fl_t[1][0:8], fl_t[3][0:8]

            act.wait_ge(s_("rcol_ready"), 1)
            acc_wait_ready(act, 0, 2, GB["FL"])
            for c in range(4):
                split_hi(act, 0, 2, JB["V2"] + c + 1)
                for b in range(4):
                    g = GB["V2"] + 4 * c + b
                    acc_wait_ready(act, 0, 2, g)
                    n = 128 if c < 2 else 64
                    f(head_parts(v2[:, b, 512 * c:512 * c + 512], n, 0), acc[g % 2][:, 0:256].rearrange("p (h n) -> p h n", n=n),
                      ACT.Copy, scale=rcol[:, b:b + 1])\
                        .then_inc(s_("v_hi"), 1)
                    if c == 1 and b == 0:
                        act.wait_ge(s_("fl_ready"), 1)
                        ex.link(f(az, z, ACT.Abs))
                        ex.link(f(az, az, ACT.Exp, scale=-1.0))
                    if c == 1 and b == 1:
                        f(az, az, ACT.Ln, bias=one1[0:8]).then_inc(s_("lnf_ready"), 1)
                    if c == 2 and b == 0:
                        act.wait_ge(s_("cum_ready"), 1)
                        f(cumst[0][0:8], lf, ACT.Copy).then_inc(s_("cum_hi"), 1)
                        f(cumst[2][0:8], lf, ACT.Copy, scale=-1.0).then_inc(s_("cum_hi"), 1)
                if c == 1:
                    act.wait_ge(s_("mkv_spilled"), 32)
                    act.dma_start(fl_sel[0:16], A["sel"]).then_inc(s_("sel_in"), 16)
                if c == 2:
                    act.wait_ge(s_("sel_in"), 16)
                    f(sel16[0:16], fl_sel[0:16], ACT.Copy).then_inc(s_("sel_ready"), 1)
                    act.wait_ge(s_("cum_lo"), 2)
                    for n, dst in ((0, cum16), (2, ncum16)):
                        act.dma_start(dst[0:8].bitcast(f32), cumst[n][0:8].bitcast(f32)).then_inc(s_("cum_in"), 16)
                        act.dma_start(dst[8:16].bitcast(f32), cumst[n + 1][0:8].bitcast(f32)).then_inc(s_("cum_in"), 16)

            act.wait_ge(s_("cum_in"), 64)
            act.wait_ge(s_("x_spilled"), 16)

            def load_strip2(n):
                src = bass.AP(t_dram.tensor, n * NDIST, [[1, 128], [1, SEQ]])
                act.dma_start(strip2[n % 2], src).then_inc(s_(f"strip2_in{n % 2}"), 16)

            load_strip2(0)
            load_strip2(1)
            act.dma_start(cmask, A["cmask"]).then_inc(s_("attn2_in"), 16)
            act.dma_start(gsub, A["gsub"]).then_inc(s_("attn2_in"), 16)

            def qk2_hi(n, x):
                wait_evacuated(act, 0, 2, GB["DQK"] + 2 * n + x)
                f((q2, k2)[x][n % 2][0], tmp, ACT.Copy).then_inc(s_("qk2_hi"), 1)

            split_hi(act, 0, 2, JB["DQK"] + 1)
            qk2_hi(0, 0)
            qk2_hi(0, 1)

            def extra2(fox):
                def extra(it, pc, i):
                    n = pc + 4 * fox + 1
                    if i == 1:
                        act.wait_ge(s_("acc_ready"), GB["DQK"] + 2 * n)
                        if n < 8:
                            split_hi(act, 0, 2, JB["DQK"] + n + 1)
                    if i == 3 and n < 8:
                        qk2_hi(n, 0)
                    if i == 6 and n < 8:
                        qk2_hi(n, 1)
                    if not fox and i == 0 and pc in (1, 2):
                        act.wait_ge(s_("bias_done"), DF.g0 + 8 * pc)
                        load_strip2(pc + 1)
                return extra


            def square_sub(pc, qb):
                act.wait_ge(s_("o_free1"), step_half(DF, 0, pc, 2 * qb + 1) + 1)
                t = 4 * qb + pc
                W(act, "subsq_done", 4 * pc + qb)
                f(subsq, odiff[:, t], ACT.Square, accum_out=ssum[:, t:t + 1]).then_inc(s_("subsq_done"), 1)

            def extra_diff(it, pc, i):
                extra2(0)(it, pc, i)
                if pc and i < 8 and i % 2:
                    square_sub(pc - 1, i // 2)

            def extra_fox(it, pc, i):
                extra2(1)(it, pc, i)
                if pc == 0 and i < 4:
                    square_sub(3, i)
                    if i == 3:
                        act.wait_ge(s_("subsq_done"), 16)
                        f(srst, ssum, ACT.Sqrt, scale=1.0 / 128, bias=eps).then_inc(s_("srms_ready"), 1)

            for pc in range(4):
                attend(DF, 0, pc, pc == 0, pc == 3, extra_diff)
            for pc in range(4):
                attend(FX, 0, pc, pc == 0, pc == 3, extra_fox)

            with act.Fori(0, 2) as it:
                for c in range(6):
                    split_hi(act, it, 6, JB["GO2"] + c + 1)
                    mp, g = c // 3, GB["GO2"] + 8 * (c // 3) + 2 * (c % 3)
                    if c % 3 < 2:
                        for t in range(2):
                            wait_evacuated(act, it, 16, g + t)
                            gate = (ga_t, gb_t)[c % 3][:, t]
                            f(gate, gate, ACT.Sigmoid).then_inc(s_("gate2_ready"), 1)
                    else:
                        for t in range(2):
                            act.wait_ge(s_("mf2_ready"), it * 4 + (2 * mp + t + 1))
                            f(merged[0][:, bass.ds(it * 4 + (2 * mp + t), 1)].rearrange("p a n -> p (a n)"), ya_t[:, t], ACT.Copy)\
                                .then_inc(s_("merged2_hi"), 1)

            def stream(name, job, group, n, gain):
                if n % 2 == 0:
                    split_hi(act, 0, 2, JB[job] + n // 2 + 1)
                wait_evacuated(act, 0, 2, GB[group] + n)
                f(xg[0][:, n], y[:, n], ACT.Copy, scale=par[:, gain + n:gain + n + 1]).then_inc(s_("xg_hi"), 1)
                W(act, name, n)
                f(sq, y[:, n], ACT.Square).then_inc(s_("sqx_ready"), 1)

            act.wait_ge(s_("merged2_ready"), KT)
            act.dma_start(y, x_dram).then_inc(s_("x_back"), 16)
            act.dma_start(mkv_all, mkv_dram).then_inc(s_("mkv_back"), 16)
            for n in range(KT):
                stream("acc2_done", "WO2", "WO2", n, P_MQ)

            split_hi(act, 0, 2, JB["QM"] + 1)
            act.wait_ge(s_("sum_done"), 3)
            f(rstd, S[0][:], ACT.Sqrt, scale=1.0 / D, bias=eps).then_inc(s_("rms_ready"), 1)

            def qm_hi(n, x):
                wait_evacuated(act, 0, 2, GB["QM"] + 2 * n + x)
                f(qm[n % 2][0][:, x], tmp, ACT.Copy).then_inc(s_("qm_hi"), 1)

            qm_hi(0, 0)
            qm_hi(0, 1)

            def extram(it, pc, i):
                if i == 0 and pc < 3:
                    act.wait_ge(s_("acc_ready"), GB["QM"] + 2 * pc + 2)
                    split_hi(act, 0, 2, JB["QM"] + pc + 2)
                if i in (1, 2) and pc < 3:
                    qm_hi(pc + 1, i - 1)

            for pc in range(4):
                attend(MM, 0, pc, pc == 0, pc == 3, extram)
            for n in range(KT):
                stream("acc3_done", "OM", "OM", n, P_MLP)

            def up(it, per, gper, c, jb, gb, done0):
                split_hi(act, it, per, jb + c + 1)
                if done0 == 0 and c == 0:
                    act.wait_ge(s_("sum_done"), 4)
                    f(rstd, S[0][:], ACT.Sqrt, scale=1.0 / D, bias=eps).then_inc(s_("rms_ready"), 1)
                for t in range(2):
                    act.wait_ge(s_("actf_ready"), it * 8 + (done0 + 2 * c + t + 1))
                    f(act2[0][:, 2 * c + t], mt[t], ACT.Copy).then_inc(s_("act_hi"), 1)

            def down(it, per, gper, c, jb, gb):
                split_hi(act, it, per, jb + c + 1)
                for t in range(2):
                    acc_wait_ready(act, it, gper, gb + 2 * c + t)

            for c in range(4):
                up(0, 8, 16, c, JB["MLP"], GB["MLP"], 0)
            for c in range(4, 8):
                down(0, 8, 16, c, JB["MLP"], GB["MLP"])
            with act.Fori(0, 2) as it:
                for c in range(4):
                    up(it, 8, 16, c, JB["MLP"] + 8, GB["MLP"] + 16, 8)
                for c in range(4, 8):
                    down(it, 8, 16, c, JB["MLP"] + 8, GB["MLP"] + 16)
            for c in range(4):
                up(0, 8, 16, c, JB["MLP"] + 24, GB["MLP"] + 48, 24)
            for n in range(KT):
                if n % 2 == 0 and n < 6:
                    split_hi(act, 0, 2, JB["MLP"] + 24 + 4 + n // 2 + 1)
                wait_evacuated(act, 0, 2, GB["MLP"] + 56 + n)
                W(act, "acc4_done", n)
                f(sq, y[:, n], ACT.Square).then_inc(s_("sqx_ready"), 1)
                if n >= DVE_LAST:
                    f(y[:, n], y[:, n], ACT.Copy, scale=par[:, P_FIN + n:P_FIN + n + 1]).then_inc(s_("y_gained"), 1)
            act.wait_ge(s_("sum_done"), 5)
            f(rstd, S[0][:], ACT.Sqrt, scale=1.0 / D, bias=eps).then_inc(s_("rms_ready"), 1)

        @block.vector
        def _(v):
            own = Chain(v, s_("dve_own"))
            link = own.link
            tt, stt, ts = nc.vector.tensor_tensor, nc.vector.scalar_tensor_tensor, nc.vector.tensor_scalar
            MUL, ADD, SUB, MAX, MIN = ALU.mult, ALU.add, ALU.subtract, ALU.max, ALU.min

            def lo(dst, src, hi):
                return tt(dst, src, hi.bitcast(f32), SUB)

            def vec(col, n=1):
                return par[:, col:col + n]

            def reciprocal_of(sem_value, t):
                v.wait_ge(s_("rms_ready"), sem_value)
                link(nc.vector.reciprocal(t, t))

            v.sem_inc(s_("acc_free0"), 1)
            v.sem_inc(s_("acc_free1"), 1)
            v.wait_ge(s_("par_in"), 16)
            v.wait_ge(s_("sigc_ready"), 1)
            tt(silc, silc, par[:, P_C:P_C + 16], MUL).then_inc(s_("silc_ready"), 1)
            v.wait_ge(s_("silr_hi"), 1)
            lo(silr[:, 1], silc, silr[:, 0])

            for x, w, total in ((0, CTX, acc_c), (1, SEQ, acc_x)):
                for k in range(KT):
                    v.wait_ge(s_("sq0_ready"), KT * x + k + 1)
                    if k == 0:
                        nc.vector.tensor_copy(total, sq0[0][:, 0:w]).then_inc(s_("acc0_done"), 1)
                    else:
                        v.wait_ge(s_("acc0_done"), KT * x + k)
                        tt(total, total, sq0[k % 2][:, 0:w], ADD).then_inc(s_("acc0_done"), 1)
            v.wait_ge(s_("rms0_ready"), 1)
            link(nc.vector.reciprocal(rstd_c, rstd_c))
            for k in range(KT):
                last = tt(ctx0[:, k], ctx0[:, k], rstd_c, MUL)
            link(last)
            v.wait_ge(s_("rms0_ready"), 2)
            link(nc.vector.reciprocal(rstd_x, rstd_x))
            for k in range(KT):
                last = tt(x0[:, k], x0[:, k], rstd_x, MUL)
            link(last)
            v.wait_ge(s_("mod_done"), 1)
            modp = T[0][:, 0:32].rearrange("p (m s) -> p m s", s=2)
            for s in range(2):
                last = tt(mods[:, 0:16, s], modp[:, 0:16, s], vec(P_BMOD, 16), ADD)
            link(last)
            for s, ax in ((1, mod_ac), (0, mod_ax)):
                last = stt(ax, mods[:, 8:16, s], 1.0, vec(P_PRE, 8), ADD, MUL)
            link(last)
            for k in range(KT + 2):
                if k < KT:
                    ts(ctx0[:, k], ctx0[:, k], mod_ac[:, k:k + 1], mods[:, k, 1:2], MUL, ADD).then_inc(s_("hcf_ready"), 1)
                if k >= 2:
                    v.wait_ge(s_("hc_hi"), k - 1)
                    lo(hc[1][:, k - 2], ctx0[:, k - 2], hc[0][:, k - 2]).then_inc(s_("hc_ready"), 1)
            ts(x0[:, 0], x0[:, 0], mod_ax[:, 0:1], mods[:, 0, 0:1], MUL, ADD).then_inc(s_("hf_ready"), 1)
            for k in range(KT):
                if k + 1 < KT:
                    ts(x0[:, k + 1], x0[:, k + 1], mod_ax[:, k + 1:k + 2], mods[:, k + 1, 0:1], MUL, ADD)\
                        .then_inc(s_("hf_ready"), 1)
                v.wait_ge(s_("h_hi"), k + 1)
                lo(h[1][:, k], x0[:, k], h[0][:, k]).then_inc(s_("h_ready"), 1)

            with v.Fori(0, 2) as it:
                for c in range(2):
                    for gi in range(6):
                        if gi == 2:
                            if c == 0:
                                v.wait_ge(s_("lo_done"), it * 2 + (JB["V"] + 1))
                            split_job(v, it, 2, JB["V"] + c + 1)
                        g = GB["V"] + 6 * c + gi
                        t = Vc if gi < 2 else V
                        t = t[:, gi if gi < 2 else gi - 2][:, bass.ds(it * 1024 + 512 * c, 512)]
                        v.wait_ge(s_("v_hi"), it * 12 + (6 * c + gi + 1))
                        free_acc(lo(head_parts(t, 64, 1), acc[g % 2][:, 0:256].rearrange("p (h n) -> p h n", n=64),
                                    head_parts(t, 64, 0)), g)

            v.wait_ge(s_("lam_in"), 16)
            link(tt(lamv[:, 0:2], lamv[:, 0:2], lamv[:, 2:4], MUL))
            nc.vector.tensor_reduce(lamt[:, 0:2], lamv[:, 0:2], axis=AX.X, op=ADD).then_inc(s_("lam_sum"), 1)
            v.wait_ge(s_("lam_exp"), 1)
            link(stt(nlam, lamt[:, 3:4], LAMBDA_INIT, lamt[:, 2:3], SUB, SUB))
            v.wait_ge(s_("relt_done"), 1)
            v.wait_ge(s_("relt_in"), 16)
            tt(relt[0:4, 0:SEQ], S[0][0:4, :], relt[0:4, 0:SEQ], ADD)
            tt(relt[0:4, SEQ:NDIST], S[1][0:4, 0:128], relt[0:4, SEQ:NDIST], ADD).then_inc(s_("relt_sum"), 1)

            split_job(v, 0, 2, JB["QK"] + 1)
            v.wait_ge(s_("relt_out"), 16)
            v.wait_ge(s_("rope_in"), 48)
            swap = [(n + 16) % 32 for n in range(32)]

            def rope(it, pc, x):
                g = GB["QK"] + 3 * pc + x
                W(v, "rope_lo", it * 4 + (2 * pc + x))
                acc_wait_ready(v, it, 6, g)
                stt(rope_a, acc[g % 2][:], (0.125, 1.0)[x], cos_t, MUL, MUL).then_inc(s_("rope_cos"), 1)
                free_acc(nc.vector.stream_shuffle(rope_b, acc[g % 2][:], swap), g)

            def kc_lo(it, pc):
                g = GB["QK"] + 3 * pc + 2
                v.wait_ge(s_("kc_hi"), it * 2 + pc + 1)
                free_acc(lo(kcs[pc % 2][1], acc[g % 2][:, 0:CTX], kcs[pc % 2][0]), g)

            rope(0, 0, 0)
            rope(0, 0, 1)
            kc_lo(0, 0)

            def attend(s, it, pc, first, last_pair, extra=None):
                def made(j):
                    return (j >= 0 or not first) and j < s.n
                for i in range(s.n + (4 if last_pair else 0)):
                    g = step_no(s, it, pc, i)
                    a, b = i % 2, 1 - i % 2
                    if i < s.n:
                        n, cc = s.cols(i), i % 8
                        v.wait_ge(s_("qk_done"), g + 1)
                        if s is NB:
                            v.wait_ge(s_("bm_done"), g + 1)
                            tt(S[a][:, 0:256], S[a][:, 0:256], bm[a], ADD).then_inc(s_("bias_done"), 1)
                        if s is DF:
                            v.wait_ge(s_(f"strip2_in{pc % 2}"), 16 * (pc // 2 + 1))
                            rev = strip2[pc % 2][:, n - 1::-1] if n == SEQ else strip2[pc % 2][:, 0:n][:, ::-1]
                            tt(S[a][:, 0:n], S[a][:, 0:n], rev, ADD).then_inc(s_("bias_done"), 1)
                        if s is FX:
                            v.wait_ge(s_("attn2_in"), 32)
                            tt(S[a][:, n - 128:n], S[a][:, n - 128:n], cmask, ADD).then_inc(s_("bias_done"), 1)
                        if s is not MM:
                            v.wait_ge(s_("bias_done"), g + 1)
                        nc.vector.tensor_reduce(negmax[:, cc:cc + 1], S[a][:, 0:n], axis=AX.X, op=MAX, negate=True)\
                            .then_inc(s_("max_done"), 1)
                    if made(i - 1):
                        n, cc = s.cols((i - 1) % s.n), (i - 1) % s.n % 8
                        v.wait_ge(s_("exp_done"), g)
                        if s is DF and b == 1:
                            link(nc.vector.reciprocal(rinv[:, cc:cc + 1], rowsum[:, cc:cc + 1]))
                            tt(rinv[:, cc:cc + 1], rinv[:, cc:cc + 1], nlam, MUL).then_inc(s_("rinv_done"), 1)
                        else:
                            nc.vector.reciprocal(rinv[:, cc:cc + 1], rowsum[:, cc:cc + 1]).then_inc(s_("rinv_done"), 1)
                        v.wait_ge(s_("phi_done"), g)
                        lo(s.pt[b][1][:, 0:n], T[b][:, 0:n], s.pt[b][0][:, 0:n]).then_inc(s_("plo_done"), 1)
                    if s is FX and a == 0 and made(i - 4) and made(i - 3):
                        qb, pr = (i // 2 - 2) % 4, pc - 1 if i < 4 else pc
                        v.wait_ge(s_("ot_hi"), ot_no(s, it, pc, i) - 32 + 1)
                        cols = slice(128 * qb, 128 * qb + 128)
                        lo(oab2[:, :, 1, pr, cols], O[1][:, 256:512].rearrange("p (x n) -> p x n", x=2),
                           oab2[:, :, 0, pr, cols]).then_inc(s_("ot_free"), 1)
                    if s is MM and made(i - 3):
                        j, pr = (i - 3) % 4, pc - 1 if i < 3 else pc
                        v.wait_ge(s_("ot_hi"), 16 + 4 * pc + i - 3 + 1)
                        cols = slice(128 * j, 128 * j + 128)
                        lo(om[1][:, 2 * pr:2 * pr + 2, cols], O[b][:, 256:512].rearrange("p (t n) -> p t n", t=2),
                           om[0][:, 2 * pr:2 * pr + 2, cols]).then_inc(s_("ot_free"), 1)
                    if s is DF and a == 1 and made(i - 2):
                        j = (i - 2) % 8
                        pr = pc - 1 if i < 2 else pc
                        v.wait_ge(s_("pv_done"), g - 1)
                        v.wait_ge(s_("o_free0"), step_half(s, it, pc, i - 3) + 1)
                        od, r = odiff[:, 4 * (j // 2) + pr], rinv[:, j:j + 1]
                        link(stt(od, O[1][:, 0:128], r, osb2[(j // 2) % 2], MUL, ADD))
                        stt(od, O[1][:, 128:256], r, od, MUL, ADD).then_inc(s_("o_free1"), 1)
                    elif s is not MM and made(i - 2):
                        j = (i - 2) % 8
                        v.wait_ge(s_(f"o_main{a}"), step_half(s, it, pc, i - 2) + (1 - 16 if s is FX and a else 1))
                        v.wait_ge(s_("rinv_done"), g - 1)
                        if s is DF:
                            dst, w = s.osb[(j // 2) % 2], 128
                        else:
                            dst, w = s.osb[(j // 2) % 2][:, 64 * a:64 * a + 64], 64
                        stt(dst, O[a][:, w:2 * w], rinv[:, j:j + 1], dst, MUL, ADD).then_inc(s_(f"o_free{a}"), 1)
                    if extra:
                        extra(it, pc, i)

            def nb_extra(it, pc, i):
                if i == 2:
                    rope(it, pc + 1, 0)
                if i == 5:
                    rope(it, pc + 1, 1)
                if i == 6:
                    kc_lo(it, pc + 1)

            attend(NB, 0, 0, True, False, nb_extra)
            with v.Fori(0, 3) as it:
                for pc in (1, 2):
                    attend(NB, it, pc, False, False, nb_extra)
            attend(NB, 0, 7, False, True)

            v.wait_ge(s_("lo_done"), JB["CONV"] + 1)
            with v.Fori(0, 4) as it:
                own.loop(it, 4)
                for c in range(4):
                    split_job(v, it, 4, JB["CONV"] + c + 1)
                    g = GB["CONV"] + 2 * c
                    if c == 0:
                        acc_wait_ready(v, it, 8, g + 1)
                    for t in range(2):
                        if c == 1:
                            wait_evacuated(v, it, 8, g - 2 + t)
                            acc_wait_ready(v, it, 8, g + t)
                            free_acc(tt(u_t[:, t], acc[(g + t) % 2][:], c_t[:, t], MUL), g + t)
                        if c == 2:
                            v.wait_ge(s_("tap_ready"), it * 2 + (t + 1))
                            u, yy = u_t[:, t], y_t[:, t]
                            w0 = par[:, bass.ds(it * 2 + (P_CW + t), 1)]
                            w2 = par[:, bass.ds(it * 2 + (P_CW + 16 + t), 1)]
                            stt(yy[:, GR:], u[:, 0:SEQ - GR], w0, yy[:, GR:], MUL, ADD)
                            link(stt(yy[:, 1:GR], u[:, SEQ - GR:SEQ - 1], w0, yy[:, 1:GR], MUL, ADD))
                            stt(yy[:, 0:SEQ - GR], u[:, GR:], w2, yy[:, 0:SEQ - GR], MUL, ADD)
                            link(stt(yy[:, SEQ - GR:SEQ - 1], u[:, 1:GR], w2, yy[:, SEQ - GR:SEQ - 1], MUL, ADD))
                            acc_wait_ready(v, it, 8, g + t)
                            free_acc(tt(yy, acc[(g + t) % 2][:], yy, MUL), g + t)
                        if c == 3:
                            v.wait_ge(s_("zsig_ready"), it * 2 + (t + 1))
                            free_acc(tt(sg_t[:, t], acc[(g + t) % 2][:], sg_t[:, t], MUL), g + t)
                            wait_evacuated(v, it, 8, g + t)
                            tt(y_t[:, t], y_t[:, t], sg_t[:, t], MUL).then_inc(s_("cinf_ready"), 1)
                for t in range(2):
                    v.wait_ge(s_("cin_hi"), it * 2 + (t + 1))
                    m = bass.ds(it * 2 + t, 1)
                    lo(cin[1][:, m].rearrange("p a n -> p (a n)"), y_t[:, t], cin[0][:, m].rearrange("p a n -> p (a n)"))\
                        .then_inc(s_("cin_ready"), 1)
            own.done(4)

            for c in range(4):
                split_job(v, 0, 2, JB["ZB"] + 2 * c + 1)
                for t in range(2):
                    g = GB["ZB"] + 3 * c + t
                    if t == 1:
                        split_job(v, 0, 2, JB["ZB"] + 2 * c + 2)
                    v.wait_ge(s_("bsig_ready"), 2 * c + t + 1)
                    free_acc(tt(sg_t[:, t], acc[g % 2][:], sg_t[:, t], MUL), g)
                    v.wait_ge(s_(f"o_in{c % 2}"), 16 * (c // 2 + 1))
                    wait_evacuated(v, 0, 2, g)
                    tt(y_t[:, t], sg_t[:, t], o_in[c % 2][:, t], MUL).then_inc(s_("ogf_ready"), 1)
                for t in range(2):
                    m = 2 * c + t
                    v.wait_ge(s_("og_hi"), m + 1)
                    lo(og[1][:, m], y_t[:, t], og[0][:, m]).then_inc(s_("og_ready"), 1)

            with v.Fori(0, 4) as it:
                for c in range(4):
                    split_job(v, it, 4, JB["GO"] + c + 1)
                    g = GB["GO"] + 2 * c
                    if c % 2 == 0:
                        acc_wait_ready(v, it, 8, g + 1)
                        continue
                    for t in range(2):
                        wait_evacuated(v, it, 8, g - 2 + t)
                        acc_wait_ready(v, it, 8, g + t)
                        free_acc(tt((ya_t, yb_t)[c // 2][:, t], acc[(g + t) % 2][:], (ga_t, gb_t)[c // 2][:, t], MUL), g + t)
                for t in range(2):
                    wait_evacuated(v, it, 8, GB["GO"] + 6 + t)
                    tt(ya_t[:, t], ya_t[:, t], yb_t[:, t], ADD).then_inc(s_("mf_ready"), 1)
                for t in range(2):
                    v.wait_ge(s_("merged_hi"), it * 2 + (t + 1))
                    m = bass.ds(it * 2 + t, 1)
                    lo(merged[1][:, m].rearrange("p a n -> p (a n)"), ya_t[:, t],
                       merged[0][:, m].rearrange("p a n -> p (a n)")).then_inc(s_("merged_ready"), 1)

            v.wait_ge(s_("gcol_done"), 4)
            gcol = T[0][:, 0:16].rearrange("p (m s) -> p m s", s=2)[:, :, 0]
            link(tt(gtp, gcol, vec(P_BMOD + 16, 8), ADD))
            tt(gtp, gtp, vec(P_POST, 8), MUL).then_inc(s_("gtp_ready"), 1)

            for c in range(4):
                split_job(v, 0, 2, JB["WO"] + c + 1)
                if c == 2:
                    v.wait_ge(s_("rmsm_ready"), 1)
                    link(nc.vector.reciprocal(rstd_m, rstd_m))
                    for k in range(KT):
                        stt(mem[:, k], mem[:, k], vec(P_MKV + k), rstd_m, MUL, MUL).then_inc(s_("hmf_ready"), 1)
                if c == 3:
                    for k in range(KT):
                        v.wait_ge(s_("hm_hi"), k + 1)
                        lo(hm[1][:, k], mem[:, k], hm[0][:, k]).then_inc(s_("hm_ready"), 1)
                acc_wait_ready(v, 0, 2, GB["WO"] + 2 * c + 1)

            def x1_tile(k):
                if k < KT:
                    link(tt(y[:, k], y[:, k], rstd, MUL))
                    v.wait_ge(s_(f"xin{k % 2}"), 16 * (k // 2 + 1))
                    tt(y[:, k], y[:, k], xin[k % 2], ADD).then_inc(s_("x1_ready"), 1)
                if k > 0:
                    k -= 1
                    v.wait_ge(s_("h2_hi"), k + 1)
                    stt(h2[1][:, k], y[:, k], vec(P_MIX + k), h2[0][:, k].bitcast(f32), MUL, SUB).then_inc(s_("h2_ready"), 1)
                    v.wait_ge(s_("sq1_ready"), k + 1)
                    if k == 0:
                        nc.vector.tensor_copy(acc_sq, sq).then_inc(s_("acc1_done"), 1)
                    else:
                        v.wait_ge(s_("acc1_done"), k)
                        tt(acc_sq, acc_sq, sq, ADD).then_inc(s_("acc1_done"), 1)

            for c in range(8):
                if c == 0 or c > 4:
                    v.wait_ge(s_("lo_done"), JB["MKV"] + c + 1)
                    split_job(v, 0, 2, JB["MKV"] + c + 1)
                for t in range(2):
                    g = GB["MKV"] + 2 * c + t
                    v.wait_ge(s_("mkv_hi"), 2 * c + t + 1)
                    d = (mk[0][:, 2 * c + t], mk[1][:, 2 * c + t]) if c < 4 else \
                        tuple(p[:, t, 256 * (c - 4):256 * (c - 4) + 256] for p in mv)
                    free_acc(lo(d[1], acc[g % 2][:, 0:256], d[0]), g)
                if c == 0:
                    reciprocal_of(1, rstd)
                if 1 <= c < 5:
                    x1_tile(2 * c - 2)
                    x1_tile(2 * c - 1)
                if c == 5:
                    x1_tile(KT)
                if c == 7:
                    reciprocal_of(2, rstd)
                    v.wait_ge(s_("rms_ready"), 3)
                    nc.vector.reciprocal(rcol, rcol).then_inc(s_("rcol_ready"), 1)

            split_job(v, 0, 2, JB["FL"] + 1)
            z, m0, cum = fl_t[0][0:8], fl_t[2][0:8], fl_t[3][0:8]
            g = GB["FL"]
            acc_wait_ready(v, 0, 2, g)
            free_acc(tt(z, acc[g % 2][0:8], rstd[0:8], MUL), g)
            wait_evacuated(v, 0, 2, g)
            link(ts(z, z, par[0:8, P_BF:P_BF + 1], None, ADD))
            ts(m0, z, 0.0, None, MIN).then_inc(s_("fl_ready"), 1)

            for c in range(4):
                split_job(v, 0, 2, JB["V2"] + c + 1)
                for b in range(4):
                    g = GB["V2"] + 4 * c + b
                    v.wait_ge(s_("v_hi"), 24 + 4 * c + b + 1)
                    n, t = 128 if c < 2 else 64, v2[:, b, 512 * c:512 * c + 512]
                    free_acc(stt(head_parts(t, n, 1), acc[g % 2][:, 0:256].rearrange("p (h n) -> p h n", n=n),
                                 rcol[:, b:b + 1], head_parts(t, n, 0).bitcast(f32), MUL, SUB), g)
                    if c == 1 and b == 2:
                        v.wait_ge(s_("lnf_ready"), 1)
                        v.wait_ge(s_("fl_ready"), 1)
                        tt(m0, m0, fl_t[1][0:8], SUB)
                        link(nc.vector.memset(z, 1.0))
                        nc.vector.tensor_tensor_scan(cum, z, m0, 0.0, MUL, ADD).then_inc(s_("cum_ready"), 1)
                    if c == 2 and b == 0:
                        v.wait_ge(s_("cum_hi"), 2)
                        lo(cumst[1][0:8], cum, cumst[0][0:8]).then_inc(s_("cum_lo"), 1)
                        stt(cumst[3][0:8], cum, -1.0, cumst[2][0:8].bitcast(f32), MUL, SUB).then_inc(s_("cum_lo"), 1)

            def qk2_sum(n, x):
                g = GB["DQK"] + 2 * n + x
                W(v, "qk2_lo", 2 * n + x)
                acc_wait_ready(v, 0, 2, g)
                free_acc(stt(tmp, acc[g % 2][:], (0.125, 1.0)[x], rstd, MUL, MUL), g)

            def qk2_lo(n, x):
                v.wait_ge(s_("qk2_hi"), 2 * n + x + 1)
                p = (q2, k2)[x][n % 2]
                lo(p[1], tmp, p[0]).then_inc(s_("qk2_lo"), 1)

            split_job(v, 0, 2, JB["DQK"] + 1)
            for x in range(2):
                qk2_sum(0, x)
                qk2_lo(0, x)

            def extra2(fox):
                def extra(it, pc, i):
                    n = pc + 4 * fox + 1
                    if n < 8 and i in (2, 5):
                        qk2_sum(n, i // 3)
                return extra

            for pc in range(4):
                attend(DF, 0, pc, pc == 0, pc == 3, extra2(0))

            def extra_fox(it, pc, i):
                extra2(1)(it, pc, i)
                if pc == 0 and i == 3:
                    v.wait_ge(s_("srms_ready"), 1)
                    v.wait_ge(s_("attn2_in"), 32)
                    link(nc.vector.reciprocal(srst, srst))
                    link(ts(srst, srst, 1.0 - LAMBDA_INIT, None, MUL))
                    scale_sub(0)
                if i % 2 and (pc or i > 3) and i < 11:
                    scale_sub(4 * pc + i // 2 - 1)

            def scale_sub(u):
                t = 4 * (u % 4) + u // 4
                stt(odiff[:, t], odiff[:, t], srst[:, t:t + 1], gsub, MUL, MUL).then_inc(s_("sub_ready"), 1)

            for pc in range(4):
                attend(FX, 0, pc, pc == 0, pc == 3, extra_fox)

            v.wait_ge(s_("lo_done"), JB["GO2"] + 1)
            with v.Fori(0, 2) as it:
                for c in range(6):
                    split_job(v, it, 6, JB["GO2"] + c + 1)
                    mp, g = c // 3, GB["GO2"] + 8 * (c // 3) + 2 * (c % 3)
                    if c % 3 < 2:
                        for t in range(2):
                            gate = (ga_t, gb_t)[c % 3][:, t]
                            acc_wait_ready(v, it, 16, g + t)
                            free_acc(tt(gate, acc[(g + t) % 2][:], rstd, MUL), g + t)
                        continue
                    for u in range(4):
                        e, t = u % 2, u // 2
                        v.wait_ge(s_("gate2_ready"), it * 8 + (4 * mp + 2 * e + t + 1))
                        acc_wait_ready(v, it, 16, g + u)
                        free_acc(tt((ya_t, yb_t)[e][:, t], acc[(g + u) % 2][:], (ga_t, gb_t)[e][:, t], MUL), g + u)
                    for t in range(2):
                        wait_evacuated(v, it, 16, g + 2 + t)
                        tt(ya_t[:, t], ya_t[:, t], yb_t[:, t], ADD).then_inc(s_("mf2_ready"), 1)
                    for t in range(2):
                        v.wait_ge(s_("merged2_hi"), it * 4 + (2 * mp + t + 1))
                        m = bass.ds(it * 4 + (2 * mp + t), 1)
                        lo(merged[1][:, m].rearrange("p a n -> p (a n)"), ya_t[:, t],
                           merged[0][:, m].rearrange("p a n -> p (a n)")).then_inc(s_("merged2_ready"), 1)

            def add_stream(it, gper, g, n):
                acc_wait_ready(v, it, gper, g)
                free_acc(tt(y[:, n], acc[g % 2][:], y[:, n], ADD), g)

            def stream(name, n, gain, made0):
                if n % 2 == 0 and (name, n) != ("WO2", 0):
                    split_job(v, 0, 2, JB[name] + n // 2 + 1)
                g = GB[name] + n
                add_stream(0, 2, g, n)
                wait_evacuated(v, 0, 2, g)
                v.wait_ge(s_("xg_hi"), made0 + n + 1)
                stt(xg[1][:, n], y[:, n], vec(gain + n), xg[0][:, n].bitcast(f32), MUL, SUB).then_inc(s_("xg_ready"), 1)

            split_job(v, 0, 2, JB["WO2"] + 1)
            v.wait_ge(s_("x_back"), 16)
            for n in range(KT):
                stream("WO2", n, P_MQ, 0)

            split_job(v, 0, 2, JB["QM"] + 1)
            reciprocal_of(4, rstd)

            def qm_tile(n, x):
                g = GB["QM"] + 2 * n + x
                acc_wait_ready(v, 0, 2, g)
                W(v, "qm_lo", 2 * n + x)
                free_acc(stt(tmp, acc[g % 2][:], 1.0 / 16, rstd, MUL, MUL), g)
                v.wait_ge(s_("qm_hi"), 2 * n + x + 1)
                lo(qm[n % 2][1][:, x], tmp, qm[n % 2][0][:, x]).then_inc(s_("qm_lo"), 1)

            qm_tile(0, 0)
            qm_tile(0, 1)

            def extram(it, pc, i):
                if i == 0 and pc < 3:
                    v.wait_ge(s_("acc_ready"), GB["QM"] + 2 * pc + 2)
                    split_job(v, 0, 2, JB["QM"] + pc + 2)
                if i in (1, 2) and pc < 3:
                    qm_tile(pc + 1, i - 1)

            for pc in range(4):
                attend(MM, 0, pc, pc == 0, pc == 3, extram)
            for n in range(KT):
                stream("OM", n, P_MLP, KT)

            def up(it, per, gper, c, jb, gb, done0):
                split_job(v, it, per, jb + c + 1)
                if done0 == 0 and c == 0:
                    reciprocal_of(5, rstd)
                for t in range(2):
                    g = gb + 2 * c + t
                    W(v, "act_ready", it * 8 + (done0 + 2 * c + t) - 1)
                    acc_wait_ready(v, it, gper, g)
                    free_acc(tt(mt[t], acc[g % 2][:], rstd, MUL), g)
                    wait_evacuated(v, it, gper, g)
                    stt(mt[t], mt[t], 0.0, mt[t], MAX, MUL).then_inc(s_("actf_ready"), 1)
                for t in range(2):
                    v.wait_ge(s_("act_hi"), it * 8 + (done0 + 2 * c + t + 1))
                    lo(act2[1][:, 2 * c + t], mt[t], act2[0][:, 2 * c + t]).then_inc(s_("act_ready"), 1)

            def down(it, per, gper, c, jb, gb, split=True):
                if split:
                    split_job(v, it, per, jb + c + 1)
                for t in range(2):
                    add_stream(it, gper, gb + 2 * c + t, 2 * (c - 4) + t)

            def quarter(it, jb, gb, done0, final=False):
                for c in range(4):
                    up(it, 8, 16, c, jb, gb, done0)
                for c in range(4, 8):
                    down(it, 8, 16, c, jb, gb, not (final and c == 7))
            quarter(0, JB["MLP"], GB["MLP"], 0)
            with v.Fori(0, 2) as it:
                quarter(it, JB["MLP"] + 8, GB["MLP"] + 16, 8)
            quarter(0, JB["MLP"] + 24, GB["MLP"] + 48, 24, True)

            v.wait_ge(s_("rms_ready"), 6)
            nc.vector.reciprocal(rstd, rstd).then_inc(s_("rstd_ready"), 1)
            v.wait_ge(s_("rstd_ready"), 1)
            for k in range(DVE_LAST):
                stt(y[:, k], y[:, k], vec(P_FIN + k), rstd, MUL, MUL).then_inc(s_("final_ready"), 1)

        @block.gpsimd
        def _(gp):
            gt = nc.gpsimd.tensor_tensor
            MUL, ADD, SUB = ALU.mult, ALU.add, ALU.subtract
            nc.gpsimd.memset(ones[:], 1.0).then_inc(s_("consts_ready"), 1)
            nc.gpsimd.memset(eps, EPS).then_inc(s_("consts_ready"), 1)
            gp.wait_ge(s_("consts_ready"), 1)
            gp.wait_ge(s_("consts_ready"), 2)
            nc.gpsimd.affine_select(out=ident[:], in_=ones[:], compare_op=ALU.is_equal, fill=0.0, base=0,
                                    pattern=[[-1, 128]], channel_multiplier=1).then_inc(s_("consts_ready"), 1)
            split_job(gp, 0, 2, 0)
            gp.wait_ge(s_("h_ready"), KT)
            nc.gpsimd.memset(relb[0:32], 0.0).then_inc(s_("relb_ready"), 1)
            for n in range(2):
                for dst, src in ((slice(0, 64), slice(SEQ - 64, SEQ)), (slice(64, 128), slice(0, 64))):
                    nc.gpsimd.tensor_copy(hseam[n][:, :, dst], h[n][:, :, src]).then_inc(s_("seam_ready"), 1)

            def rope_sum(it, pc, x):
                r = it * 4 + (2 * pc + x)
                g = GB["QK"] + 3 * pc + x
                gp.wait_ge(s_("rope_cos"), r + 1)
                wait_evacuated(gp, it, 6, g)
                gt(rope_b, rope_b, sin_q if x == 0 else sin_t, MUL).then_inc(s_("rope_sin"), 1)
                gp.wait_ge(s_("rope_sin"), r + 1)
                gt(rope_a, rope_a, rope_b, ADD).then_inc(s_("rope_sum"), 1)

            def rope_lo(it, pc, x):
                gp.wait_ge(s_("rope_hi"), it * 4 + (2 * pc + x) + 1)
                p = (qs, ks)[x][pc % 2]
                gt(p[1], rope_a, p[0].bitcast(f32), SUB).then_inc(s_("rope_lo"), 1)

            def bias(it, pc, i):
                if i == 8:
                    pc, i = pc + 1, 0
                qb, e, a = i // 2, i % 2, i % 2
                if i == 0:
                    gp.wait_ge(s_(f"strip_in{pc % 2}"), it * 32 + 32 * (pc // 2 + 1))
                W(gp, "bias_done", step_no(NB, it, pc, i) - 1)
                kind = (0, 1, 1, 2)[qb]
                rev = strip[:, 2 * (pc % 2) + e].rearrange("p (u v) -> p u v", v=15)[:, ::-1, 7::-1]
                gt(bm[a].rearrange("p (u v) -> p u v", v=GR), rev, wmask[:, kind].rearrange("p (u v) -> p u v", v=GR), ADD)\
                    .then_inc(s_("bm_done"), 1)

            gp.wait_ge(s_("rope_in"), 48)
            for x in range(2):
                rope_sum(0, 0, x)
                rope_lo(0, 0, x)
            gp.wait_ge(s_("wmask_in"), 16)
            gp.wait_ge(s_("lam_sum"), 1)
            bias(0, 0, 0)
            gp.wait_ge(s_("lo_done"), JB["QK"] + 2)

            def body(it, pc, last):
                for i in range(8):
                    if not (last and i == 7):
                        bias(it, pc, i + 1)
                    if last:
                        continue
                    if i == 1:
                        gp.wait_ge(s_("acc_ready"), it * 6 + (GB["QK"] + 3 * (pc + 1)))
                        split_job(gp, it, 2, JB["QK"] + pc + 2)
                    if i in (2, 5):
                        rope_sum(it, pc + 1, i // 3)
                    if i in (3, 6):
                        rope_lo(it, pc + 1, i // 3 - 1)

            body(0, 0, False)
            with gp.Fori(0, 3) as it:
                for pc in (1, 2):
                    body(it, pc, False)
            body(0, 7, True)

            def add_square(name, n, dst, src):
                if n == 0:
                    nc.gpsimd.tensor_copy(dst, src).then_inc(s_(name), 1)
                else:
                    gp.wait_ge(s_(name), n)
                    gt(dst, dst, src, ADD).then_inc(s_(name), 1)

            for n in range(KT):
                if n == 2:
                    for k in range(KT):
                        gp.wait_ge(s_("sqm_ready"), k + 1)
                        add_square("accm_done", k, rstd_m, sqm)
                wait_evacuated(gp, 0, 2, GB["WO"] + n)
                add_square("accy_done", n, acc_sq, sq)
            for c in range(1, 5):
                gp.wait_ge(s_("acc_ready"), GB["MKV"] + 2 * c)
                gp.wait_ge(s_("lo_done"), JB["MKV"] + c + 1)
                split_job(gp, 0, 2, JB["MKV"] + c + 1)

            gp.wait_ge(s_("lo_done"), JB["DQK"] + 2)
            for n in range(1, 8):
                gp.wait_ge(s_("acc_ready"), GB["DQK"] + 2 * n)
                split_job(gp, 0, 2, JB["DQK"] + n + 1)
                for x in range(2):
                    gp.wait_ge(s_("qk2_hi"), 2 * n + x + 1)
                    p = (q2, k2)[x][n % 2]
                    gt(p[1], tmp, p[0].bitcast(f32), SUB).then_inc(s_("qk2_lo"), 1)

            for i, name in enumerate(("acc2_done", "acc3_done", "acc4_done")):
                gp.wait_ge(s_("sum_done"), i + 2)
                for n in range(KT):
                    gp.wait_ge(s_("sqx_ready"), KT * i + n + 1)
                    add_square(name, n, acc_sq, sq)
            gp.wait_ge(s_("rstd_ready"), 1)
            gp.wait_ge(s_("y_gained"), KT - DVE_LAST)
            for k in range(DVE_LAST, KT):
                gt(y[:, k], y[:, k], rstd, MUL).then_inc(s_("final_ready_gp"), 1)


def _pair_cols(w, cols):
    w = w.reshape(KT, 128, -1, 128)
    return [np.concatenate([w[:, :, a], w[:, :, b]], axis=-1).transpose(1, 0, 2) for a, b in cols]


def _layout(i):
    win, win2 = np.asarray(i["w_in"][0]), np.asarray(i["w_in_2"][0])

    def seq(first, n):
        return [(first + 2 * j, first + 2 * j + 1) for j in range(n)]

    def square(w, n=4):
        return _pair_cols(np.asarray(w), seq(0, n))

    gate = square(np.asarray(i["w_mod"][0])[:, 2 * D:])
    jobs = _pair_cols(win, seq(48, 4))
    jobs += _pair_cols(win, [(32 + p, 40 + p) for p in range(8)])
    for p in range(4):
        jobs += _pair_cols(win, [(t + 2 * p, t + 2 * p + 1) for t in (8, 16, 0, 24)])
    for p, job in enumerate(_pair_cols(win, seq(56, 4))):
        jobs += [job, gate[p]]
    oc, oa = square(i["w_out_conv"][0]), square(i["w_out_attn"][0])
    ga, gb = _pair_cols(win, seq(64, 4)), _pair_cols(win, seq(72, 4))
    for p in range(4):
        jobs += [ga[p], oc[p], gb[p], oa[p]]
    jobs += square(i["w_o"][0]) + square(i["w_kv_mem_2"][0], 8)
    fl = np.zeros((KT, 128, JW), np.float32)
    fl[:, :, 0:8] = win2[:, 3072:3080].reshape(KT, 128, 8)
    jobs += [fl.transpose(1, 0, 2)]
    jobs += _pair_cols(win2[:, :3072], seq(8, 2)) + _pair_cols(win2[:, :3072], seq(20, 2))
    jobs += _pair_cols(win2[:, :3072], [(p, 4 + p) for p in range(4)] + [(12 + p, 16 + p) for p in range(4)])
    gates = np.ascontiguousarray(win2[:, 3080:])
    ga, gb = _pair_cols(gates, seq(0, 4)), _pair_cols(gates, seq(8, 4))
    both = np.concatenate([np.asarray(i["w_diff_out_2"][0]), np.asarray(i["w_fox_out_2"][0])], axis=0)
    both = square(both)
    for p in range(4):
        jobs += [ga[p], gb[p], both[p]]
    jobs += square(i["w_o_2"][0]) + square(i["w_q_mem_2"][0]) + square(i["w_o_mem_2"][0])
    w1, w2 = np.asarray(i["w1_2"][0]), np.asarray(i["w2_2"][0])
    for q in range(4):
        jobs += _pair_cols(w1, seq(8 * q, 4)) + square(w2[1024 * q:1024 * q + 1024])
    assert len(jobs) == NJ, (len(jobs), NJ)

    def feat(t):
        return np.asarray(t).T.reshape(KT, 128, -1).transpose(1, 0, 2)

    def vecs(t):
        return np.asarray(t).reshape(-1, 128).T

    x = np.asarray(i["x"][0])
    grid = x.reshape(GR, GW, D).transpose(1, 0, 2).reshape(SEQ, D)
    par = np.zeros((128, NPAR), np.float32)
    for col, t in ((P_PRE, i["pre_g"]), (P_POST, i["post_g"]), (P_BMOD, i["b_mod"]), (P_CW, i["conv_w"]),
                   (P_CB, i["conv_b"]), (P_MIX, i["g_mix_2"]), (P_MQ, i["g_mem_q_2"]), (P_MKV, i["g_mem_kv_2"]),
                   (P_MLP, i["g_mlp_2"]), (P_FIN, i["g_final_2"])):
        t = vecs(t)
        par[:, col:col + t.shape[1]] = t
    par[:, P_C:P_C + 16:2] = vecs(i["c"])
    par[:, P_C + 1:P_C + 16:2] = vecs(i["c_ctx"])
    par[0:8, P_BF] = np.asarray(i["b_forget_2"][0])

    rpb = np.asarray(i["rpb"][0])
    strips = np.zeros((16, 48, 15), np.float32)
    strips[:, 8:39, :] = rpb[:, ::-1, ::-1].transpose(0, 2, 1)
    lam = np.concatenate([np.asarray(i[n][0]) for n in ("lambda_q1_2", "lambda_q2_2", "lambda_k1_2", "lambda_k2_2")])

    f = np.float32
    inv = (f(10000.0) ** (-np.arange(0, 32, 2, dtype=f) / f(32))).astype(f)
    col, row = np.repeat(np.arange(GW), GR).astype(f), np.tile(np.arange(GR), GW).astype(f)
    ang = np.concatenate([row[:, None] * inv] * 2 + [col[:, None] * inv] * 2, axis=1).astype(f)
    sign = np.tile(np.repeat(np.array([-1.0, 1.0], f), 16), 2)
    cos, sin = np.cos(ang).astype(f), (np.sin(ang) * sign).astype(f)
    cos, sin = (np.tile(t.T, (2, 1)) for t in (cos, sin))
    wmask = np.zeros((128, 3, 256), f)
    for n, qb in enumerate((0, 1, 3)):
        qc = 16 * qb + np.arange(128) // GR
        kc = 16 * qb - 8 + np.arange(256) // GR
        start = np.clip(qc - WIN // 2, 0, GW - WIN)
        ok = (kc >= 0) & (kc < GW) & (kc >= start[:, None]) & (kc < start[:, None] + WIN)
        wmask[:, n] = np.where(ok, 0.0, MASKED)
    dist = np.arange(NDIST) - 127
    d = np.maximum(dist, 1).astype(f)
    large = 16 + (np.log(d / f(16)) / f(math.log(128 / 16)) * f(16)).astype(np.int32)
    bucket = np.where(dist < 16, np.maximum(dist, 0), np.minimum(large, 31))
    onehot = ((bucket == np.arange(32)[:, None]) & (dist >= 0)).astype(f)
    masked_rows = np.tile(np.where(dist < 0, MASKED, 0.0).astype(f), (4, 1))
    cmask = np.where(np.arange(128) <= np.arange(128)[:, None], 0.0, MASKED).astype(f)
    sel = np.zeros((16, 8, 128), f)
    sel[np.arange(16), np.arange(16) % 8] = 1.0

    arrays = {
        "w": np.stack(jobs), "par": par, "ctx": feat(i["ctx"][0]), "x_grid": feat(grid), "x_natural": feat(x),
        "mem": feat(i["mem_2"][0]), "wmod": np.asarray(i["w_mod"][0])[:, :2 * D].reshape(KT, 128, -1).transpose(1, 0, 2),
        "rpb": strips.reshape(16, 720), "lam": np.broadcast_to(lam, (128, 256)), "rel_bias": np.asarray(i["rel_bias_2"]),
        "gsub": np.broadcast_to(np.asarray(i["g_subln_2"][0]), (128, 128)),
        "onehot": onehot, "masked_rows": masked_rows, "cos": cos, "sin": sin, "sin_eighth": sin / 8, "wmask": wmask, "cmask": cmask, "sel": sel,
    }
    return {"in_" + k: np.ascontiguousarray(t) for k, t in arrays.items()}


def kernel(**inputs):
    import concourse.bacc as bacc
    from concourse.bass_utils import run_bass_kernel_spmd

    nc = bacc.Bacc("TRN2", target_bir_lowering=False, num_devices=1)
    arrays = _layout(inputs)
    A = {k[3:]: nc.dram_tensor(k, t.shape, mybir.dt.from_np(t.dtype), kind="ExternalInput").ap()
         for k, t in arrays.items()}
    out = nc.dram_tensor("out", (128, KT, SEQ), mybir.dt.float32, kind="ExternalOutput").ap()
    build(nc, A, out)
    got = run_bass_kernel_spmd(nc, [arrays], core_ids=[0]).results[0]["out"]
    return np.ascontiguousarray(got.transpose(2, 1, 0).reshape(1, SEQ, D))
```
